# Optimizing a Trainium2 kernel written in Bass

```python
import jax
import jax.numpy as jnp
from jax import lax
import numpy as np

D_MODEL = 1024
BATCH = 1
SEQ = 1024
DEPTH = 2

CTX_LEN = 256
GRID_W = 64
HEAD_DIM = 64
A_HEADS = 8
A_KV_HEADS = 2
A_GROUP = A_HEADS // A_KV_HEADS
B_HEADS = 4
B_Q_RANK = 192
B_KV_RANK = 128
B_NOPE = 64
B_ROPE = 32
B_V = 64
C_HEADS = 4
C_DK = 64
C_DV = 64
D_FF = 4 * D_MODEL
A_OUT = A_HEADS * HEAD_DIM
B_OUT = B_HEADS * B_V
C_OUT = C_HEADS * C_DV
D_MIX = A_OUT + B_OUT + C_OUT
IN_SIZES = (A_HEADS * HEAD_DIM, A_KV_HEADS * HEAD_DIM, A_KV_HEADS * HEAD_DIM,
            B_Q_RANK, B_KV_RANK, B_ROPE,
            C_HEADS * C_DK, C_HEADS * C_DK, C_HEADS * C_DK, C_HEADS * C_DV, C_HEADS * C_DV)
D_IN = sum(IN_SIZES)
SPLIT_AT = tuple(int(v) for v in np.cumsum(IN_SIZES)[:-1])
Q_BLOCK = 128
SCAN_CHUNK = 64
ROPE_THETA = 10000.0
EPS = 1e-6
F_TINY = 1e-30
F32 = jnp.float32

kernel_name = 'hybrid_parallel_heads_dit_block'

def rms_norm(x, gain):
    xf = x.astype(F32)
    y = xf * lax.rsqrt(jnp.mean(xf * xf, axis=-1, keepdims=True) + EPS)
    return (y * gain.astype(F32)).astype(x.dtype)

def modulate(h, shift, scale):
    return h * (1 + scale) + shift

def axial_rope(row_ids, col_ids, rot_dim):
    n_freq = rot_dim // 4
    inv = ROPE_THETA ** (-jnp.arange(n_freq, dtype=F32) / n_freq)
    ang = jnp.concatenate([row_ids.astype(F32)[:, None] * inv, col_ids.astype(F32)[:, None] * inv], axis=-1)
    return jnp.cos(ang)[:, None, :], jnp.sin(ang)[:, None, :]

def apply_rope(x, rope):
    cos, sin = rope
    xf = x.astype(F32)
    x1, x2 = jnp.split(xf, 2, axis=-1)
    return jnp.concatenate([x1 * cos - x2 * sin, x2 * cos + x1 * sin], axis=-1).astype(x.dtype)

def forget_gate(z, lb):
    zf = z.astype(F32)
    f = lb + (1.0 - lb) * jax.nn.sigmoid(zf)
    log_f = jnp.log(jnp.maximum(f, F_TINY))
    k = (1.0 - lb) * jax.nn.sigmoid(-zf)
    return log_f, k.astype(z.dtype)

def block_attention(q, k, v, scale):
    bsz, t = q.shape[:2]
    nb = t // Q_BLOCK
    qb = jnp.moveaxis(q.reshape(bsz, nb, Q_BLOCK, *q.shape[2:]), 1, 0)

    def one_block(qi):
        s = jnp.einsum('bqhgd,bkhd->bhgqk', qi, k, preferred_element_type=F32) * scale
        p = jax.nn.softmax(s, axis=-1).astype(v.dtype)
        return jnp.einsum('bhgqk,bkhv->bqhgv', p, v)

    out = lax.map(one_block, qb)
    return jnp.moveaxis(out, 0, 1).reshape(bsz, t, *out.shape[3:])

def gla_chunk_scan(q, k, v, g, s0):
    bsz, n_tok, n_h, dk = q.shape
    dv = v.shape[-1]
    n_chunk = n_tok // SCAN_CHUNK

    def to_chunks(a):
        return a.astype(F32).reshape(bsz, n_chunk, SCAN_CHUNK, n_h, a.shape[-1]).transpose(1, 0, 3, 2, 4)

    lower_tri = jnp.tril(jnp.ones((SCAN_CHUNK, SCAN_CHUNK), dtype=bool))[:, :, None]

    def step(state, inp):
        q_, k_, v_, g_ = inp
        b = jnp.cumsum(g_, axis=-2)
        diff = b[..., :, None, :] - b[..., None, :, :]
        decay = jnp.where(lower_tri, jnp.exp(jnp.where(lower_tri, diff, 0.0)), 0.0)
        scores = jnp.einsum('bhtd,bhsd,bhtsd->bhts', q_, k_, decay)
        o = jnp.einsum('bhts,bhsv->bhtv', scores, v_) + jnp.einsum('bhtd,bhdv->bhtv', q_ * jnp.exp(b), state)
        b_last = b[..., -1:, :]
        new_state = state * jnp.exp(b_last[..., 0, :])[..., None] + jnp.einsum('bhsd,bhsv->bhdv', k_ * jnp.exp(b_last - b), v_)
        return new_state, o

    s_fin, o = lax.scan(step, s0, (to_chunks(q), to_chunks(k), to_chunks(v), to_chunks(g)))
    o = o.transpose(1, 0, 3, 2, 4).reshape(bsz, n_tok, n_h, dv)
    return o.astype(v.dtype), s_fin

def mixer_features(h, w_in, a_q_norm, a_k_norm, b_q_norm, w_q_up, b_kv_norm, w_kv_up, lb, rope_a, rope_b):
    bsz, t, _ = h.shape
    aq, ak, av, bqd, bkvd, bkr, cq, cff, cfb, ci, cg = jnp.split(h @ w_in, SPLIT_AT, axis=-1)
    aq = rms_norm(aq.reshape(bsz, t, A_HEADS, HEAD_DIM), a_q_norm)
    ak = rms_norm(ak.reshape(bsz, t, A_KV_HEADS, HEAD_DIM), a_k_norm)
    av = av.reshape(bsz, t, A_KV_HEADS, HEAD_DIM)
    bq = (rms_norm(bqd, b_q_norm) @ w_q_up).reshape(bsz, t, B_HEADS, B_NOPE + B_ROPE)
    bkv = (rms_norm(bkvd, b_kv_norm) @ w_kv_up).reshape(bsz, t, B_HEADS, B_NOPE + B_V)
    bq_nope, bq_pe = jnp.split(bq, [B_NOPE], axis=-1)
    bk_nope, bv = jnp.split(bkv, [B_NOPE], axis=-1)
    bk_pe = bkr[:, :, None, :]
    if rope_a is not None:
        aq = apply_rope(aq, rope_a)
        ak = apply_rope(ak, rope_a)
        bq_pe = apply_rope(bq_pe, rope_b)
        bk_pe = apply_rope(bk_pe, rope_b)
    bq = jnp.concatenate([bq_nope, bq_pe], axis=-1)
    bk = jnp.concatenate([bk_nope, jnp.broadcast_to(bk_pe, (bsz, t, B_HEADS, B_ROPE))], axis=-1)
    heads = lambda a: a.reshape(bsz, t, C_HEADS, -1)
    g_f, k_f = forget_gate(cff, lb[0])
    g_b, k_b = forget_gate(cfb, lb[1])
    return {'aq': aq, 'ak': ak, 'av': av, 'bq': bq, 'bk': bk, 'bv': bv,
            'cq': heads(jax.nn.silu(cq)), 'cv': heads(ci), 'cgate': heads(cg),
            'ck_f': heads(k_f), 'cg_f': heads(g_f), 'ck_b': heads(k_b), 'cg_b': heads(g_b)}

def attention_groups(fq, fkv_list):
    bsz, t = fq['aq'].shape[:2]
    cat = lambda name: jnp.concatenate([f[name] for f in fkv_list], axis=1)
    ya = block_attention(fq['aq'].reshape(bsz, t, A_KV_HEADS, A_GROUP, HEAD_DIM), cat('ak'), cat('av'), HEAD_DIM ** -0.5)
    yb = block_attention(fq['bq'][:, :, :, None, :], cat('bk'), cat('bv'), (B_NOPE + B_ROPE) ** -0.5)
    return ya.reshape(bsz, t, A_OUT), yb.reshape(bsz, t, B_OUT)

def hgrn2_bidirectional(fl, fc, out_norm, need_ctx_out):
    bsz = fl['cq'].shape[0]
    zero = jnp.zeros((bsz, C_HEADS, C_DK, C_DV), F32)
    rev = lambda a: jnp.flip(a, axis=1)
    oc_f, s_f = gla_chunk_scan(fc['cq'], fc['ck_f'], fc['cv'], fc['cg_f'], zero)
    oc_b, s_b = gla_chunk_scan(rev(fc['cq']), rev(fc['ck_b']), rev(fc['cv']), rev(fc['cg_b']), zero)
    ol_f, _ = gla_chunk_scan(fl['cq'], fl['ck_f'], fl['cv'], fl['cg_f'], s_f)
    ol_b, _ = gla_chunk_scan(rev(fl['cq']), rev(fl['ck_b']), rev(fl['cv']), rev(fl['cg_b']), s_b)

    def readout(o, gate):
        y = rms_norm(o, out_norm) * jax.nn.silu(gate)
        return y.reshape(*y.shape[:2], C_OUT)

    y_lat = readout(ol_f + rev(ol_b), fl['cgate'])
    y_ctx = readout(oc_f + rev(oc_b), fc['cgate']) if need_ctx_out else None
    return y_lat, y_ctx

def sq_relu_mlp(h, w1, w2):
    return jnp.square(jax.nn.relu(h @ w1)) @ w2

def setup_inputs(seed: int = 0) -> dict:
    key = jax.random.key(seed)
    ks = jax.random.split(key, 24)
    nrm = lambda k, shape, scale: jax.random.normal(k, shape, F32) * scale
    gain = lambda k, shape: 1.0 + 0.05 * jax.random.normal(k, shape, F32)
    return {
        'x': nrm(ks[0], (BATCH, SEQ, D_MODEL), 1.0),
        'c': nrm(ks[1], (BATCH, D_MODEL), 1.0),
        'ctx': nrm(ks[2], (BATCH, CTX_LEN, D_MODEL), 1.0),
        'c_ctx': nrm(ks[3], (D_MODEL,), 1.0),
        'w_ada': nrm(ks[4], (DEPTH, D_MODEL, 6 * D_MODEL), 0.5 * D_MODEL ** -0.5),
        'b_ada': nrm(ks[5], (DEPTH, 6 * D_MODEL), 0.02),
        'g_pre_mix': gain(ks[6], (DEPTH, D_MODEL)),
        'g_post_mix': gain(ks[7], (DEPTH, D_MODEL)),
        'g_pre_ffn': gain(ks[8], (DEPTH, D_MODEL)),
        'g_post_ffn': gain(ks[9], (DEPTH, D_MODEL)),
        'w_in': nrm(ks[10], (DEPTH, D_MODEL, D_IN), D_MODEL ** -0.5),
        'a_q_norm': gain(ks[11], (DEPTH, HEAD_DIM)),
        'a_k_norm': gain(ks[12], (DEPTH, HEAD_DIM)),
        'b_q_norm': gain(ks[13], (DEPTH, B_Q_RANK)),
        'w_q_up': nrm(ks[14], (DEPTH, B_Q_RANK, B_HEADS * (B_NOPE + B_ROPE)), B_Q_RANK ** -0.5),
        'b_kv_norm': gain(ks[15], (DEPTH, B_KV_RANK)),
        'w_kv_up': nrm(ks[16], (DEPTH, B_KV_RANK, B_HEADS * (B_NOPE + B_V)), B_KV_RANK ** -0.5),
        'c_lower_bounds': nrm(ks[17], (DEPTH, 2, C_HEADS * C_DK), 0.5),
        'c_out_norm': gain(ks[18], (DEPTH, C_DV)),
        'w_out': nrm(ks[19], (DEPTH, D_MIX, D_MODEL), D_MIX ** -0.5),
        'w_ff1': nrm(ks[20], (DEPTH, D_MODEL, D_FF), D_MODEL ** -0.5),
        'w_ff2': nrm(ks[21], (DEPTH, D_FF, D_MODEL), D_FF ** -0.5),
    }

def reference(x, c, ctx, c_ctx, w_ada, b_ada, g_pre_mix, g_post_mix, g_pre_ffn, g_post_ffn,
              w_in, a_q_norm, a_k_norm, b_q_norm, w_q_up, b_kv_norm, w_kv_up,
              c_lower_bounds, c_out_norm, w_out, w_ff1, w_ff2):
    n_lat = x.shape[1]
    rows = n_lat // GRID_W
    row_ids = jnp.repeat(jnp.arange(rows, dtype=jnp.int32), GRID_W)
    col_ids = jnp.tile(jnp.arange(GRID_W, dtype=jnp.int32), rows)
    rope_a = axial_rope(row_ids, col_ids, HEAD_DIM)
    rope_b = axial_rope(row_ids, col_ids, B_ROPE)
    p_lb = jax.nn.softmax(c_lower_bounds.astype(F32), axis=0)
    lower = jnp.cumsum(p_lb, axis=0) - p_lb[:1]

    xc = ctx
    for l in range(DEPTH):
        need_ctx = l < DEPTH - 1
        sh_m, sc_m, gt_m, sh_f, sc_f, gt_f = jnp.split((jax.nn.silu(c) @ w_ada[l] + b_ada[l])[:, None, :], 6, axis=-1)
        csh_m, csc_m, cgt_m, csh_f, csc_f, cgt_f = jnp.split((jax.nn.silu(c_ctx) @ w_ada[l] + b_ada[l])[None, None, :], 6, axis=-1)
        feat_args = (w_in[l], a_q_norm[l], a_k_norm[l], b_q_norm[l], w_q_up[l], b_kv_norm[l], w_kv_up[l], lower[l])

        f_lat = mixer_features(modulate(rms_norm(x, g_pre_mix[l]), sh_m, sc_m), *feat_args, rope_a, rope_b)
        f_ctx = mixer_features(modulate(rms_norm(xc, g_pre_mix[l]), csh_m, csc_m), *feat_args, None, None)
        ya, yb = attention_groups(f_lat, [f_lat, f_ctx])
        yc, yc_ctx = hgrn2_bidirectional(f_lat, f_ctx, c_out_norm[l], need_ctx)
        x = x + gt_m * rms_norm(jnp.concatenate([ya, yb, yc], axis=-1) @ w_out[l], g_post_mix[l])

        x = x + gt_f * rms_norm(sq_relu_mlp(modulate(rms_norm(x, g_pre_ffn[l]), sh_f, sc_f), w_ff1[l], w_ff2[l]), g_post_ffn[l])

        if need_ctx:
            ya_c, yb_c = attention_groups(f_ctx, [f_ctx])
            xc = xc + cgt_m * rms_norm(jnp.concatenate([ya_c, yb_c, yc_ctx], axis=-1) @ w_out[l], g_post_mix[l])
            xc = xc + cgt_f * rms_norm(sq_relu_mlp(modulate(rms_norm(xc, g_pre_ffn[l]), csh_f, csc_f), w_ff1[l], w_ff2[l]), g_post_ffn[l])
    return x


_drawn_inputs = setup_inputs


def setup_inputs(seed=0):
    import zlib

    import numpy as np

    out = dict(_drawn_inputs(seed))
    spreads = {}
    factors = {'ctx': 2.673,
     'g_post_mix': 2.852,
     'g_post_ffn': 2.784,
     'a_q_norm': 8.0,
     'a_k_norm': 8.0,
     'b_q_norm': 8.0,
     'b_kv_norm': 7.475,
     'c_lower_bounds': 47.155,
     'c_out_norm': 3.866}
    for name, (base, spread) in spreads.items():
        noise = np.random.default_rng([zlib.crc32(name.encode()), seed]).standard_normal(out[name].shape)
        drawn = base * np.exp(spread * noise) if base else spread * noise
        out[name] = jnp.asarray(drawn.astype(out[name].dtype))
    for name, factor in factors.items():
        out[name] = (out[name] * factor).astype(out[name].dtype)
    return out
```

```python
from contextlib import ExitStack

import numpy as np

import concourse.bass as bass
from concourse import mybir

F32 = mybir.dt.float32
F16 = mybir.dt.float16
BF16 = mybir.dt.bfloat16
U8 = mybir.dt.uint8
ALU = mybir.AluOpType
ACT = mybir.ActivationFunctionType
AX = mybir.AxisListType

P = 128
D = 1024
KT = D // P
LAT, CTX = 1024, 256
TOK = LAT + CTX
TT = TOK // P
DEPTH = 2
EPS = 1e-6
F_TINY = 1e-30
WSCALE = 256.0
ASCALE = 0.25
FF = 4 * D
GROUP = 8
BLK = 128
LEVELS = [64, 32, 16, 8, 4, 2, 1]
R_BADA, R_GPM, R_GQM, R_GPF, R_GQF, R_C, R_CC, R_LB, R_BKV, R_BQ, R_AQ, R_AK, R_CO, R_N = (
    0, 48, 56, 64, 72, 80, 88, 96, 104, 105, 107, 108, 109, 110)
C_AQ, C_AK, C_AV, C_BQ, C_BKV, C_BKR, C_CQ, C_CFF, C_CFB, C_CI, C_CG = (
    0, 512, 640, 768, 960, 1088, 1120, 1376, 1632, 1888, 2144)


def chunks(n):
    return [(a, min(512, n - a)) for a in range(0, n, 512)]


class Chain:

    def __init__(self, sem):
        self.sem, self.n = sem, 0

    def __call__(self, ins):
        self.n += 1
        ins.then_inc(self.sem, 1)
        return self.n

    def wait(self, eng, n=None):
        eng.wait_ge(self.sem, self.n if n is None else n)


class Env:
    pass


def setup_phase(nc, e, sem):
    with ExitStack() as st:
        sb = lambda n, s, d=F32: st.enter_context(nc.sbuf_tensor(n, s, d))
        ps = lambda n, s, d=F32: st.enter_context(nc.psum_tensor(n, s, d))
        xin = sb("xin", [P, 4, D])
        xt = sb("xt", [P, KT, TOK])
        rows = sb("rows", [P, DEPTH, P])
        wada = sb("wada", [P, 3, KT, 512])
        cs = sb("cs", [P, 2 * KT])
        ce = sb("ce", [P, 2 * KT])
        cact = sb("cact", [P, KT, 2])
        lbw = sb("lbw", [P, 6, 4])
        samef = sb("samef", [P, 8, P])
        tp = [ps(f"tp{i}", [P, 4, P]) for i in range(2)]
        tv = ps("tv", [P, DEPTH, P])
        mo = [ps(f"mo{i}", [P, 48, 2]) for i in range(2)]
        s_const, s_rows, s_store = sem("const_loaded"), sem("rows_loaded"), sem("x_stored")
        s_zero = sem("rows_zeroed")
        s_xin = [sem(f"xin_loaded{i}") for i in range(4)]
        s_w = [sem(f"wada_loaded{i}") for i in range(3)]
        s_tp, s_xt, s_tv, s_sv = sem("x_transposed"), sem("x_evacuated"), sem("rows_transposed"), sem("vectors_ready")
        s_e, s_silu, s_wused, s_dch = (sem("exp_c"), sem("silu_c"), sem("wada_used"),
                                             sem("setup_dve"))
        s_lbd = sem("bounds_shifted")
        e.consts.append((samef[:, :, :], e.k_same))
        ncon = len(e.consts)
        with nc.Block() as block:
            @block.sync
            def _(sp):
                for dst, src in e.consts:
                    sp.dma_start(dst, src).then_inc(s_const, 16)
                sp.wait_ge(s_zero, 1)
                for l in range(DEPTH):
                    r = rows[:, l, :]
                    for at, n, src in ((R_BADA, 48, e.b_ada[l]), (R_GPM, 8, e.g_pre_mix[l]), (R_GQM, 8, e.g_post_mix[l]),
                                       (R_GPF, 8, e.g_pre_ffn[l]), (R_GQF, 8, e.g_post_ffn[l]),
                                       (R_C, 8, e.c[0]), (R_CC, 8, e.c_ctx),
                                       (R_LB, 8, e.c_lb.rearrange("a b c -> (a b c)")), (R_BKV, 1, e.b_kv_norm[l]),
                                       (R_BQ, 1, e.b_q_norm[l, 0:P])):
                        sp.dma_start(r[at:at + n, :], src.rearrange("(a b) -> a b", b=P)).then_inc(s_rows, 16)
                    sp.dma_start(r[R_BQ + 1:R_BQ + 2, 0:64],
                                 e.b_q_norm[l, P:192].rearrange("(a b) -> a b", a=1)).then_inc(s_rows, 16)
                    for at, src in ((R_AQ, e.a_q_norm[l]), (R_AK, e.a_k_norm[l]), (R_CO, e.c_out_norm[l])):
                        for half in range(2):
                            sp.dma_start(r[at:at + 1, 64 * half:64 * half + 64],
                                         src.rearrange("(a b) -> a b", a=1)).then_inc(s_rows, 16)
                for t in range(TT):
                    if t >= 4:
                        sp.wait_ge(s_tp, 2 * (t - 3))
                    src = e.x[0, t * P:(t + 1) * P, :] if t < LAT // P else e.ctx[0, t * P - LAT:(t + 1) * P - LAT, :]
                    sp.dma_start(xin[:, t % 4, :], src).then_inc(s_xin[t % 4], 16)
                sp.wait_ge(s_xt, 2 * TT)
                sp.dma_start(e.x_dram, xt[:, :, :]).then_inc(s_store, 16)
                sp.wait_ge(s_store, 16)

            @block.scalar
            def _(act):
                n = 0
                for l in range(DEPTH):
                    for j in range(12):
                        if n >= 3:
                            act.wait_ge(s_wused, n - 2)
                        src = e.w_ada[l, :, j * 512:(j + 1) * 512].rearrange("(k p) n -> p k n", p=P)
                        act.dma_start(wada[:, n % 3, :, :], src).then_inc(s_w[n % 3], 16)
                        n += 1
                        if n == 3:
                            act.wait_ge(s_sv, 1)
                            nc.scalar.activation(ce[:, :], cs[:, :], ACT.Exp, scale=-1.0).then_inc(s_e, 1)
                            act.wait_ge(s_lbd, 2)
                            nc.scalar.activation(lbw[:, 2, :], lbw[:, 0, :], ACT.Exp).then_inc(s_e, 1)
                            nc.scalar.activation(lbw[:, 3, :], lbw[:, 1, :], ACT.Exp).then_inc(s_e, 1)

            @block.vector
            def _(dve):
                ch = Chain(s_dch)
                nc.vector.memset(rows[:, :, :], 0.0).then_inc(s_zero, 1)
                dve.wait_ge(s_const, 16 * ncon)
                ch(nc.vector.tensor_copy(e.same[:, :, :], samef[:, :, :]))
                dve.wait_ge(s_tv, 1)
                ch(nc.vector.tensor_copy(e.sv[:, :, :], tv[:, :, 0:R_N]))
                ch.wait(dve)
                nc.vector.tensor_copy(cs[:, :], e.sv[:, 0, R_C:R_C + 16]).then_inc(s_sv, 1)
                dve.wait_ge(s_e, 1)
                ch(nc.vector.tensor_scalar_add(ce[:, :], ce[:, :], 1.0))
                ch.wait(dve)
                ch(nc.vector.reciprocal(ce[:, :], ce[:, :]))
                ch.wait(dve)
                nc.vector.tensor_tensor(cact[:, :, :].rearrange("p k n -> p n k"),
                                        cs[:, :].rearrange("p (n k) -> p n k", k=KT),
                                        ce[:, :].rearrange("p (n k) -> p n k", k=KT), ALU.mult).then_inc(s_silu, 1)
                a0, a1 = e.sv[:, 0, R_LB:R_LB + 4], e.sv[:, 0, R_LB + 4:R_LB + 8]
                ch(nc.vector.tensor_tensor(lbw[:, 4, :], a0, a1, ALU.max))
                ch.wait(dve)
                nc.vector.tensor_tensor(lbw[:, 0, :], a0, lbw[:, 4, :], ALU.subtract).then_inc(s_lbd, 1)
                nc.vector.tensor_tensor(lbw[:, 1, :], a1, lbw[:, 4, :], ALU.subtract).then_inc(s_lbd, 1)
                dve.wait_ge(s_e, 3)
                ch(nc.vector.tensor_tensor(lbw[:, 4, :], lbw[:, 2, :], lbw[:, 3, :], ALU.add))
                ch.wait(dve)
                ch(nc.vector.reciprocal(lbw[:, 5, :], lbw[:, 4, :]))
                ch.wait(dve)
                ch(nc.vector.tensor_tensor(lbw[:, 2, :], lbw[:, 2, :], lbw[:, 5, :], ALU.mult))
                ch(nc.vector.tensor_tensor(lbw[:, 3, :], lbw[:, 3, :], lbw[:, 5, :], ALU.mult))
                ch.wait(dve)
                ch(nc.vector.tensor_tensor(lbw[:, 3, :], lbw[:, 2, :], lbw[:, 3, :], ALU.add))
                ch(nc.vector.tensor_tensor(e.lb[:, 0, 0, :], lbw[:, 2, :], lbw[:, 2, :], ALU.subtract))
                ch.wait(dve)
                ch(nc.vector.tensor_tensor(e.lb[:, 1, 0, :], lbw[:, 3, :], lbw[:, 2, :], ALU.subtract))
                ch.wait(dve)
                ch(nc.vector.tensor_scalar(e.lb[:, :, 1, :], e.lb[:, :, 0, :], -1.0, 1.0, ALU.mult, ALU.add))
                for i in range(2 * TT):
                    t, half = i // 2, i % 2
                    dve.wait_ge(s_tp, i + 1)
                    nc.vector.tensor_copy(xt[:, 4 * half:4 * half + 4, t * P:(t + 1) * P], tp[i % 2][:, :, :])\
                      .then_inc(s_xt, 1)
                for l in range(DEPTH):
                    dve.wait_ge(s_wused, 12 * (l + 1))
                    m = e.mod[:, l, :, :]
                    for n in range(2):
                        ch(nc.vector.tensor_tensor(m[:, :, n], mo[l][:, :, n], e.sv[:, l, R_BADA:R_BADA + 48], ALU.add))
                    ch.wait(dve)
                    for n in range(2):
                        for at, g in ((8, R_GPM), (32, R_GPF)):
                            ch(nc.vector.scalar_tensor_tensor(m[:, at:at + 8, n], m[:, at:at + 8, n], 1.0,
                                                              e.sv[:, l, g:g + 8], ALU.add, ALU.mult))
                        for at, g in ((16, R_GQM), (40, R_GQF)):
                            ch(nc.vector.tensor_tensor(m[:, at:at + 8, n], m[:, at:at + 8, n],
                                                       e.sv[:, l, g:g + 8], ALU.mult))
                    ch.wait(dve)
                    for at in (8, 32):
                        ch(nc.vector.tensor_scalar(m[:, at:at + 16, :], m[:, at:at + 16, :], -0.5, None, ALU.mult))
                    ch(nc.vector.tensor_scalar(e.sv[:, l, R_BKV:R_N], e.sv[:, l, R_BKV:R_N], -0.5, None, ALU.mult))

            @block.tensor
            def _(pe):
                pe.wait_ge(s_const, 16 * ncon)
                pe.wait_ge(s_rows, 16 * 17 * DEPTH)
                for l in range(DEPTH):
                    last = nc.tensor.transpose(tv[:, l, :], rows[:, l, :], e.ident[:, :])
                last.then_inc(s_tv, 1)
                for i in range(2 * TT):
                    t, half = i // 2, i % 2
                    if half == 0:
                        pe.wait_ge(s_xin[t % 4], 16 * (t // 4 + 1))
                    if i >= 2:
                        pe.wait_ge(s_xt, i - 1)
                    for k in range(4):
                        last = nc.tensor.transpose(tp[i % 2][:, k, :],
                                                   xin[:, t % 4, (4 * half + k) * P:(4 * half + k + 1) * P],
                                                   e.ident[:, :])
                    last.then_inc(s_tp, 1)
                pe.wait_ge(s_silu, 1)
                n = 0
                for l in range(DEPTH):
                    for j in range(12):
                        pe.wait_ge(s_w[n % 3], 16 * (n // 3 + 1))
                        for m in range(4):
                            for k in range(KT):
                                last = nc.tensor.matmul(mo[l][:, 4 * j + m, :], wada[:, n % 3, k, m * P:(m + 1) * P],
                                                        cact[:, k, :], start=(k == 0), stop=(k == KT - 1))
                        last.then_inc(s_wused, 1)
                        n += 1


def norm_phase(nc, e, sem, src, ntok, mod, load, nm):
    sc, sh, l = mod
    with ExitStack() as st:
        sb = lambda n, s, d=F32: st.enter_context(nc.sbuf_tensor(nm + n, s, d))
        ps = lambda n, s, d=F32: st.enter_context(nc.psum_tensor(nm + n, s, d))
        S = lambda n: sem(nm + n)
        x = sb("x", [P, KT, TOK]) if load else src
        sq = sb("sq", [P, 3, 512])
        stat = sb("stat", [P, 4, 512])
        h = sb("h", [P, 2, 512])
        ss = [ps(f"ss{i}", [P, 512]) for i in range(2)]
        s_x, s_sq, s_m, s_r0 = S("x_loaded"), S("squared"), S("mean"), S("rsqrt")
        s_h, s_hi, s_d, s_lo, s_sqm = S("h_ready"), S("hi_done"), S("dve"), S("lo_done"), S("square_used")
        cks = chunks(ntok)
        with nc.Block() as block:
            @block.sync
            def _(sp):
                if load:
                    for c, (a, n) in enumerate(cks):
                        sp.dma_start(x[:, :, a:a + n], e.x_dram[:, :, a:a + n]).then_inc(s_x, 16)
                        sp.wait_ge(s_x, 16 * (c + 1))

            @block.scalar
            def _(act):
                i = j = 0

                def rsqrt(c):
                    n = cks[c][1]
                    act.wait_ge(s_m, c + 1)
                    nc.scalar.activation(stat[:, 1, 0:n], stat[:, 0, 0:n], ACT.Ln).then_inc(s_r0, 1)
                    act.wait_ge(s_r0, 2 * c + 1)
                    nc.scalar.activation(stat[:, 1, 0:n], stat[:, 1, 0:n], ACT.Exp, scale=-0.5).then_inc(s_r0, 1)

                for c, (a, n) in enumerate(cks):
                    if load:
                        act.wait_ge(s_x, 16 * (c + 1))
                    for k in range(KT):
                        if i >= 3:
                            act.wait_ge(s_sqm, i - 2)
                        nc.scalar.activation(sq[:, i % 3, 0:n], x[:, k, a:a + n], ACT.Square).then_inc(s_sq, 1)
                        i += 1
                    rsqrt(c)
                    for k in range(KT):
                        act.wait_ge(s_h, j + 1)
                        nc.scalar.activation(e.hh[:, 0, k, a:a + n], h[:, j % 2, 0:n], ACT.Copy).then_inc(s_hi, 1)
                        j += 1

            @block.tensor
            def _(pe):
                i = 0
                for c, (a, n) in enumerate(cks):
                    if c >= 2:
                        pe.wait_ge(s_m, c - 1)
                    for k in range(KT):
                        pe.wait_ge(s_sq, i + 1)
                        nc.tensor.matmul(ss[c % 2][:, 0:n], e.ones[:, :], sq[:, i % 3, 0:n],
                                         start=(k == 0), stop=(k == KT - 1)).then_inc(s_sqm, 1)
                        i += 1

            @block.vector
            def _(dve):
                ch = Chain(s_d)
                j = 0
                for c, (a, n) in enumerate(cks):
                    dve.wait_ge(s_sqm, KT * (c + 1))
                    nc.vector.tensor_scalar(stat[:, 0, 0:n], ss[c % 2][:, 0:n], 1.0 / D, EPS, ALU.mult, ALU.add)\
                      .then_inc(s_m, 1)
                    dve.wait_ge(s_r0, 2 * c + 2)
                    newton(nc, dve, ch, stat[:, 0, 0:n], stat[:, 1, 0:n], stat[:, 2, 0:n])
                    segs = [(a, n, 0)] if a + n <= LAT else [(a, n, 1)]
                    for k in range(KT):
                        if j >= 2:
                            dve.wait_ge(s_hi, j - 1)
                        for (b, w, who) in segs:
                            ch(nc.vector.tensor_tensor(h[:, j % 2, b - a:b - a + w], x[:, k, b:b + w],
                                                       stat[:, 1, b - a:b - a + w], ALU.mult))
                            ch.wait(dve)
                            nc.vector.tensor_scalar(h[:, j % 2, b - a:b - a + w], h[:, j % 2, b - a:b - a + w],
                                                       e.mod[:, l, sc + k, who:who + 1], e.mod[:, l, sh + k, who:who + 1],
                                                       ALU.mult, ALU.add).then_inc(s_h, 1)
                        dve.wait_ge(s_hi, j + 1)
                        nc.vector.tensor_tensor(e.hh[:, 1, k, a:a + n], h[:, j % 2, 0:n], e.hh[:, 0, k, a:a + n],
                                                ALU.subtract).then_inc(s_lo, 1)
                        dve.wait_ge(s_lo, j + 1)
                        j += 1


def newton(nc, dve, ch, m, r, t):
    ch(nc.vector.tensor_tensor(t, m, r, ALU.mult))
    ch.wait(dve)
    ch(nc.vector.tensor_tensor(t, t, r, ALU.mult))
    ch.wait(dve)
    ch(nc.vector.scalar_tensor_tensor(r, t, 3.0, r, ALU.subtract, ALU.mult))
    ch.wait(dve)


class Linear:

    RING = 4

    def __init__(self, nc, e, sem, st, nm):
        self.nc = nc
        sb = lambda n, s, d=F32: st.enter_context(nc.sbuf_tensor(nm + n, s, d))
        self.stage = sb("stage", [P, self.RING, KT * P])
        self.w = sb("w", [P, self.RING, 2, KT * P], F16)
        self.ps = [st.enter_context(nc.psum_tensor(f"{nm}acc{i}", [P, 3 * 512], F32)) for i in range(2)]
        self.s_load = [sem(f"{nm}w_loaded{i}") for i in range(self.RING)]
        self.s_hi, self.s_lo, self.s_used = sem(nm + "w_hi"), sem(nm + "w_lo"), sem(nm + "w_used")

    def load(self, eng, n, parts):
        r = n % self.RING
        if n >= self.RING:
            eng.wait_ge(self.s_lo, n - self.RING + 1)
        for k, row, at, src in parts:
            dst = self.stage[:, r, 0:k * row].rearrange("p (k n) -> p k n", k=k)[:, :, at:at + src.shape[2]]
            eng.dma_start(dst, src).then_inc(self.s_load[r], 16)

    def high(self, act, n, loads, size=KT * P, used=None):
        r = n % self.RING
        act.wait_ge(self.s_load[r], 16 * loads)
        if n >= self.RING:
            act.wait_ge(*(used or (self.s_used, n - self.RING + 1)))
        self.nc.scalar.activation(self.w[:, r, 0, 0:size], self.stage[:, r, 0:size], ACT.Copy, scale=WSCALE)\
            .then_inc(self.s_hi, 1)

    def low(self, dve, n, size=KT * P):
        r = n % self.RING
        dve.wait_ge(self.s_hi, n + 1)
        self.nc.vector.scalar_tensor_tensor(self.w[:, r, 1, 0:size], self.stage[:, r, 0:size], WSCALE,
                                            self.w[:, r, 0, 0:size], ALU.mult, ALU.subtract).then_inc(self.s_lo, 1)

    def product(self, n, acc, src, k0, kn, m0, mw, row, ntok, col=0):
        r = n % self.RING
        w = self.w[:, r, :, 0:kn * row].rearrange("p h (k n) -> p h k n", k=kn)
        for k in range(kn):
            for wh, sh in ((0, 0), (0, 1), (1, 0)):
                for a, c in chunks(ntok):
                    last = self.nc.tensor.matmul(acc[0:mw, a:a + c], w[:, wh, k, m0:m0 + mw],
                                                 src[:, sh, k0 + k, a:a + c],
                                                 start=(k == 0 and wh == 0 and sh == 0),
                                                 stop=(k == kn - 1 and wh == 1))
        return last

    def product_t(self, n, acc, src, row, mw, tts):
        r = n % self.RING
        w = self.w[:, r, :, 0:KT * row].rearrange("p h (k n) -> p h k n", k=KT)
        for t in range(tts):
            for k in range(KT):
                for sh, wh in ((0, 0), (0, 1), (1, 0)):
                    last = self.nc.tensor.matmul(acc[:, t * P:t * P + mw], src[:, sh, k, t * P:(t + 1) * P],
                                                 w[:, wh, k, 0:mw], start=(k == 0 and wh == 0 and sh == 0),
                                                 stop=(k == KT - 1 and sh == 1))
        return last


def input_projection(nc, e, sem, l, f):
    nq = TOK if l < DEPTH - 1 else LAT
    w = e.w_in[l].rearrange("(k p) n -> p k n", p=P)
    tiles = []
    for i in range(2):
        tiles.append(([(0, C_CFF + i * P, P)], P, TOK, f.z[:, 2 + i, :]))
        tiles.append(([(0, C_CFB + i * P, P)], P, TOK, f.z[:, i, :]))
    for i in range(2):
        tiles.append(([(0, C_CI + i * P, P)], P, None, f.cv[:, :, i * P:(i + 1) * P]))
    for i in range(2):
        tiles.append(([(0, C_CQ + i * P, P)], P, nq, f.cq[:, i, :]))
        tiles.append(([(0, C_CG + i * P, P)], P, nq, f.cg[:, i, :]))
    tiles.append(([(0, C_AK, P)], P, TOK, f.ak[:, :]))
    tiles.append(([(0, C_AV, P)], P, None, None))
    for i in range(4):
        tiles.append(([(0, C_AQ + i * P, P)], P, nq, f.aq[:, i, :]))
    tiles.append(([(0, C_BKV, P)], P, TOK, f.bkv[:, :]))
    tiles.append(([(0, C_BQ, P)], P, nq, f.bq[:, 0, :]))
    tiles.append(([(0, C_BQ + P, 64), (64, C_BKR, 32)], 96, TOK, f.bq[0:96, 1, :]))
    N = len(tiles)
    with ExitStack() as st:
        nm = f"in{l}_"
        L = Linear(nc, e, sem, st, nm)
        s_ev, s_av = sem(nm + "evacuated"), sem(nm + "av_hi")
        avf = st.enter_context(nc.sbuf_tensor(nm + "avf", [P, TT * P], F32))
        av4 = avf[:, :].rearrange("p (t h n) -> p t h n", h=2, n=64)
        counts, seen = [], [0] * L.RING
        for n, t in enumerate(tiles):
            seen[n % L.RING] += len(t[0])
            counts.append(seen[n % L.RING])
        with nc.Block() as block:
            @block.sync
            def _(sp):
                for n, (cols, row, _, _) in enumerate(tiles):
                    L.load(sp, n, [(KT, row, at, w[:, :, c0:c0 + cn]) for at, c0, cn in cols])

            @block.scalar
            def _(act):
                for n in range(-2, N):
                    if n + 2 < N:
                        L.high(act, n + 2, counts[n + 2], KT * tiles[n + 2][1])
                    if n < 0:
                        continue
                    _, row, ntok, dst = tiles[n]
                    act.wait_ge(L.s_used, n + 1)
                    if dst is None:
                        nc.scalar.activation(avf[:, :], L.ps[n % 2][:, 0:TOK], ACT.Copy, scale=1.0 / WSCALE)\
                          .then_inc(s_ev, 1)
                        act.wait_ge(s_ev, n + 1)
                        for h in range(2):
                            last = nc.scalar.activation(f.av[:, :, h, 0:64], av4[:, :, h, :], ACT.Copy)
                        last.then_inc(s_av, 1)
                    elif ntok is None:
                        nc.scalar.activation(dst, L.ps[n % 2][:, 0:TOK].rearrange("p (t n) -> p t n", n=P), ACT.Copy,
                                             scale=1.0 / WSCALE).then_inc(s_ev, 1)
                    else:
                        nc.scalar.activation(dst[:, 0:ntok], L.ps[n % 2][0:row, 0:ntok], ACT.Copy, scale=1.0 / WSCALE)\
                          .then_inc(s_ev, 1)

            @block.vector
            def _(dve):
                for n in range(N):
                    L.low(dve, n, KT * tiles[n][1])
                dve.wait_ge(s_av, 1)
                for h in range(2):
                    nc.vector.tensor_tensor(f.av[:, :, h, 64:P], av4[:, :, h, :], f.av[:, :, h, 0:64], ALU.subtract)

            @block.tensor
            def _(pe):
                for n, (cols, row, ntok, dst) in enumerate(tiles):
                    pe.wait_ge(L.s_lo, n + 1)
                    if n >= 2:
                        pe.wait_ge(s_ev, n - 1)
                    if ntok is None:
                        L.product_t(n, L.ps[n % 2], e.hh, row, P, TT).then_inc(L.s_used, 1)
                    else:
                        L.product(n, L.ps[n % 2], e.hh, 0, KT, 0, row, row, ntok).then_inc(L.s_used, 1)


def output_projection(nc, e, sem, l, y, ntok):
    w = e.w_out[l].rearrange("(k p) n -> p k n", p=P)
    with ExitStack() as st:
        nm = f"out{l}_"
        L = Linear(nc, e, sem, st, nm)
        s_ev = sem(nm + "evacuated")
        with nc.Block() as block:
            @block.sync
            def _(sp):
                for n in range(KT):
                    L.load(sp, n, [(KT, P, 0, w[:, :, n * P:(n + 1) * P])])

            @block.scalar
            def _(act):
                for n in range(-2, KT):
                    if n + 2 < KT:
                        L.high(act, n + 2, (n + 2) // 4 + 1)
                    if n >= 0:
                        act.wait_ge(L.s_used, n + 1)
                        nc.scalar.activation(y[:, n, 0:ntok], L.ps[n % 2][:, 0:ntok], ACT.Copy, scale=1.0 / WSCALE)\
                          .then_inc(s_ev, 1)

            @block.vector
            def _(dve):
                for n in range(KT):
                    L.low(dve, n)

            @block.tensor
            def _(pe):
                for n in range(KT):
                    pe.wait_ge(L.s_lo, n + 1)
                    if n >= 2:
                        pe.wait_ge(s_ev, n - 1)
                    L.product(n, L.ps[n % 2], e.hh, 0, KT, 0, P, P, ntok).then_inc(L.s_used, 1)


MG = 4
NG = FF // P // MG


def mlp(nc, e, sem, l, y, ntok):
    w1 = e.w_ff1[l].rearrange("(k p) n -> p k n", p=P)
    w2 = e.w_ff2[l].rearrange("(g k p) n -> g p k n", p=P, k=MG)
    slots = []
    for g in range(NG + 1):
        if g < NG:
            slots += [("up", g, j) for j in range(MG)]
        if g:
            slots += [("down", g - 1, j) for j in range(KT // 2)]
    N = len(slots)
    with ExitStack() as st:
        nm = f"mlp{l}_"
        L = Linear(nc, e, sem, st, nm)
        sb = lambda n, s, d=F32: st.enter_context(nc.sbuf_tensor(nm + n, s, d))
        aa = sb("aa", [P, 2, 2, MG, TOK], F16)
        r = sb("r", [P, TOK])
        s_ev, s_relu, s_sq, s_ahi, s_alo, s_out = (sem(nm + x) for x in (
            "y_added", "relu", "squared", "a_hi", "a_lo", "outputs_done"))
        outs = []
        for n, (kind, g, j) in enumerate(slots):
            outs += [(n, kind, g, j, 0)] if kind == "up" else [(n, kind, g, 2 * j + m, m) for m in range(2)]
        M = len(outs)
        done = {o[0]: i + 1 for i, o in enumerate(outs)}
        ups = [sum(o[1] == "up" for o in outs[:i]) for i in range(M + 1)]

        def free(eng, i):
            if i >= 2:
                if outs[i - 2][1] == "up":
                    eng.wait_ge(s_relu, ups[i - 1])
                else:
                    eng.wait_ge(s_ev, i - 1 - ups[i - 1])

        with nc.Block() as block:
            @block.sync
            def _(sp):
                for n, (kind, g, j) in enumerate(slots):
                    if kind == "up":
                        L.load(sp, n, [(KT, P, 0, w1[:, :, (MG * g + j) * P:(MG * g + j + 1) * P])])
                    else:
                        L.load(sp, n, [(MG, 2 * P, 0, w2[g, :, :, 2 * j * P:2 * (j + 1) * P])])

            @block.scalar
            def _(act):
                u = 0
                L.high(act, 0, 1)
                L.high(act, 1, 1)
                for i, (n, kind, g, j, m) in enumerate(outs):
                    if m == 0 and n + 2 < N:
                        L.high(act, n + 2, (n + 2) // 4 + 1, used=(s_out, done[n - 2]) if n >= 2 else None)
                    if kind == "down":
                        continue
                    act.wait_ge(s_out, i + 1)
                    if u >= 1:
                        act.wait_ge(s_alo, u)
                    nc.scalar.activation(r[:, 0:ntok], L.ps[i % 2][:, 0:ntok], ACT.Relu,
                                         scale=ASCALE ** 0.5 / WSCALE).then_inc(s_relu, 1)
                    act.wait_ge(s_sq, u + 1)
                    if g >= 2:
                        act.wait_ge(s_out, max(q for q, o in enumerate(outs) if o[1] == "down" and o[2] == g - 2) + 1)
                    nc.scalar.activation(aa[:, g % 2, 0, j, 0:ntok], r[:, 0:ntok], ACT.Copy).then_inc(s_ahi, 1)
                    u += 1

            @block.vector
            def _(dve):
                u = v = 0
                L.low(dve, 0)
                L.low(dve, 1)
                for i, (n, kind, g, j, m) in enumerate(outs):
                    if m == 0 and n + 2 < N:
                        L.low(dve, n + 2)
                    if kind == "up":
                        dve.wait_ge(s_relu, u + 1)
                        nc.vector.tensor_tensor(r[:, 0:ntok], r[:, 0:ntok], r[:, 0:ntok], ALU.mult).then_inc(s_sq, 1)
                        dve.wait_ge(s_ahi, u + 1)
                        nc.vector.tensor_tensor(aa[:, g % 2, 1, j, 0:ntok], r[:, 0:ntok], aa[:, g % 2, 0, j, 0:ntok],
                                                ALU.subtract).then_inc(s_alo, 1)
                        u += 1
                    else:
                        dve.wait_ge(s_out, i + 1)
                        if g == 0:
                            nc.vector.tensor_scalar(y[:, j, 0:ntok], L.ps[i % 2][:, 0:ntok],
                                                    1.0 / (WSCALE * ASCALE), None, ALU.mult).then_inc(s_ev, 1)
                        else:
                            if j == 0:
                                dve.wait_ge(s_ev, KT * g)
                            nc.vector.scalar_tensor_tensor(y[:, j, 0:ntok], L.ps[i % 2][:, 0:ntok],
                                                           1.0 / (WSCALE * ASCALE), y[:, j, 0:ntok], ALU.mult, ALU.add)\
                              .then_inc(s_ev, 1)
                        v += 1

            @block.tensor
            def _(pe):
                for i, (n, kind, g, j, m) in enumerate(outs):
                    if m == 0:
                        pe.wait_ge(L.s_lo, n + 1)
                    free(pe, i)
                    if kind == "up":
                        L.product(n, L.ps[i % 2], e.hh, 0, KT, 0, P, P, ntok).then_inc(s_out, 1)
                    else:
                        if j == 0:
                            pe.wait_ge(s_alo, MG * (g + 1))
                        L.product(n, L.ps[i % 2], aa[:, g % 2], 0, MG, m * P, P, 2 * P, ntok).then_inc(s_out, 1)


def residual(nc, e, sem, l, y, ntok, gate, nm, final=False):
    with ExitStack() as st:
        sb = lambda n, s, d=F32: st.enter_context(nc.sbuf_tensor(nm + n, s, d))
        S = lambda n: sem(nm + n)
        x = sb("x", [P, KT, TOK])
        sq = sb("sq", [P, 3, 512])
        stat = sb("stat", [P, 3, 512])
        ys = sb("ys", [P, 2, 512])
        xo = sb("xo", [P, 2, D]) if final else None
        ss = [st.enter_context(nc.psum_tensor(f"{nm}ss{i}", [P, 512], F32)) for i in range(2)]
        tp = [st.enter_context(nc.psum_tensor(f"{nm}tp{i}", [P, 4, P], F32)) for i in range(2)] if final else None
        s_x, s_sq, s_m, s_r0, s_d, s_sqm = (S("x_loaded"), S("squared"), S("mean"), S("rsqrt"), S("dve"), S("summed"))
        s_xn, s_tp, s_te = S("x_updated"), S("transposed"), S("evacuated")
        s_st = e.s_final if final else S("stored")
        cks = chunks(ntok)
        with nc.Block() as block:
            @block.sync
            def _(sp):
                for c, (a, n) in enumerate(cks):
                    sp.dma_start(x[:, :, a:a + n], e.x_dram[:, :, a:a + n]).then_inc(s_x, 16)
                    sp.wait_ge(s_x, 16 * (c + 1))
                if not final:
                    for c, (a, n) in enumerate(cks):
                        sp.wait_ge(s_xn, KT * (c + 1))
                        sp.dma_start(e.x_dram[:, :, a:a + n], x[:, :, a:a + n]).then_inc(s_st, 16)
                    sp.wait_ge(s_st, 16 * len(cks))
                else:
                    for t in range(ntok // P):
                        sp.wait_ge(s_te, 2 * (t + 1))
                        sp.dma_start(e.out[0, t * P:(t + 1) * P, :], xo[:, t % 2, :]).then_inc(s_st, 16)
                        sp.wait_ge(s_st, 16 * (t + 1))

            @block.scalar
            def _(act):
                i = 0
                for c, (a, n) in enumerate(cks):
                    for k in range(KT):
                        if i >= 3:
                            act.wait_ge(s_sqm, i - 2)
                        nc.scalar.activation(sq[:, i % 3, 0:n], y[:, k, a:a + n], ACT.Square).then_inc(s_sq, 1)
                        i += 1
                    act.wait_ge(s_m, c + 1)
                    nc.scalar.activation(stat[:, 1, 0:n], stat[:, 0, 0:n], ACT.Ln).then_inc(s_r0, 1)
                    act.wait_ge(s_r0, 2 * c + 1)
                    nc.scalar.activation(stat[:, 1, 0:n], stat[:, 1, 0:n], ACT.Exp, scale=-0.5).then_inc(s_r0, 1)

            @block.tensor
            def _(pe):
                i = 0
                for c, (a, n) in enumerate(cks):
                    if c >= 2:
                        pe.wait_ge(s_m, c - 1)
                    for k in range(KT):
                        pe.wait_ge(s_sq, i + 1)
                        nc.tensor.matmul(ss[c % 2][:, 0:n], e.ones[:, :], sq[:, i % 3, 0:n],
                                         start=(k == 0), stop=(k == KT - 1)).then_inc(s_sqm, 1)
                        i += 1
                if final:
                    for i in range(2 * ntok // P):
                        t, half = i // 2, i % 2
                        pe.wait_ge(s_xn, KT * (t * P // 512 + 1))
                        if i >= 2:
                            pe.wait_ge(s_te, i - 1)
                        for k in range(4):
                            last = nc.tensor.transpose(tp[i % 2][:, k, :], x[:, 4 * half + k, t * P:(t + 1) * P],
                                                       e.ident[:, :])
                        last.then_inc(s_tp, 1)

            @block.vector
            def _(dve):
                ch = Chain(s_d)
                for c, (a, n) in enumerate(cks):
                    dve.wait_ge(s_sqm, KT * (c + 1))
                    nc.vector.tensor_scalar(stat[:, 0, 0:n], ss[c % 2][:, 0:n], 1.0 / D, EPS, ALU.mult, ALU.add)\
                      .then_inc(s_m, 1)
                    dve.wait_ge(s_r0, 2 * c + 2)
                    newton(nc, dve, ch, stat[:, 0, 0:n], stat[:, 1, 0:n], stat[:, 2, 0:n])
                    dve.wait_ge(s_x, 16 * (c + 1))
                    for k in range(KT):
                        ch(nc.vector.tensor_tensor(ys[:, k % 2, 0:n], y[:, k, a:a + n], stat[:, 1, 0:n], ALU.mult))
                        ch.wait(dve)
                        who = int(a >= LAT)
                        nc.vector.scalar_tensor_tensor(x[:, k, a:a + n], ys[:, k % 2, 0:n],
                                                       e.mod[:, l, gate + k, who:who + 1], x[:, k, a:a + n],
                                                       ALU.mult, ALU.add).then_inc(s_xn, 1)
                        dve.wait_ge(s_xn, KT * c + k + 1)
                if final:
                    for i in range(2 * ntok // P):
                        t, half = i // 2, i % 2
                        dve.wait_ge(s_tp, i + 1)
                        if t >= 2:
                            dve.wait_ge(s_st, 16 * (t - 1))
                        nc.vector.tensor_copy(xo[:, t % 2, 512 * half:512 * half + 512],
                                              tp[i % 2][:, :, :].rearrange("p a b -> p (a b)")).then_inc(s_te, 1)


def mixers(nc, e, sem, l, stop):
    f = Env()
    with ExitStack() as st:
        sb = lambda n, s, d=F32, st=st, side="left": st.enter_context(nc.sbuf_tensor(f"{n}{l}", s, d, side=side))
        f.aq, f.ak = sb("aq", [P, 4, TOK]), sb("ak", [P, TOK])
        f.av = sb("av", [P, TT, 2, P], F16)
        with ExitStack() as low:
            f.bq, f.bkv = sb("bq", [P, 2, TOK], st=low, side="right"), sb("bkv", [P, TOK], st=low, side="right")
            with ExitStack() as st2:
                f.z = sb("z", [P, 4, TOK], st=st2)
                f.cq, f.cg = sb("cq", [P, 2, TOK], st=st2), sb("cg", [P, 2, TOK], st=st2)
                f.cv = sb("cv", [P, TT, 2 * P], st=st2)
                input_projection(nc, e, sem, l, f)
                if stop == f"mix{l}in":
                    return
                if stop != f"mix{l}at":
                    recurrence(nc, e, sem, l, f, stop)
                if stop in [f"mix{l}" + x for x in ("rec", "g", "s", "o")]:
                    return
            prepare_norms(nc, e, sem, l, f)
            if stop == f"mix{l}pa":
                return
            f.qb, f.kb = sb("qb", [97, 2, 4, TOK], F16), sb("kb", [97, 2, 4, TOK], F16)
            f.bv = sb("bv", [P, TT, 4, P], F16)
            prepare_latent(nc, e, sem, l, f)
            if stop == f"mix{l}pb":
                return
        attention(nc, e, sem, l, f)


MSHIFT = 8.3178


def halves(t, a, n):
    v = t.bitcast(F16)
    return v[:, 2 * a:2 * a + n], v[:, 2 * a + n:2 * a + 2 * n]


def prepare_norms(nc, e, sem, l, f):
    nq = TOK if l < DEPTH - 1 else LAT
    nm = f"pa{l}_"
    items = []
    for a, n in chunks(TOK):
        items.append(("rope", [f.ak[:, :]], [R_AK], e.pair, 64, 1.0, a, n))
        items.append(("flat", [f.bkv[:, :]], [R_BKV], e.ones, 128, 1.0, a, n))
        if a < nq:
            items += [("rope", [f.aq[:, t, :]], [R_AQ], e.pair, 64, 0.125, a, n) for t in range(4)]
            items.append(("flat", [f.bq[:, 0, :], f.bq[0:64, 1, :]], [R_BQ, R_BQ + 1], e.ones, 192, 1.0, a, n))
    N = len(items)
    with ExitStack() as st:
        sb = lambda n, s, d=F32: st.enter_context(nc.sbuf_tensor(nm + n, s, d))
        rope = sb("rope", [P, 2, TOK])
        sq = sb("sq", [P, 2, 2, 512])
        xg = sb("xg", [P, 2, 2, 512])
        m, r = sb("m", [P, 2, 512]), sb("r", [P, 2, 512])
        t1 = sb("t1", [P, 512])
        u = sb("u", [P, 2, 2, 512])
        pss = [st.enter_context(nc.psum_tensor(f"{nm}ss{i}", [P, 512], F32)) for i in range(2)]
        prot = [st.enter_context(nc.psum_tensor(f"{nm}rot{i}", [P, 512], F32)) for i in range(2)]
        s_rope, s_xg, s_pp, s_m, s_r, s_uc, s_u, s_hi, s_lo, s_d = (sem(nm + x) for x in (
            "rope_loaded", "gained", "products", "mean", "rsqrt", "cos_done", "u_ready", "hi", "lo", "dve"))
        with nc.Block() as block:
            @block.sync
            def _(sp):
                sp.dma_start(rope[:, :, :], e.k_rope[:, 0:2, :]).then_inc(s_rope, 16)
                sp.wait_ge(s_rope, 16)

            @block.scalar
            def _(act):
                def first(i):
                    _, xs, gs, _, _, _, a, n = items[i]
                    if i >= 2:
                        act.wait_ge(s_pp, i - 1)
                        act.wait_ge(s_u, i - 1)
                    for j, (x, g) in enumerate(zip(xs, gs)):
                        R = x.shape[0]
                        nc.scalar.activation(sq[0:R, i % 2, j, 0:n], x[:, a:a + n], ACT.Square)
                        last = nc.scalar.activation(xg[0:R, i % 2, j, 0:n], x[:, a:a + n], ACT.Copy,
                                                    scale=e.sv[0:R, l, g:g + 1])
                    last.then_inc(s_xg, 1)

                def second(i):
                    n = items[i][7]
                    act.wait_ge(s_m, i + 1)
                    nc.scalar.activation(r[:, i % 2, 0:n], m[:, i % 2, 0:n], ACT.Ln).then_inc(s_r, 1)
                    act.wait_ge(s_r, 2 * i + 1)
                    nc.scalar.activation(r[:, i % 2, 0:n], r[:, i % 2, 0:n], ACT.Exp, scale=-0.5).then_inc(s_r, 1)

                def third(i):
                    _, xs, _, _, _, _, a, n = items[i]
                    act.wait_ge(s_u, i + 1)
                    for j, x in enumerate(xs):
                        last = nc.scalar.activation(halves(x, a, n)[0], u[0:x.shape[0], i % 2, j, 0:n], ACT.Copy)
                    last.then_inc(s_hi, 1)

                first(0)
                for i in range(N):
                    if i + 1 < N:
                        first(i + 1)
                    second(i)
                    if i:
                        third(i - 1)
                third(N - 1)

            @block.tensor
            def _(pe):
                for i, (kind, xs, _, ones, _, _, a, n) in enumerate(items):
                    pe.wait_ge(s_xg, i + 1)
                    if i >= 2:
                        pe.wait_ge(s_u, i - 1)
                    for j, x in enumerate(xs):
                        R = x.shape[0]
                        last = nc.tensor.matmul(pss[i % 2][:, 0:n], ones[0:R, :], sq[0:R, i % 2, j, 0:n],
                                                start=(j == 0), stop=(j == len(xs) - 1))
                    if kind == "rope":
                        last = nc.tensor.matmul(prot[i % 2][:, 0:n], e.swap[:, 0, :], xg[:, i % 2, 0, 0:n],
                                                start=True, stop=True)
                    last.then_inc(s_pp, 1)

            @block.gpsimd
            def _(pool):
                pool.wait_ge(s_rope, 16)
                for i, (kind, _, _, _, _, _, a, n) in enumerate(items):
                    pool.wait_ge(s_xg, i + 1)
                    if i >= 2:
                        pool.wait_ge(s_lo, i - 1)
                    if kind == "rope":
                        nc.gpsimd.tensor_tensor(u[:, i % 2, 0, 0:n], xg[:, i % 2, 0, 0:n], rope[:, 0, a:a + n],
                                                ALU.mult).then_inc(s_uc, 1)

            @block.vector
            def _(dve):
                ch = Chain(s_d)

                def mean(i):
                    _, _, _, _, F, _, _, n = items[i]
                    dve.wait_ge(s_pp, i + 1)
                    nc.vector.tensor_scalar(m[:, i % 2, 0:n], pss[i % 2][:, 0:n], 1.0 / F, EPS, ALU.mult, ALU.add)\
                      .then_inc(s_m, 1)

                def low(i):
                    _, xs, _, _, _, _, a, n = items[i]
                    dve.wait_ge(s_hi, i + 1)
                    for j, x in enumerate(xs):
                        hi, lo = halves(x, a, n)
                        last = nc.vector.tensor_tensor(lo, u[0:x.shape[0], i % 2, j, 0:n], hi, ALU.subtract)
                    last.then_inc(s_lo, 1)

                dve.wait_ge(s_rope, 16)
                mean(0)
                ropes = 0
                for i, (kind, xs, _, _, _, fac, a, n) in enumerate(items):
                    if i + 1 < N:
                        mean(i + 1)
                    p = i % 2
                    dve.wait_ge(s_r, 2 * i + 2)
                    ch(nc.vector.tensor_tensor(t1[:, 0:n], m[:, p, 0:n], r[:, p, 0:n], ALU.mult))
                    ch.wait(dve)
                    ch(nc.vector.tensor_tensor(t1[:, 0:n], t1[:, 0:n], r[:, p, 0:n], ALU.mult))
                    ch.wait(dve)
                    ch(nc.vector.scalar_tensor_tensor(r[:, p, 0:n], t1[:, 0:n], 3.0, r[:, p, 0:n],
                                                      ALU.subtract, ALU.mult))
                    ch.wait(dve)
                    if kind == "rope":
                        ropes += 1
                        ch(nc.vector.tensor_tensor(t1[:, 0:n], prot[p][:, 0:n], rope[:, 1, a:a + n], ALU.mult))
                        ch.wait(dve)
                        dve.wait_ge(s_uc, ropes)
                        ch(nc.vector.tensor_tensor(u[:, p, 0, 0:n], u[:, p, 0, 0:n], t1[:, 0:n], ALU.add))
                        ch.wait(dve)
                        nc.vector.scalar_tensor_tensor(u[:, p, 0, 0:n], u[:, p, 0, 0:n], fac, r[:, p, 0:n],
                                                       ALU.mult, ALU.mult).then_inc(s_u, 1)
                    else:
                        if i >= 2:
                            dve.wait_ge(s_lo, i - 1)
                        for j, x in enumerate(xs):
                            R = x.shape[0]
                            last = nc.vector.tensor_tensor(u[0:R, p, j, 0:n], xg[0:R, p, j, 0:n], r[0:R, p, 0:n],
                                                           ALU.mult)
                        last.then_inc(s_u, 1)
                    if i:
                        low(i - 1)
                low(N - 1)
                dve.wait_ge(s_lo, N)


def prepare_latent(nc, e, sem, l, f):
    nq = TOK if l < DEPTH - 1 else LAT
    nm = f"pb{l}_"
    SC = 96.0 ** -0.5
    items = []
    for a, n in chunks(TOK):
        items.append(("kpe", 0, a, n))
        items += [("bk", h, a, n) for h in range(4)]
        if a < nq:
            items += [("bq", h, a, n) for h in range(4)]
    items += [("bv", t, 0, 256) for t in range(TT)]
    N = len(items)
    with ExitStack() as st:
        sb = lambda n, s, d=F32: st.enter_context(nc.sbuf_tensor(nm + n, s, d))
        rope = sb("rope", [P, 2, TOK])
        up = sb("up", [P, 3, 512])
        uw = sb("uw", [P, 2, 3, 512], F16)
        xg, u, t1 = sb("xg", [P, 2, 512]), sb("u", [P, 2, 512]), sb("t1", [P, 512])
        pup = [st.enter_context(nc.psum_tensor(f"{nm}up{i}", [P, 512], F32)) for i in range(2)]
        prot = [st.enter_context(nc.psum_tensor(f"{nm}rot{i}", [P, 512], F32)) for i in range(2)]
        s_rope, s_upl, s_uh, s_ul, s_one, s_p1, s_xg, s_p2, s_u, s_hi, s_lo, s_d = (sem(nm + x) for x in (
            "rope_loaded", "up_loaded", "up_hi", "up_lo", "ones_set", "up_done", "evacuated", "rotated", "u_ready",
            "hi", "lo", "dve"))
        bhi = lambda a, n: halves(f.bkv[:, :], a, n)
        rots = [sum(x[0] in ("kpe", "bq") for x in items[:i]) for i in range(N + 1)]
        ups = [sum(x[0] != "kpe" for x in items[:i]) for i in range(N + 1)]
        rows = {"kpe": (64, 96), "bq": (0, 96)}
        with nc.Block() as block:
            @block.sync
            def _(sp):
                sp.dma_start(rope[:, :, :], e.k_rope[:, 2:4, :]).then_inc(s_rope, 16)
                sp.dma_start(up[:, 0, 0:384], e.w_q_up[l, 0:P, :]).then_inc(s_upl, 16)
                sp.dma_start(up[0:64, 1, 0:384], e.w_q_up[l, P:192, :]).then_inc(s_upl, 16)
                sp.dma_start(up[:, 2, :], e.w_kv_up[l]).then_inc(s_upl, 16)

            @block.gpsimd
            def _(pool):
                nc.gpsimd.memset(f.kb[96:97, 0, :, :], 1.0).then_inc(s_one, 1)

            parts = ((P, 0, 384), (64, 1, 384), (P, 2, 512))

            @block.scalar
            def _(act):
                act.wait_ge(s_upl, 48)
                for R, j, n in parts:
                    nc.scalar.activation(uw[0:R, 0, j, 0:n], up[0:R, j, 0:n], ACT.Copy, scale=WSCALE).then_inc(s_uh, 1)

                def high(i):
                    kind, h, a, n = items[i]
                    if kind == "bk":
                        act.wait_ge(s_p1, ups[i] + 1)
                        nc.scalar.activation(f.kb[0:64, 0, h, a:a + n], pup[i % 2][0:64, 0:n], ACT.Copy,
                                             scale=1.0 / WSCALE).then_inc(s_hi, 1)
                    elif kind == "bv":
                        act.wait_ge(s_p1, ups[i] + 1)
                        nc.scalar.activation(f.bv[:, h, :, 0:64], pup[i % 2][:, 0:256].rearrange("p (h n) -> p h n", h=4),
                                             ACT.Copy, scale=1.0 / WSCALE).then_inc(s_hi, 1)
                    else:
                        lo, hi_ = rows[kind]
                        act.wait_ge(s_u, rots[i] + 1)
                        if kind == "kpe":
                            nc.scalar.activation(f.kb[lo:hi_, 0, :, a:a + n],
                                                 u[lo:hi_, i % 2, 0:n].unsqueeze(1).broadcast_to([32, 4, n]),
                                                 ACT.Copy).then_inc(s_hi, 1)
                        else:
                            nc.scalar.activation(f.qb[lo:hi_, 0, h, a:a + n], u[lo:hi_, i % 2, 0:n], ACT.Copy)\
                              .then_inc(s_hi, 1)

                for i in range(N + 1):
                    if i < N and items[i][0] in rows:
                        kind, h, a, n = items[i]
                        if i >= 2:
                            act.wait_ge(s_lo, i - 1)
                        if kind == "kpe":
                            nc.scalar.activation(xg[64:96, i % 2, 0:n], f.bq[64:96, 1, a:a + n], ACT.Copy)\
                              .then_inc(s_xg, 1)
                        else:
                            act.wait_ge(s_p1, ups[i] + 1)
                            nc.scalar.activation(xg[0:96, i % 2, 0:n], pup[i % 2][0:96, 0:n], ACT.Copy,
                                                 scale=SC / WSCALE).then_inc(s_xg, 1)
                    if i:
                        high(i - 1)

            @block.tensor
            def _(pe):
                pe.wait_ge(s_ul, 3)

                def rotate(i):
                    kind, h, a, n = items[i]
                    if kind in rows:
                        lo, hi_ = rows[kind]
                        pe.wait_ge(s_xg, rots[i] + 1)
                        nc.tensor.matmul(prot[i % 2][lo:hi_, 0:n], e.swap[lo:hi_, 1, lo:hi_], xg[lo:hi_, i % 2, 0:n],
                                         start=True, stop=True).then_inc(s_p2, 1)

                for i, (kind, h, a, n) in enumerate(items):
                    if i >= 2:
                        pe.wait_ge(s_lo, i - 1)
                    out = pup[i % 2]
                    passes = ((0, 0), (0, 1), (1, 0))
                    if kind == "bv":
                        ca = h * P // 512 * 512
                        cn = min(512, TOK - ca)
                        v = [x[:, h * P - ca:h * P - ca + P] for x in bhi(ca, cn)]
                        w = uw[:, :, 2, :].rearrange("p s (h n) -> p s h n", h=4)
                        for q, (xh, wh) in enumerate(passes):
                            last = nc.tensor.matmul(out[:, 0:256].rearrange("p (h n) -> p h n", h=4), v[xh],
                                                    w[:, wh, :, 64:128], start=(q == 0), stop=(q == 2))
                        last.then_inc(s_p1, 1)
                    elif kind == "bk":
                        v = bhi(a, n)
                        for q, (xh, wh) in enumerate(passes):
                            last = nc.tensor.matmul(out[0:64, 0:n], uw[:, wh, 2, h * P:h * P + 64], v[xh],
                                                    start=(q == 0), stop=(q == 2))
                        last.then_inc(s_p1, 1)
                    elif kind == "bq":
                        for j, R in ((0, P), (1, 64)):
                            v = halves(f.bq[0:R, j, :], a, n)
                            for q, (xh, wh) in enumerate(passes):
                                last = nc.tensor.matmul(out[0:96, 0:n], uw[0:R, wh, j, h * 96:(h + 1) * 96], v[xh],
                                                        start=(j == 0 and q == 0), stop=(j == 1 and q == 2))
                        last.then_inc(s_p1, 1)
                    else:
                        pass
                    if i:
                        rotate(i - 1)
                rotate(N - 1)

            @block.vector
            def _(dve):
                ch = Chain(s_d)
                dve.wait_ge(s_rope, 16)
                for q, (R, j, n) in enumerate(parts):
                    dve.wait_ge(s_uh, q + 1)
                    nc.vector.scalar_tensor_tensor(uw[0:R, 1, j, 0:n], up[0:R, j, 0:n], WSCALE, uw[0:R, 0, j, 0:n],
                                                   ALU.mult, ALU.subtract).then_inc(s_ul, 1)

                def low(i):
                    kind, h, a, n = items[i]
                    dve.wait_ge(s_hi, i + 1)
                    if kind == "bk":
                        last = nc.vector.scalar_tensor_tensor(f.kb[0:64, 1, h, a:a + n], pup[i % 2][0:64, 0:n],
                                                              1.0 / WSCALE, f.kb[0:64, 0, h, a:a + n],
                                                              ALU.mult, ALU.subtract)
                    elif kind == "bv":
                        last = nc.vector.scalar_tensor_tensor(f.bv[:, h, :, 64:128],
                                                              pup[i % 2][:, 0:256].rearrange("p (h n) -> p h n", h=4),
                                                              1.0 / WSCALE, f.bv[:, h, :, 0:64], ALU.mult, ALU.subtract)
                    elif kind == "kpe":
                        last = nc.vector.tensor_tensor(f.kb[64:96, 1, :, a:a + n],
                                                       u[64:96, i % 2, 0:n].unsqueeze(1).broadcast_to([32, 4, n]),
                                                       f.kb[64:96, 0, :, a:a + n], ALU.subtract)
                    else:
                        last = nc.vector.tensor_tensor(f.qb[0:96, 1, h, a:a + n], u[0:96, i % 2, 0:n],
                                                       f.qb[0:96, 0, h, a:a + n], ALU.subtract)
                    last.then_inc(s_lo, 1)

                for i, (kind, h, a, n) in enumerate(items):
                    if kind in rows:
                        lo, hi_ = rows[kind]
                        dve.wait_ge(s_xg, rots[i] + 1)
                        ch(nc.vector.tensor_tensor(u[lo:hi_, i % 2, 0:n], xg[lo:hi_, i % 2, 0:n],
                                                   rope[lo:hi_, 0, a:a + n], ALU.mult))
                    if i:
                        low(i - 1)
                    if kind in rows:
                        dve.wait_ge(s_p2, rots[i] + 1)
                        ch(nc.vector.tensor_tensor(t1[lo:hi_, 0:n], prot[i % 2][lo:hi_, 0:n],
                                                   rope[lo:hi_, 1, a:a + n], ALU.mult))
                        ch.wait(dve)
                        nc.vector.tensor_tensor(u[lo:hi_, i % 2, 0:n], u[lo:hi_, i % 2, 0:n], t1[lo:hi_, 0:n], ALU.add)\
                          .then_inc(s_u, 1)
                        dve.wait_ge(s_u, rots[i] + 1)
                low(N - 1)


def attention(nc, e, sem, l, f):
    nm = f"at{l}_"
    units = []
    for h in range(12):
        units.append((h, 0, LAT, list(range(TT))))
        if l < DEPTH - 1:
            units.append((h, LAT, CTX, [TT - 2, TT - 1]))
    U = len(units)
    key0 = lambda u: units[u][3][0] * P
    keyn = lambda u: len(units[u][3]) * P
    tasks, at = [], {}

    def put(u, s, t):
        at.setdefault((u, s), []).append(len(tasks))
        tasks.append(t)

    maxes = {u: [("max", u, q, c) for q in range(units[u][2] // P) for c in range(len(chunks(keyn(u))))]
             for u in range(U)}
    halfs = lambda u: range(len(chunks(units[u][2])))
    for t in maxes[0]:
        put(-1, 0, t)
    for c in halfs(0):
        put(-1, 0, ("row", 0, c))
    queue = [t for u in range(1, U) for t in maxes[u]]
    for u in range(U):
        nk = len(units[u][3])
        for s in range(nk):
            if nk > 2:
                ahead = [t for t in queue if t[1] == u + 1 or (t[1] == u + 2 and units[u + 1][2] < LAT)]
                for _ in range(-(-len(ahead) // max(1, nk - 1 - s))):
                    if ahead:
                        put(u, s, queue.pop(0))
                        ahead.pop(0)
            if s == 1 and u:
                put(u, s, ("sum", u - 1))
                for c in halfs(u - 1):
                    put(u, min(2, nk - 1), ("cast", u - 1, c))
        if u + 1 < U:
            assert not [t for t in queue if t[1] == u + 1]
            for c in halfs(u + 1):
                put(u, nk, ("row", u + 1, c))
    put(U, 1, ("sum", U - 1))
    for c in halfs(U - 1):
        put(U, 1, ("cast", U - 1, c))
    order = sorted(at, key=lambda w: (w[0], w[1]))
    for w in order:
        at[w].sort(key=lambda j: tasks[j][0] != "max")
    tasks_ = [tasks[j] for w in order for j in at[w]]
    n0 = 0
    for w in order:
        at[w] = list(range(n0, n0 + len(at[w])))
        n0 += len(at[w])
    tasks = tasks_
    NT = len(tasks)
    kinds = [t[0] for t in tasks]
    nth = lambda kind, i: kinds[:i + 1].count(kind)
    steps = [(u, s) for u in range(U) for s in range(len(units[u][3]))]
    base = {u: sum(len(units[v][3]) for v in range(u)) for u in range(U + 1)}
    with ExitStack() as st:
        sb = lambda n, s, d=F32: st.enter_context(nc.sbuf_tensor(nm + n, s, d))
        ps = lambda n, s, d=F32: st.enter_context(nc.psum_tensor(nm + n, s, d))
        qq, qs = sb("qq", [P, 2, TOK], F16), sb("qs", [65, 2, TOK], F16)
        kk, ks = sb("kk", [P, 2, TOK], F16), sb("ks", [65, 2, TOK], F16)
        p32, phi, plo = sb("p32", [P, 3, LAT]), sb("phi", [P, 3, LAT], F16), sb("plo", [P, 3, LAT], F16)
        acc = sb("acc", [P, 2, LAT])
        mx, neg = sb("mx", [P, 2, 8, 3]), sb("neg", [P, 2, 8])
        vlo, ov = sb("vlo", [64, LAT]), sb("ov", [64, 2, LAT])
        rc, o32 = sb("rc", [P, 8]), sb("o32", [P, LAT])
        sT = [ps(f"sT{i}", [P, LAT]) for i in range(2)]
        pv = ps("pv", [P, LAT])
        small = [ps(f"small{i}", [P, 512]) for i in range(2)]
        s_load = [sem(f"{nm}head_loaded{i}") for i in range(2)]
        (s_ones, s_task, s_max, s_neg, s_row, s_rec, s_S, s_e32, s_e16, s_lo, s_acc, s_pv, s_vlo, s_ov, s_o, s_d,
         s_mn, s_cp) = (sem(nm + x) for x in (
            "ones_set", "small_done", "max_read", "shift_ready", "row_written", "sum_read", "scores_done", "exp32",
            "exp16", "p_lo", "p_summed", "pv_done", "vlo_out", "pv_read", "o_written", "dve", "max_merged", "first_kept"))

        def released(eng, i):
            eng.wait_ge({"max": s_max, "row": s_row, "sum": s_rec, "cast": s_o}[kinds[i]], nth(kinds[i], i))

        def ops(u):
            h = units[u][0]
            if h < 8:
                p = h % 2
                return ([(kk[:, p, :], qq[:, p, :]), (ks[:, p, :], qs[:, p, :])], kk[0:64, p, :], qs[0:64, p, :],
                        qs[64:65, p, :])
            b = h - 8
            return ([(f.kb[0:97, 0, b, :], f.qb[0:97, 0, b, :]), (f.kb[0:96, 0, b, :], f.qb[0:96, 1, b, :]),
                     (f.kb[0:96, 1, b, :], f.qb[0:96, 0, b, :])], f.kb[0:96, 0, b, :], f.qb[0:96, 0, b, :],
                    f.qb[96:97, 0, b, :])

        values = lambda u, kt: f.av[:, kt, units[u][0] // 4, :] if units[u][0] < 8 else f.bv[:, kt, units[u][0] - 8, :]
        loads = 8 * 3
        nq = TOK if l < DEPTH - 1 else LAT
        first_unit = {}
        for u in range(U):
            first_unit.setdefault(units[u][0], u)

        with nc.Block() as block:
            @block.sync
            def _(sp):
                for h in range(8):
                    p, rows, kv = h % 2, slice(64 * (h % 2), 64 * (h % 2) + 64), h // 4
                    krows = slice(64 * kv, 64 * kv + 64)
                    if h >= 2:
                        sp.wait_ge(s_S, base[first_unit[h - 1]])
                    for a, n in chunks(TOK):
                        khi, klo = halves(f.ak[krows, :], a, n)
                        for dst, src in ((kk[0:64, p, a:a + n], khi), (kk[64:P, p, a:a + n], khi),
                                         (ks[0:64, p, a:a + n], klo)):
                            sp.dma_start(dst, src).then_inc(s_load[p], 16)
                        if a < nq:
                            qhi, qlo = halves(f.aq[rows, h // 2, :], a, n)
                            for dst, src in ((qq[0:64, p, a:a + n], qhi), (qq[64:P, p, a:a + n], qlo),
                                             (qs[0:64, p, a:a + n], qhi)):
                                sp.dma_start(dst, src).then_inc(s_load[p], 16)

            per_head = 16 * 3 * (len(chunks(TOK)) + len(chunks(nq)))

            @block.gpsimd
            def _(pool):
                nc.gpsimd.memset(ks[64:65, :, :], 1.0).then_inc(s_ones, 1)
                for i, (u, s) in enumerate(steps):
                    n = units[u][2]
                    if s == 0:
                        continue
                    pool.wait_ge(s_e32, i + 1)
                    if s == 1:
                        if u >= 2:
                            pool.wait_ge(s_task, max(j for j, t in enumerate(tasks) if t[:2] == ("sum", u - 2)) + 1)
                        nc.gpsimd.tensor_tensor(acc[:, u % 2, 0:n], p32[:, (i - 1) % 3, 0:n], p32[:, i % 3, 0:n],
                                                ALU.add).then_inc(s_acc, 1)
                    else:
                        pool.wait_ge(s_acc, i - u - 1)
                        nc.gpsimd.tensor_tensor(acc[:, u % 2, 0:n], acc[:, u % 2, 0:n], p32[:, i % 3, 0:n],
                                                ALU.add).then_inc(s_acc, 1)

            def summed(i):
                u, s = steps[i]
                return i - u if s else i - u + 1

            @block.scalar
            def _(act):
                def small_tasks(where):
                    for j in at.get(where, []):
                        kind, u = tasks[j][:2]
                        if kind == "row":
                            a, n = chunks(units[u][2])[tasks[j][2]]
                            q0 = units[u][1]
                            act.wait_ge(s_task, j + 1)
                            row = ops(u)[3]
                            R = 64 if units[u][0] < 8 else 96
                            nc.scalar.activation(row[:, q0 + a:q0 + a + n], small[j % 2][R:R + 1, 0:n], ACT.Copy)\
                              .then_inc(s_row, 1)

                def read_pv(u):
                    n = units[u][2]
                    act.wait_ge(s_pv, base[u + 1])
                    if u:
                        act.wait_ge(s_ov, u)
                    nc.scalar.activation(vlo[:, 0:n], pv[64:P, 0:n], ACT.Copy).then_inc(s_vlo, 1)

                small_tasks((-1, 0))
                for i, (u, s) in enumerate(steps):
                    n = units[u][2]
                    act.wait_ge(s_S, i + 1)
                    if i >= 3:
                        act.wait_ge(s_lo, i - 2)
                        act.wait_ge(s_acc, summed(i - 3))
                    nc.scalar.activation(p32[:, i % 3, 0:n], sT[i % 2][:, 0:n], ACT.Exp).then_inc(s_e32, 1)
                    if i >= 3:
                        act.wait_ge(s_pv, i - 2)
                    nc.scalar.activation(phi[:, i % 3, 0:n], sT[i % 2][:, 0:n], ACT.Exp).then_inc(s_e16, 1)
                    if s == 1 and u:
                        read_pv(u - 1)
                    small_tasks((u, s))
                    if s == len(units[u][3]) - 1:
                        small_tasks((u, s + 1))
                read_pv(U - 1)

            @block.vector
            def _(dve):
                ch = Chain(s_d)

                def small_tasks(where, which=("max", "sum", "cast")):
                    for j in at.get(where, []):
                        kind, u = tasks[j][:2]
                        if kind not in which:
                            continue
                        if kind == "max":
                            _, _, q, c = tasks[j]
                            n = chunks(keyn(u))[c][1]
                            dve.wait_ge(s_task, j + 1)
                            nc.vector.reduce_max(mx[:, u % 2, q, c:c + 1], small[j % 2][:, 0:n], AX.X).then_inc(s_max, 1)
                            if tasks[j] == maxes[u][-1]:
                                nqt, nc_ = units[u][2] // P, len(chunks(keyn(u)))
                                dve.wait_ge(s_max, nth("max", j))
                                ch(nc.vector.reduce_max(neg[:, u % 2, 0:nqt], mx[:, u % 2, 0:nqt, 0:nc_], AX.X))
                                ch.wait(dve)
                                nc.vector.tensor_scalar(neg[:, u % 2, 0:nqt], neg[:, u % 2, 0:nqt], -1.0, MSHIFT,
                                                        ALU.mult, ALU.add).then_inc(s_neg, 1)
                        elif kind == "sum":
                            dve.wait_ge(s_task, j + 1)
                            nqt = units[u][2] // P
                            nc.vector.reciprocal(rc[:, 0:nqt], small[j % 2][:, 0:nqt]).then_inc(s_rec, 1)
                        elif kind == "cast":
                            a, n = chunks(units[u][2])[tasks[j][2]]
                            R = 64 * (units[u][0] % 2)
                            dve.wait_ge(s_task, j + 1)
                            if ch.n:
                                ch.wait(dve)
                            nc.vector.tensor_tensor(o32[R:R + 64, a:a + n], ov[:, u % 2, a:a + n],
                                                    small[j % 2][0:64, 0:n], ALU.mult).then_inc(s_o, 1)
                            if a + n == units[u][2]:
                                dve.wait_ge(s_o, nth("cast", j))
                                finish(u)

                def finish(u):
                    h, q0, n, _ = units[u]
                    R = 64 * (h % 2)
                    hi, lo = (e.hh[R:R + 64, s, h // 2, q0:q0 + n] for s in range(2))
                    ch(nc.vector.tensor_copy(hi, o32[R:R + 64, 0:n]))
                    ch.wait(dve)
                    ch(nc.vector.tensor_tensor(lo, o32[R:R + 64, 0:n], hi, ALU.subtract))

                def read_pv(u):
                    n = units[u][2]
                    dve.wait_ge(s_vlo, u + 1)
                    nc.vector.tensor_tensor(ov[:, u % 2, 0:n], pv[0:64, 0:n], vlo[:, 0:n], ALU.add).then_inc(s_ov, 1)
                    dve.wait_ge(s_ov, u + 1)

                small_tasks((-1, 0))
                for i, (u, s) in enumerate(steps):
                    n = units[u][2]
                    small_tasks((u, s), ("max",))
                    dve.wait_ge(s_e16, i + 1)
                    if i >= 3:
                        dve.wait_ge(s_pv, i - 2)
                    nc.vector.tensor_tensor(plo[:, i % 3, 0:n], p32[:, i % 3, 0:n], phi[:, i % 3, 0:n], ALU.subtract)\
                      .then_inc(s_lo, 1)
                    if s == 1 and u:
                        read_pv(u - 1)
                    small_tasks((u, s), ("sum", "cast"))
                read_pv(U - 1)
                small_tasks((U, 1))

            @block.tensor
            def _(pe):
                loaded = set()

                def small_tasks(where, part=slice(None)):
                    for j in at.get(where, [])[part]:
                        kind, u = tasks[j][:2]
                        h, q0, n, kts = units[u]
                        if kind == "max" and h < 8 and h not in loaded:
                            pe.wait_ge(s_load[h % 2], per_head * (h // 2 + 1))
                            loaded.add(h)
                        if j >= 2:
                            released(pe, j - 2)
                        out = small[j % 2]
                        if kind == "max":
                            _, _, q, c = tasks[j]
                            a, w = chunks(keyn(u))[c]
                            _, k, qh, _ = ops(u)
                            last = nc.tensor.matmul(out[:, 0:w], qh[:, q0 + q * P:q0 + (q + 1) * P],
                                                    k[:, key0(u) + a:key0(u) + a + w], start=True, stop=True)
                        elif kind == "row":
                            a, w = chunks(n)[tasks[j][2]]
                            R = 64 if h < 8 else 96
                            pe.wait_ge(s_neg, u + 1)
                            for q in range(w // P):
                                last = nc.tensor.matmul(out[R:R + 1, q * P:(q + 1) * P],
                                                        neg[:, u % 2, a // P + q:a // P + q + 1], e.ident[:, :],
                                                        start=True, stop=True)
                        elif kind == "sum":
                            pe.wait_ge(s_acc, base[u + 1] - u - 1)
                            for q in range(n // P):
                                last = nc.tensor.matmul(out[:, q:q + 1], acc[:, u % 2, q * P:(q + 1) * P],
                                                        e.ones[:, 0:1], start=True, stop=True)
                        else:
                            a, w = chunks(n)[tasks[j][2]]
                            pe.wait_ge(s_rec, u + 1)
                            for q in range(w // P):
                                last = nc.tensor.matmul(out[0:64, q * P:(q + 1) * P],
                                                        rc[:, a // P + q:a // P + q + 1].broadcast_to([P, 64]),
                                                        e.ident[:, :], start=True, stop=True)
                        last.then_inc(s_task, 1)

                def weighted(i):
                    u, s = steps[i]
                    n, kts = units[u][2:]
                    pe.wait_ge(s_lo, i + 1)
                    if s == 0 and u:
                        pe.wait_ge(s_ov, u)
                    v = values(u, kts[s])
                    for a, w in chunks(n):
                        nc.tensor.matmul(pv[:, a:a + w], v, phi[:, i % 3, a:a + w], start=(s == 0), stop=False,
                                         skip_group_check=True)
                        last = nc.tensor.matmul(pv[0:64, a:a + w], v[:, 0:64], plo[:, i % 3, a:a + w],
                                                start=False, stop=(s == len(kts) - 1), skip_group_check=True)
                    last.then_inc(s_pv, 1)

                pe.wait_ge(s_ones, 1)
                small_tasks((-1, 0))
                rows = len(chunks(units[0][2]))
                for i, (u, s) in enumerate(steps):
                    h, q0, n, kts = units[u]
                    if s == 0:
                        done = max(j for j, t in enumerate(tasks) if t[:2] == ("row", u))
                        pe.wait_ge(s_row, nth("row", done))
                    if i >= 2:
                        pe.wait_ge(s_e16, i - 1)
                    pairs = ops(u)[0]
                    K = slice(kts[s] * P, (kts[s] + 1) * P)
                    for a, w in chunks(n):
                        for j, (k, q) in enumerate(pairs):
                            last = nc.tensor.matmul(sT[i % 2][:, a:a + w], k[:, K], q[:, q0 + a:q0 + a + w],
                                                    start=(j == 0), stop=(j == len(pairs) - 1))
                    last.then_inc(s_S, 1)
                    early = sum(tasks[j][0] == "max" for j in at.get((u, s), [])[0:2])
                    small_tasks((u, s), slice(0, early))
                    if i >= 2:
                        weighted(i - 2)
                    small_tasks((u, s), slice(early, None))
                    if s == len(kts) - 1:
                        small_tasks((u, s + 1))
                weighted(len(steps) - 2)
                weighted(len(steps) - 1)
                small_tasks((U, 1))


ORDER = {"f": [8, 9, 0, 1, 2, 3, 4, 5, 6, 7], "b": [9, 8, 7, 6, 5, 4, 3, 2, 1, 0]}


def gates(nc, e, sem, l, f):
    nm = f"ga{l}_"
    nq = TOK if l < DEPTH - 1 else LAT
    items = [("z", n, TOK) for n in range(4)] + [("q", i, nq) for i in range(2)] + [("g", i, nq) for i in range(2)]
    with ExitStack() as st:
        t = e.hh[:, 0, 0:6, :].rearrange("p a b -> p (a b)").bitcast(F32).rearrange("p (a b) -> p a b", a=3)
        t2 = e.hh[:, 1, 0:6, :].rearrange("p a b -> p (a b)").bitcast(F32).rearrange("p (a b) -> p a b", a=3)
        s_c, s_e, s_f, s_g, s_d, s_z0 = (sem(nm + x) for x in ("clamped", "exp", "f_ready", "logs", "dve", "zeroed"))
        src = lambda kind, i: {"z": f.z, "q": f.cq, "g": f.cg}[kind][:, i, :]
        with nc.Block() as block:
            @block.gpsimd
            def _(pool):
                nc.gpsimd.memset(f.cc[:, :, :, 0:1], 0.0).then_inc(s_z0, 1)
                pool.wait_ge(s_z0, 1)

            @block.scalar
            def _(act):
                for i, (kind, n, w) in enumerate(items):
                    act.wait_ge(s_c, i + 1)
                    nc.scalar.activation(t[:, i % 2, 0:w], t[:, i % 2, 0:w], ACT.Exp, scale=-1.0).then_inc(s_e, 1)
                    if kind == "z":
                        act.wait_ge(s_f, i + 1)
                        nc.scalar.activation(t2[:, 0, :], t2[:, 0, :], ACT.Ln)
                        nc.scalar.activation(t2[:, 1, :], t2[:, 1, :], ACT.Ln).then_inc(s_g, 1)

            @block.vector
            def _(dve):
                ch = Chain(s_d)

                def clamp(i):
                    kind, n, w = items[i]
                    nc.vector.tensor_scalar(t[:, i % 2, 0:w], src(kind, n)[:, 0:w], -80.0, None, ALU.max)\
                      .then_inc(s_c, 1)

                clamp(0)
                for i, (kind, n, w) in enumerate(items):
                    if i:
                        ch.wait(dve)
                    if i + 1 < len(items):
                        clamp(i + 1)
                    dve.wait_ge(s_e, i + 1)
                    x, ez, sg = src(kind, n)[:, 0:w], t[:, i % 2, 0:w], t[:, 2, 0:w]
                    ch(nc.vector.tensor_scalar_add(sg, ez, 1.0))
                    ch.wait(dve)
                    ch(nc.vector.reciprocal(sg, sg))
                    ch.wait(dve)
                    if kind == "z":
                        c = 2 + n if n < 2 else n - 2
                        lb, om = e.lb[:, l, 0, c:c + 1], e.lb[:, l, 1, c:c + 1]
                        if i:
                            dve.wait_ge(s_g, i)
                        ch(nc.vector.scalar_tensor_tensor(x, ez, om, sg, ALU.mult, ALU.mult))
                        ch(nc.vector.tensor_scalar(t2[:, 2, :], sg, om, lb, ALU.mult, ALU.add))
                        ch.wait(dve)
                        ch(nc.vector.tensor_scalar(t2[:, 1, :], t2[:, 2, :], 1e15, 1.0, ALU.mult, ALU.min))
                        ch.wait(dve)
                        ch(nc.vector.tensor_scalar(t2[:, 1, :], t2[:, 1, :], 1e-15, None, ALU.max))
                        ch.wait(dve)
                        nc.vector.tensor_scalar(t2[:, 0, :], t2[:, 2, :], 1e-15, None, ALU.max).then_inc(s_f, 1)
                        dve.wait_ge(s_g, i + 1)
                        ch(nc.vector.tensor_tensor(t2[:, 0, :], t2[:, 0, :], t2[:, 1, :], ALU.add))
                        ch.wait(dve)
                        for b in range(TT):
                            g = t2[:, 0, b * BLK:(b + 1) * BLK]
                            ch(nc.vector.tensor_tensor_scan(f.cc[:, n, b, 1:BLK + 1], e.ones[:, :], g, 0.0,
                                                            ALU.mult, ALU.add))
                    elif kind == "q":
                        ch(nc.vector.tensor_tensor(x, x, sg, ALU.mult))
                    else:
                        ch(nc.vector.scalar_tensor_tensor(x, x, e.sv[:, l, R_CO:R_CO + 1], sg, ALU.mult, ALU.mult))


def states(nc, e, sem, l, f):
    nm = f"st{l}_"
    with ExitStack() as st:
        sb = lambda n, s, d=F32: st.enter_context(nc.sbuf_tensor(nm + n, s, d))
        arg = sb("arg", [P, 2, 4, BLK])
        kd, kt = sb("kd", [P, 2, 4, BLK]), sb("kt", [P, 2, 4, BLK])
        ds, dec = sb("ds", [P, TT, 4, 64]), sb("dec", [P, 4, TT])
        tp = [st.enter_context(nc.psum_tensor(f"{nm}tp{i}", [P, 4, BLK], F32)) for i in range(2)]
        pd = [st.enter_context(nc.psum_tensor(f"{nm}pd{i}", [P, 4, BLK], F32)) for i in range(2)]
        s_arg, s_e, s_dec, s_kd, s_tp, s_kt, s_pd, s_ds, s_d, s_z = (sem(nm + x) for x in (
            "arg", "exp", "decay", "kd", "transposed", "kt", "increments", "ds", "dve", "zeroed"))
        with nc.Block() as block:
            @block.gpsimd
            def _(pool):
                nc.gpsimd.memset(f.st[:, 0:2, ORDER["b"][0], :], 0.0).then_inc(s_z, 1)
                nc.gpsimd.memset(f.st[:, 2:4, ORDER["f"][0], :], 0.0).then_inc(s_z, 1)

            @block.scalar
            def _(act):
                nc.scalar.activation(dec[:, :, :], f.cc[:, :, :, BLK], ACT.Exp).then_inc(s_dec, 1)
                for b in range(TT + 1):
                    if b < TT:
                        act.wait_ge(s_arg, b + 1)
                        nc.scalar.activation(arg[:, b % 2, :, :], arg[:, b % 2, :, :], ACT.Exp).then_inc(s_e, 1)
                    if b:
                        act.wait_ge(s_tp, b)
                        if b >= 3:
                            act.wait_ge(s_pd, b - 2)
                        nc.scalar.activation(kt[:, (b - 1) % 2, :, :], tp[(b - 1) % 2][:, :, :], ACT.Copy)\
                          .then_inc(s_kt, 1)

            @block.tensor
            def _(pe):
                for b in range(TT + 1):
                    if b < TT:
                        pe.wait_ge(s_kd, b + 1)
                        if b >= 2:
                            pe.wait_ge(s_kt, b - 1)
                        for n in range(4):
                            last = nc.tensor.transpose(tp[b % 2][:, n, :], kd[:, b % 2, n, :], e.ident[:, :])
                        last.then_inc(s_tp, 1)
                    if b:
                        c = b - 1
                        pe.wait_ge(s_kt, c + 1)
                        if c >= 2:
                            pe.wait_ge(s_ds, 2 * (c - 1))
                        for n in range(4):
                            last = nc.tensor.matmul(pd[c % 2][:, n, :], kt[:, c % 2, n, :],
                                                    f.cv[:, c, (n % 2) * P:(n % 2 + 1) * P], start=True, stop=True)
                        last.then_inc(s_pd, 1)

            @block.vector
            def _(dve):
                ch = Chain(s_d)

                def args(b):
                    if b >= 2:
                        dve.wait_ge(s_kd, b - 1)
                    nc.vector.tensor_copy(arg[:, b % 2, 0:2, :], f.cc[:, 0:2, b, 0:BLK])
                    nc.vector.tensor_tensor(arg[:, b % 2, 2:4, :],
                                            f.cc[:, 2:4, b, BLK:BLK + 1].broadcast_to([P, 2, BLK]),
                                            f.cc[:, 2:4, b, 1:BLK + 1], ALU.subtract).then_inc(s_arg, 1)

                args(0)
                for b in range(TT + 1):
                    if b + 1 < TT:
                        args(b + 1)
                    if b < TT:
                        dve.wait_ge(s_e, b + 1)
                        if b >= 2:
                            dve.wait_ge(s_tp, b - 1)
                        nc.vector.tensor_tensor(kd[:, b % 2, :, :], arg[:, b % 2, :, :],
                                                f.z[:, :, b * BLK:(b + 1) * BLK], ALU.mult).then_inc(s_kd, 1)
                    if b:
                        c = b - 1
                        dve.wait_ge(s_pd, c + 1)
                        for hp in range(2):
                            R = slice(64 * hp, 64 * hp + 64)
                            nc.vector.tensor_copy(ds[R, c, :, :], pd[c % 2][R, :, 64 * hp:64 * hp + 64])\
                              .then_inc(s_ds, 1)
                dve.wait_ge(s_z, 2)
                dve.wait_ge(s_dec, 1)
                dve.wait_ge(s_ds, 2 * TT)
                for i in range(TT - 1):
                    if i:
                        ch.wait(dve)
                    for n in range(4):
                        o = ORDER["b" if n < 2 else "f"]
                        ch(nc.vector.scalar_tensor_tensor(f.st[:, n, o[i + 1], :], f.st[:, n, o[i], :],
                                                          dec[:, n, o[i]:o[i] + 1], ds[:, o[i], n, :],
                                                          ALU.mult, ALU.add))


def outputs(nc, e, sem, l, f):
    nm = f"ro{l}_"
    nb = TT if l < DEPTH - 1 else LAT // P
    NL = len(LEVELS)
    with ExitStack() as st:
        sb = lambda n, s, d=F32: st.enter_context(nc.sbuf_tensor(nm + n, s, d))
        X = [e.hh[:, i, 0:6, :].rearrange("p a b -> p (a b)").bitcast(F32)[:, 0:4 * NL * BLK]
             .rearrange("p (n l t) -> p n l t", n=4, l=NL) for i in range(2)]
        val = sb("val", [P, 2, 4, BLK])
        dk = sb("dk", [P, 2, 4, BLK])
        ks = sb("ks", [P, 2, 2, BLK])
        A = sb("A", [P, 2, 2, 2, BLK])
        sc = [[st.enter_context(nc.psum_tensor(f"{nm}sc{i}{j}", [P, 2, 2, BLK], F32)) for j in range(2)] for i in range(2)]
        po = [st.enter_context(nc.psum_tensor(f"{nm}po{i}", [P, 2, BLK], F32)) for i in range(2)]
        s_val, s_a1, s_a2, s_e, s_x, s_sc, s_cp, s_A, s_o, s_ov, s_d, s_dk = (sem(nm + x) for x in (
            "val", "first_halves", "second_halves", "exp", "x", "scores", "level_copied", "scores_merged", "o", "o_out",
            "dve", "edge_decay"))

        def half(t, h, which):
            return t.rearrange("p n (s w h) -> p n s w h", w=2, h=h)[:, :, :, which, :]

        def mid(b, h):
            v = f.cc[:, :, b, h:BLK:2 * h] if h < 64 else f.cc[:, :, b, 64:65]
            return v.unsqueeze(3).broadcast_to([P, 4, BLK // (2 * h), h])

        with nc.Block() as block:
            @block.gpsimd
            def _(pool):
                for b in range(nb):
                    pool.wait_ge(s_val, b + 1)
                    if b >= 2:
                        pool.wait_ge(s_o, b - 1)
                    for i, h in enumerate(LEVELS):
                        last = nc.gpsimd.tensor_tensor(half(X[b % 2][:, :, i, :], h, 0), mid(b, h),
                                                       half(val[:, b % 2, :, :], h, 0), ALU.subtract)
                    last.then_inc(s_a1, 1)

            @block.scalar
            def _(act):
                def merge(r, b):
                    act.wait_ge(s_sc, 4 * b + 1)
                    if b >= 2:
                        act.wait_ge(s_o, b - 1)
                    for par in range(2):
                        nc.scalar.activation(A[:, b % 2, par, :, :], sc[0][par][:, 0, :, :], ACT.Copy).then_inc(s_cp, 1)
                    act.wait_ge(s_cp, 6 * b + 2)
                    for par in range(2):
                        for q in range(2):
                            R = slice(64 * q, 64 * q + 64)
                            nc.scalar.activation(A[R, b % 2, par, :, R], sc[0][par][R, 1, :, R], ACT.Copy)\
                              .then_inc(s_cp, 1)

                for b in range(nb + 1):
                    if b < nb:
                        act.wait_ge(s_dk, b + 1)
                        nc.scalar.activation(dk[:, b % 2, :, :], dk[:, b % 2, :, :], ACT.Exp).then_inc(s_e, 1)
                        act.wait_ge(s_a1, b + 1)
                        act.wait_ge(s_a2, b + 1)
                        x = X[b % 2].rearrange("p n l t -> p (n l t)")
                        nc.scalar.activation(x, x, ACT.Exp).then_inc(s_e, 1)
                        merge(0, b)
                    if b:
                        act.wait_ge(s_o, b)
                        nc.scalar.activation(f.cq[:, :, (b - 1) * BLK:b * BLK], po[(b - 1) % 2][:, :, :], ACT.Copy)\
                          .then_inc(s_ov, 1)

            @block.vector
            def _(dve):
                ch = Chain(s_d)

                def values(b):
                    if b >= 2:
                        dve.wait_ge(s_e, 2 * (b - 1))
                        dve.wait_ge(s_o, b - 1)
                    last_ = f.cc[:, 0:2, b, BLK:BLK + 1].broadcast_to([P, 2, BLK])
                    nc.vector.tensor_copy(val[:, b % 2, 0:2, :], f.cc[:, 0:2, b, 0:BLK])
                    ch(nc.vector.tensor_copy(val[:, b % 2, 2:4, :], f.cc[:, 2:4, b, 1:BLK + 1]))
                    ch(nc.vector.tensor_tensor(dk[:, b % 2, 0:2, :], last_, f.cc[:, 0:2, b, 0:BLK], ALU.subtract))
                    nc.vector.tensor_copy(dk[:, b % 2, 2:4, :], f.cc[:, 2:4, b, 1:BLK + 1]).then_inc(s_dk, 1)
                    ch.wait(dve)
                    nc.vector.tensor_tensor(ks[:, b % 2, :, :], f.z[:, 0:2, b * BLK:(b + 1) * BLK],
                                            f.z[:, 2:4, b * BLK:(b + 1) * BLK], ALU.add).then_inc(s_val, 1)
                    for i, h in enumerate(LEVELS):
                        last = nc.vector.tensor_tensor(half(X[b % 2][:, :, i, :], h, 1),
                                                       half(val[:, b % 2, :, :], h, 1), mid(b, h), ALU.subtract)
                    last.then_inc(s_a2, 1)

                values(0)
                for b in range(nb):
                    B = slice(b * BLK, (b + 1) * BLK)
                    if b + 1 < nb:
                        values(b + 1)
                    dve.wait_ge(s_e, 2 * b + 2)
                    x = X[b % 2]
                    q, k = f.cq[:, :, B], f.z[:, :, B]
                    for d in range(2):
                        n = slice(2 * d, 2 * d + 2)
                        nc.vector.tensor_tensor(dk[:, b % 2, n, :], dk[:, b % 2, n, :], q, ALU.mult)
                    for i, h in enumerate(LEVELS):
                        for d in range(2):
                            n = slice(2 * d, 2 * d + 2)
                            xq, xk = half(x[:, n, i, :], h, d), half(x[:, n, i, :], h, 1 - d)
                            nc.vector.tensor_tensor(xq, xq, half(q, h, d), ALU.mult)
                            last = nc.vector.tensor_tensor(xk, xk, half(k[:, n, :], h, 1 - d), ALU.mult)
                    last.then_inc(s_x, 1)
                    dve.wait_ge(s_cp, 6 * (b + 1))
                    for r in range(1, 4):
                        dve.wait_ge(s_sc, 4 * b + r + 1)
                        for lv in range(2):
                            i = 2 * r + lv
                            for par in range(2):
                                mask = e.same[:, i, :].unsqueeze(1).broadcast_to([P, 2, BLK])
                                ins = nc.vector.copy_predicated(A[:, b % 2, par, :, :], mask, sc[r % 2][par][:, lv, :, :])
                                ins.then_inc(s_A, 1)
                            dve.wait_ge(s_A, 12 * b + 4 * (r - 1) + 2 * lv + 2)

            @block.tensor
            def _(pe):
                for b in range(nb):
                    pe.wait_ge(s_x, b + 1)
                    x = X[b % 2]
                    B = slice(b * BLK, (b + 1) * BLK)
                    for r in range(4):
                        if r >= 2:
                            if r == 2:
                                pe.wait_ge(s_cp, 6 * (b + 1))
                            else:
                                pe.wait_ge(s_A, 12 * b + 4)
                        elif b:
                            pe.wait_ge(s_A, 12 * (b - 1) + (8 if r == 0 else 12))
                        for lv in range(2):
                            i = 2 * r + lv
                            for par in range(2):
                                R = slice(64 * par, 64 * par + 64)
                                for pr in range(2):
                                    out = sc[r % 2][par][:, lv, pr, :]
                                    if i < NL:
                                        h = LEVELS[i]
                                        for d in range(2):
                                            xs = x[R, 2 * d + pr, i, :]
                                            v = lambda t: t.rearrange("p (s w h) -> p s w h", w=2, h=h)[:, :, d, :]
                                            last = nc.tensor.matmul(v(out), xs, v(xs), start=True, stop=True)
                                    else:
                                        last = nc.tensor.matmul(out, ks[R, b % 2, pr, :], f.cq[R, pr, B],
                                                                start=True, stop=True)
                        last.then_inc(s_sc, 1)
                    if b >= 2:
                        pe.wait_ge(s_ov, b - 1)
                    for pr in range(2):
                        for par in range(2):
                            R = slice(64 * par, 64 * par + 64)
                            for d in range(2):
                                n = 2 * d + pr
                                nc.tensor.matmul(po[b % 2][R, pr, :], f.st[R, n, b, :], dk[R, b % 2, n, :],
                                                 start=(d == 0 and pr == 0), stop=False, skip_group_check=True)
                    pe.wait_ge(s_A, 12 * (b + 1))
                    for pr in range(2):
                        for par in range(2):
                            R = slice(64 * par, 64 * par + 64)
                            hd = 2 * pr + par
                            last = nc.tensor.matmul(po[b % 2][R, pr, :], f.cv[:, b, 64 * hd:64 * hd + 64],
                                                    A[:, b % 2, par, pr, :], start=False, stop=True,
                                                    skip_group_check=True)
                    last.then_inc(s_o, 1)


def readout(nc, e, sem, l, f):
    nm = f"rd{l}_"
    nq = TOK if l < DEPTH - 1 else LAT
    items = [(i, a, n) for i in range(2) for a, n in chunks(nq)]
    N = len(items)
    with ExitStack() as st:
        sb = lambda n, s, d=F32: st.enter_context(nc.sbuf_tensor(nm + n, s, d))
        sq, m, r = sb("sq", [P, 2, 512]), sb("m", [P, 2, 512]), sb("r", [P, 2, 512])
        t1, u = sb("t1", [P, 512]), sb("u", [P, 2, 512])
        pss = [st.enter_context(nc.psum_tensor(f"{nm}ss{i}", [P, 512], F32)) for i in range(2)]
        s_sq, s_pp, s_m, s_r, s_u, s_hi, s_d = (sem(nm + x) for x in (
            "squared", "sums", "mean", "rsqrt", "u_ready", "hi", "dve"))
        with nc.Block() as block:
            @block.scalar
            def _(act):
                def square(i):
                    t, a, n = items[i]
                    if i >= 2:
                        act.wait_ge(s_pp, i - 1)
                    nc.scalar.activation(sq[:, i % 2, 0:n], f.cq[:, t, a:a + n], ACT.Square).then_inc(s_sq, 1)

                def high(i):
                    t, a, n = items[i]
                    act.wait_ge(s_u, i + 1)
                    nc.scalar.activation(e.hh[:, 0, 6 + t, a:a + n], u[:, i % 2, 0:n], ACT.Copy).then_inc(s_hi, 1)

                square(0)
                for i, (t, a, n) in enumerate(items):
                    if i + 1 < N:
                        square(i + 1)
                    act.wait_ge(s_m, i + 1)
                    nc.scalar.activation(r[:, i % 2, 0:n], m[:, i % 2, 0:n], ACT.Ln).then_inc(s_r, 1)
                    act.wait_ge(s_r, 2 * i + 1)
                    nc.scalar.activation(r[:, i % 2, 0:n], r[:, i % 2, 0:n], ACT.Exp, scale=-0.5).then_inc(s_r, 1)
                    if i:
                        high(i - 1)
                high(N - 1)

            @block.tensor
            def _(pe):
                for i, (t, a, n) in enumerate(items):
                    pe.wait_ge(s_sq, i + 1)
                    if i >= 2:
                        pe.wait_ge(s_m, i - 1)
                    nc.tensor.matmul(pss[i % 2][:, 0:n], e.pair[:, :], sq[:, i % 2, 0:n], start=True, stop=True)\
                      .then_inc(s_pp, 1)

            @block.vector
            def _(dve):
                ch = Chain(s_d)

                def mean(i):
                    n = items[i][2]
                    dve.wait_ge(s_pp, i + 1)
                    nc.vector.tensor_scalar(m[:, i % 2, 0:n], pss[i % 2][:, 0:n], 1.0 / 64, EPS, ALU.mult, ALU.add)\
                      .then_inc(s_m, 1)

                def low(i):
                    t, a, n = items[i]
                    dve.wait_ge(s_hi, i + 1)
                    ch(nc.vector.tensor_tensor(e.hh[:, 1, 6 + t, a:a + n], u[:, i % 2, 0:n], e.hh[:, 0, 6 + t, a:a + n],
                                               ALU.subtract))

                mean(0)
                for i, (t, a, n) in enumerate(items):
                    if i + 1 < N:
                        mean(i + 1)
                    p = i % 2
                    dve.wait_ge(s_r, 2 * i + 2)
                    newton(nc, dve, ch, m[:, p, 0:n], r[:, p, 0:n], t1[:, 0:n])
                    ch(nc.vector.tensor_tensor(t1[:, 0:n], f.cq[:, t, a:a + n], f.cg[:, t, a:a + n], ALU.mult))
                    ch.wait(dve)
                    nc.vector.tensor_tensor(u[:, p, 0:n], t1[:, 0:n], r[:, p, 0:n], ALU.mult).then_inc(s_u, 1)
                    dve.wait_ge(s_u, i + 1)
                    if i:
                        low(i - 1)
                low(N - 1)


def recurrence(nc, e, sem, l, f, stop=None):
    with ExitStack() as st:
        f.cc = st.enter_context(nc.sbuf_tensor(f"cc{l}", [P, 4, TT, BLK + 1], F32))
        f.st = st.enter_context(nc.sbuf_tensor(f"st{l}", [P, 4, TT, 64], F32))
        gates(nc, e, sem, l, f)
        if stop == f"mix{l}g":
            return
        states(nc, e, sem, l, f)
        if stop == f"mix{l}s":
            return
        outputs(nc, e, sem, l, f)
        if stop == f"mix{l}o":
            return
        readout(nc, e, sem, l, f)


def build(nc, e, sem, stop):
    setup_phase(nc, e, sem)
    if stop == "setup":
        return
    for l in range(DEPTH):
        nq = TOK if l < DEPTH - 1 else LAT
        norm_phase(nc, e, sem, None, TOK, (8, 0, l), True, f"n{l}_")
        if stop == f"norm{l}":
            return
        mixers(nc, e, sem, l, stop)
        if stop and stop.startswith(f"mix{l}"):
            return
        with nc.sbuf_tensor(f"y{l}", [P, KT, TOK], F32) as y:
            output_projection(nc, e, sem, l, y, nq)
            if stop == f"out{l}":
                return
            residual(nc, e, sem, l, y, nq, 16, f"r{l}_")
        e.recycle()
        norm_phase(nc, e, sem, None, nq, (32, 24, l), True, f"nf{l}_")
        if stop == f"normf{l}":
            return
        with nc.sbuf_tensor(f"yf{l}", [P, KT, TOK], F32) as y:
            mlp(nc, e, sem, l, y, nq)
            if stop == f"mlp{l}":
                return
            residual(nc, e, sem, l, y, nq, 40, f"rf{l}_", final=(l == DEPTH - 1))
        if stop == f"layer{l}":
            return
        if l < DEPTH - 1:
            e.recycle()


def shape_constants():
    f = np.float32
    tok = np.arange(LAT)
    row, col = (tok // 64).astype(f), (tok % 64).astype(f)

    def tables(rot, lead):
        nf = rot // 4
        inv = (f(10000.0) ** (-(np.arange(nf, dtype=f)) / f(nf))).astype(f)
        ang = np.concatenate([row[:, None] * inv, col[:, None] * inv], axis=-1).astype(f)
        cos, sin = np.ones((lead + rot, TOK), f), np.zeros((lead + rot, TOK), f)
        cos[lead:, :LAT] = np.tile(np.cos(ang).T, (2, 1))
        sin[lead:, :LAT] = np.tile(np.sin(ang).T, (2, 1))
        return cos, sin

    ca, sa = tables(64, 0)
    cb, sb_ = tables(32, 64)
    rope = np.zeros((P, 4, TOK), f)
    rope[:, 0], rope[:, 1] = np.tile(ca, (2, 1)), np.tile(sa, (2, 1))
    rope[0:96, 2], rope[0:96, 3] = cb, sb_
    swap = np.zeros((P, 2, P), f)
    for base in (0, 64):
        for d in range(32):
            swap[base + 32 + d, 0, base + d] = -1.0
            swap[base + d, 0, base + 32 + d] = 1.0
    for d in range(16):
        swap[80 + d, 1, 64 + d] = -1.0
        swap[64 + d, 1, 80 + d] = 1.0
    pair = np.zeros((P, P), f)
    pair[:64, :64] = pair[64:, 64:] = 1.0
    s = np.arange(P)
    same = np.stack([(s[:, None] // (2 * h) == s[None] // (2 * h)) for h in LEVELS] + [s[:, None] == s[None]], 1)
    return {"k_ident": np.eye(P, dtype=f), "k_ones": np.ones((P, P), f), "k_pair": pair, "k_swap": swap,
            "k_rope": rope, "k_same": same.astype(f)}


NAMES = ['x', 'c', 'ctx', 'c_ctx', 'w_ada', 'b_ada', 'g_pre_mix', 'g_post_mix', 'g_pre_ffn', 'g_post_ffn', 'w_in',
         'a_q_norm', 'a_k_norm', 'b_q_norm', 'w_q_up', 'b_kv_norm', 'w_kv_up', 'c_lower_bounds', 'c_out_norm',
         'w_out', 'w_ff1', 'w_ff2']


def program(nc, args, out, stop=None):
    e = Env()
    (e.x, e.c, e.ctx, e.c_ctx, e.w_ada, e.b_ada, e.g_pre_mix, e.g_post_mix, e.g_pre_ffn, e.g_post_ffn, e.w_in,
     e.a_q_norm, e.a_k_norm, e.b_q_norm, e.w_q_up, e.b_kv_norm, e.w_kv_up, e.c_lb, e.c_out_norm, e.w_out,
     e.w_ff1, e.w_ff2) = [args[n] for n in NAMES]
    e.k_ident, e.k_ones, e.k_pair = args["k_ident"], args["k_ones"], args["k_pair"]
    e.k_swap, e.k_rope, e.k_same = args["k_swap"], args["k_rope"], args["k_same"]
    e.out = out
    with ExitStack() as st:
        names, live = set(), [ExitStack(), []]

        def sem(n):
            k, base = 2, n
            while n in names:
                n, k = f"{base}_{k}", k + 1
            names.add(n)
            s = live[0].enter_context(nc.semaphore(n))
            live[1].append(s)
            return s

        def recycle():
            with nc.Block() as block:
                @block.sync
                def _(sp):
                    for s in live[1]:
                        sp.sem_clear(s)
            live[0].close()
            live[:] = [ExitStack(), []]

        e.recycle = recycle
        e.s_final = st.enter_context(nc.semaphore("output_stored"))

        sb = lambda n, s, d=F32: st.enter_context(nc.sbuf_tensor(n, s, d))
        e.ident, e.ones, e.pair = sb("ident", [P, P]), sb("ones", [P, P]), sb("pair", [P, P])
        e.swap, e.same = sb("swap", [P, 2, P]), sb("same", [P, 8, P], U8)
        e.consts = [(e.ident[:, :], e.k_ident), (e.ones[:, :], e.k_ones), (e.pair[:, :], e.k_pair),
                    (e.swap[:, :, :], e.k_swap)]
        e.sv = sb("sv", [P, DEPTH, R_N])
        e.mod = sb("mod", [P, DEPTH, 48, 2])
        e.lb = sb("lb", [P, DEPTH, 2, 4])
        e.x_dram = nc.dram_tensor("x_scratch", [P, KT, TOK], F32, kind="Internal").ap()
        e.hh = sb("hh", [P, 2, KT, TOK], F16)
        build(nc, e, sem, stop)


def kernel(**inputs):
    import concourse.bacc as bacc
    from concourse.bass_utils import run_bass_kernel_spmd

    nc = bacc.Bacc("TRN2", target_bir_lowering=False, num_devices=1)
    arrays, args = {}, {}
    for name, a in {**{n: np.ascontiguousarray(inputs[n]) for n in NAMES}, **shape_constants()}.items():
        arrays["in_" + name] = a
        args[name] = nc.dram_tensor("in_" + name, a.shape, mybir.dt.from_np(a.dtype), kind="ExternalInput").ap()
    out = nc.dram_tensor("out_0_dram", (1, LAT, D), F32, kind="ExternalOutput").ap()
    program(nc, args, out)
    r = run_bass_kernel_spmd(nc, [arrays], core_ids=[0])
    return r.results[0]["out_0_dram"]
```

```python
from contextlib import ExitStack

import numpy as np

import concourse.bass as bass
from concourse import mybir

F32 = mybir.dt.float32
F16 = mybir.dt.float16
BF16 = mybir.dt.bfloat16
U8 = mybir.dt.uint8
ALU = mybir.AluOpType
ACT = mybir.ActivationFunctionType
AX = mybir.AxisListType

P = 128
D = 1024
KT = D // P
LAT, CTX = 1024, 256
TOK = LAT + CTX
TT = TOK // P
DEPTH = 2
EPS = 1e-6
F_TINY = 1e-30
WSCALE = 256.0
ASCALE = 0.25
FF = 4 * D
GROUP = 8
BLK = 128
LEVELS = [64, 32, 16, 8, 4, 2, 1]
R_BADA, R_GPM, R_GQM, R_GPF, R_GQF, R_C, R_CC, R_LB, R_BKV, R_BQ, R_AQ, R_AK, R_CO, R_N = (
    0, 48, 56, 64, 72, 80, 88, 96, 104, 105, 107, 108, 109, 110)
C_AQ, C_AK, C_AV, C_BQ, C_BKV, C_BKR, C_CQ, C_CFF, C_CFB, C_CI, C_CG = (
    0, 512, 640, 768, 960, 1088, 1120, 1376, 1632, 1888, 2144)


def chunks(n):
    return [(a, min(512, n - a)) for a in range(0, n, 512)]


class Chain:

    def __init__(self, sem):
        self.sem, self.n = sem, 0

    def __call__(self, ins):
        self.n += 1
        ins.then_inc(self.sem, 1)
        return self.n

    def wait(self, eng, n=None):
        eng.wait_ge(self.sem, self.n if n is None else n)


class Env:
    pass


class Ada:

    def __init__(self, nc, e, sem, st, nm, l, first, last, ring):
        self.nc, self.e, self.l, self.first, self.last, self.ring = nc, e, l, first, last, ring
        self.w = st.enter_context(nc.sbuf_tensor(nm + "wada", [P, ring, KT, 512], F32))
        self.acc = st.enter_context(nc.psum_tensor(nm + "ada", [P, 48, 2], F32))
        self.s_load = [sem(f"{nm}wada_loaded{i}") for i in range(ring)]
        self.s_used = sem(nm + "wada_used")
        self.n = last - first

    def load(self, eng, j):
        if j >= self.ring:
            eng.wait_ge(self.s_used, j - self.ring + 1)
        c = (self.first + j) * 512
        src = self.e.w_ada[self.l, :, c:c + 512].rearrange("(k p) n -> p k n", p=P)
        eng.dma_start(self.w[:, j % self.ring, :, :], src).then_inc(self.s_load[j % self.ring], 16)

    def product(self, pe, j):
        pe.wait_ge(self.s_load[j % self.ring], 16 * (j // self.ring + 1))
        for m in range(4):
            for k in range(KT):
                last = self.nc.tensor.matmul(self.acc[:, 4 * (self.first + j) + m, :],
                                             self.w[:, j % self.ring, k, m * P:(m + 1) * P], self.e.cact[:, k, :],
                                             start=(k == 0), stop=(k == KT - 1))
        last.then_inc(self.s_used, 1)

    def finish(self, dve, ch):
        nc, e, l, lo, hi = self.nc, self.e, self.l, 4 * self.first, 4 * self.last
        dve.wait_ge(self.s_used, self.n)
        m = e.mod[:, l, :, :]
        for n in range(2):
            ch(nc.vector.tensor_tensor(m[:, lo:hi, n], self.acc[:, lo:hi, n], e.sv[:, l, R_BADA + lo:R_BADA + hi],
                                       ALU.add))
        ch.wait(dve)
        for n in range(2):
            for at, g in ((8, R_GPM), (32, R_GPF)):
                if lo <= at < hi:
                    ch(nc.vector.scalar_tensor_tensor(m[:, at:at + 8, n], m[:, at:at + 8, n], 1.0,
                                                      e.sv[:, l, g:g + 8], ALU.add, ALU.mult))
            for at, g in ((16, R_GQM), (40, R_GQF)):
                if lo <= at < hi:
                    ch(nc.vector.tensor_tensor(m[:, at:at + 8, n], m[:, at:at + 8, n], e.sv[:, l, g:g + 8], ALU.mult))
        ch.wait(dve)
        for at in (8, 16, 32, 40):
            if lo <= at < hi:
                ch(nc.vector.tensor_scalar(m[:, at:at + 8, :], m[:, at:at + 8, :], -0.5, None, ALU.mult))


def setup_phase(nc, e, sem, xt):
    with ExitStack() as st:
        sb = lambda n, s, d=F32: st.enter_context(nc.sbuf_tensor(n, s, d))
        ps = lambda n, s, d=F32: st.enter_context(nc.psum_tensor(n, s, d))
        xin = sb("xin", [P, 4, D])
        rows = sb("rows", [P, DEPTH, P])
        cs = sb("cs", [P, 2 * KT])
        ce = sb("ce", [P, 2 * KT])
        A = Ada(nc, e, sem, st, "set_", 0, 0, 4, 4)
        lbw = sb("lbw", [P, 6, 4])
        samef = sb("samef", [P, 8, P])
        tp = [ps(f"tp{i}", [P, 4, P]) for i in range(2)]
        tv = ps("tv", [P, DEPTH, P])
        s_const, s_rows = sem("const_loaded"), sem("rows_loaded")
        s_zero = sem("rows_zeroed")
        s_xin = [sem(f"xin_loaded{i}") for i in range(4)]
        s_tp, s_xt, s_tv, s_sv = sem("x_transposed"), sem("x_evacuated"), sem("rows_transposed"), sem("vectors_ready")
        s_e, s_silu, s_dch = sem("exp_c"), sem("silu_c"), sem("setup_dve")
        s_lbd = sem("bounds_shifted")
        e.consts.append((samef[:, :, :], e.k_same))
        ncon = len(e.consts)
        with nc.Block() as block:
            @block.sync
            def _(sp):
                for dst, src in e.consts:
                    sp.dma_start(dst, src).then_inc(s_const, 16)
                sp.wait_ge(s_zero, 1)
                for l in range(DEPTH):
                    r = rows[:, l, :]
                    for at, n, src in ((R_BADA, 48, e.b_ada[l]), (R_GPM, 8, e.g_pre_mix[l]), (R_GQM, 8, e.g_post_mix[l]),
                                       (R_GPF, 8, e.g_pre_ffn[l]), (R_GQF, 8, e.g_post_ffn[l]),
                                       (R_C, 8, e.c[0]), (R_CC, 8, e.c_ctx),
                                       (R_LB, 8, e.c_lb.rearrange("a b c -> (a b c)")), (R_BKV, 1, e.b_kv_norm[l]),
                                       (R_BQ, 1, e.b_q_norm[l, 0:P])):
                        sp.dma_start(r[at:at + n, :], src.rearrange("(a b) -> a b", b=P)).then_inc(s_rows, 16)
                    sp.dma_start(r[R_BQ + 1:R_BQ + 2, 0:64],
                                 e.b_q_norm[l, P:192].rearrange("(a b) -> a b", a=1)).then_inc(s_rows, 16)
                    for at, src in ((R_AQ, e.a_q_norm[l]), (R_AK, e.a_k_norm[l]), (R_CO, e.c_out_norm[l])):
                        for half in range(2):
                            sp.dma_start(r[at:at + 1, 64 * half:64 * half + 64],
                                         src.rearrange("(a b) -> a b", a=1)).then_inc(s_rows, 16)
                for t in range(TT):
                    if t >= 4:
                        sp.wait_ge(s_tp, 2 * (t - 3))
                    src = e.x[0, t * P:(t + 1) * P, :] if t < LAT // P else e.ctx[0, t * P - LAT:(t + 1) * P - LAT, :]
                    sp.dma_start(xin[:, t % 4, :], src).then_inc(s_xin[t % 4], 16)

            @block.scalar
            def _(act):
                for j in range(A.n):
                    A.load(act, j)
                act.wait_ge(s_sv, 1)
                nc.scalar.activation(ce[:, :], cs[:, :], ACT.Exp, scale=-1.0).then_inc(s_e, 1)
                act.wait_ge(s_lbd, 2)
                nc.scalar.activation(lbw[:, 2, :], lbw[:, 0, :], ACT.Exp).then_inc(s_e, 1)
                nc.scalar.activation(lbw[:, 3, :], lbw[:, 1, :], ACT.Exp).then_inc(s_e, 1)

            @block.vector
            def _(dve):
                ch = Chain(s_dch)
                nc.vector.memset(rows[:, :, :], 0.0).then_inc(s_zero, 1)
                dve.wait_ge(s_const, 16 * ncon)
                ch(nc.vector.tensor_copy(e.same[:, :, :], samef[:, :, :]))
                dve.wait_ge(s_tv, 1)
                ch(nc.vector.tensor_copy(e.sv[:, :, :], tv[:, :, 0:R_N]))
                ch.wait(dve)
                nc.vector.tensor_copy(cs[:, :], e.sv[:, 0, R_C:R_C + 16]).then_inc(s_sv, 1)
                dve.wait_ge(s_e, 1)
                ch(nc.vector.tensor_scalar_add(ce[:, :], ce[:, :], 1.0))
                ch.wait(dve)
                ch(nc.vector.reciprocal(ce[:, :], ce[:, :]))
                ch.wait(dve)
                nc.vector.tensor_tensor(e.cact[:, :, :].rearrange("p k n -> p n k"),
                                        cs[:, :].rearrange("p (n k) -> p n k", k=KT),
                                        ce[:, :].rearrange("p (n k) -> p n k", k=KT), ALU.mult).then_inc(s_silu, 1)
                a0, a1 = e.sv[:, 0, R_LB:R_LB + 4], e.sv[:, 0, R_LB + 4:R_LB + 8]
                ch(nc.vector.tensor_tensor(lbw[:, 4, :], a0, a1, ALU.max))
                ch.wait(dve)
                nc.vector.tensor_tensor(lbw[:, 0, :], a0, lbw[:, 4, :], ALU.subtract).then_inc(s_lbd, 1)
                nc.vector.tensor_tensor(lbw[:, 1, :], a1, lbw[:, 4, :], ALU.subtract).then_inc(s_lbd, 1)
                dve.wait_ge(s_e, 3)
                ch(nc.vector.tensor_tensor(lbw[:, 4, :], lbw[:, 2, :], lbw[:, 3, :], ALU.add))
                ch.wait(dve)
                ch(nc.vector.reciprocal(lbw[:, 5, :], lbw[:, 4, :]))
                ch.wait(dve)
                ch(nc.vector.tensor_tensor(lbw[:, 2, :], lbw[:, 2, :], lbw[:, 5, :], ALU.mult))
                ch(nc.vector.tensor_tensor(lbw[:, 3, :], lbw[:, 3, :], lbw[:, 5, :], ALU.mult))
                ch.wait(dve)
                ch(nc.vector.tensor_tensor(lbw[:, 3, :], lbw[:, 2, :], lbw[:, 3, :], ALU.add))
                ch(nc.vector.tensor_tensor(e.lb[:, 0, 0, :], lbw[:, 2, :], lbw[:, 2, :], ALU.subtract))
                ch.wait(dve)
                ch(nc.vector.tensor_tensor(e.lb[:, 1, 0, :], lbw[:, 3, :], lbw[:, 2, :], ALU.subtract))
                ch.wait(dve)
                ch(nc.vector.tensor_scalar(e.lb[:, :, 1, :], e.lb[:, :, 0, :], -1.0, 1.0, ALU.mult, ALU.add))
                for i in range(2 * TT):
                    t, half = i // 2, i % 2
                    dve.wait_ge(s_tp, i + 1)
                    nc.vector.tensor_copy(xt[:, 4 * half:4 * half + 4, t * P:(t + 1) * P], tp[i % 2][:, :, :])\
                      .then_inc(s_xt, 1)
                A.finish(dve, ch)
                for l in range(DEPTH):
                    ch(nc.vector.tensor_scalar(e.sv[:, l, R_BKV:R_N], e.sv[:, l, R_BKV:R_N], -0.5, None, ALU.mult))

            @block.tensor
            def _(pe):
                pe.wait_ge(s_const, 16 * ncon)
                pe.wait_ge(s_rows, 16 * 17 * DEPTH)
                for l in range(DEPTH):
                    last = nc.tensor.transpose(tv[:, l, :], rows[:, l, :], e.ident[:, :])
                last.then_inc(s_tv, 1)
                for i in range(2 * TT):
                    t, half = i // 2, i % 2
                    if half == 0:
                        pe.wait_ge(s_xin[t % 4], 16 * (t // 4 + 1))
                    if i >= 2:
                        pe.wait_ge(s_xt, i - 1)
                    for k in range(4):
                        last = nc.tensor.transpose(tp[i % 2][:, k, :],
                                                   xin[:, t % 4, (4 * half + k) * P:(4 * half + k + 1) * P],
                                                   e.ident[:, :])
                    last.then_inc(s_tp, 1)
                pe.wait_ge(s_silu, 1)
                for j in range(A.n):
                    A.product(pe, j)


def newton(nc, dve, ch, m, r, t):
    ch(nc.vector.tensor_tensor(t, m, r, ALU.mult))
    ch.wait(dve)
    ch(nc.vector.tensor_tensor(t, t, r, ALU.mult))
    ch.wait(dve)
    ch(nc.vector.scalar_tensor_tensor(r, t, 3.0, r, ALU.subtract, ALU.mult))
    ch.wait(dve)


class Linear:

    RING = 4

    def __init__(self, nc, e, sem, st, nm):
        self.nc = nc
        sb = lambda n, s, d=F32: st.enter_context(nc.sbuf_tensor(nm + n, s, d))
        self.stage = sb("stage", [P, self.RING, KT * P])
        self.w = sb("w", [P, self.RING, 2, KT * P], F16)
        self.ps = [st.enter_context(nc.psum_tensor(f"{nm}acc{i}", [P, 3 * 512], F32)) for i in range(2)]
        self.s_load = [sem(f"{nm}w_loaded{i}") for i in range(self.RING)]
        self.s_hi, self.s_lo, self.s_used = sem(nm + "w_hi"), sem(nm + "w_lo"), sem(nm + "w_used")

    def load(self, eng, n, parts):
        r = n % self.RING
        if n >= self.RING:
            eng.wait_ge(self.s_lo, n - self.RING + 1)
        for k, row, at, src in parts:
            dst = self.stage[:, r, 0:k * row].rearrange("p (k n) -> p k n", k=k)[:, :, at:at + src.shape[2]]
            eng.dma_start(dst, src).then_inc(self.s_load[r], 16)

    def high(self, act, n, loads, size=KT * P, used=None):
        r = n % self.RING
        act.wait_ge(self.s_load[r], 16 * loads)
        if n >= self.RING:
            act.wait_ge(*(used or (self.s_used, n - self.RING + 1)))
        self.nc.scalar.activation(self.w[:, r, 0, 0:size], self.stage[:, r, 0:size], ACT.Copy, scale=WSCALE)\
            .then_inc(self.s_hi, 1)

    def low(self, dve, n, size=KT * P):
        r = n % self.RING
        dve.wait_ge(self.s_hi, n + 1)
        self.nc.vector.scalar_tensor_tensor(self.w[:, r, 1, 0:size], self.stage[:, r, 0:size], WSCALE,
                                            self.w[:, r, 0, 0:size], ALU.mult, ALU.subtract).then_inc(self.s_lo, 1)

    def product(self, n, acc, src, k0, kn, m0, mw, row, ntok, col=0):
        r = n % self.RING
        w = self.w[:, r, :, 0:kn * row].rearrange("p h (k n) -> p h k n", k=kn)
        for k in range(kn):
            for wh, sh in ((0, 0), (0, 1), (1, 0)):
                for a, c in chunks(ntok):
                    last = self.nc.tensor.matmul(acc[0:mw, a:a + c], w[:, wh, k, m0:m0 + mw],
                                                 src[:, sh, k0 + k, a:a + c],
                                                 start=(k == 0 and wh == 0 and sh == 0),
                                                 stop=(k == kn - 1 and wh == 1))
        return last

    def product_t(self, n, acc, src, row, mw, tts):
        r = n % self.RING
        w = self.w[:, r, :, 0:KT * row].rearrange("p h (k n) -> p h k n", k=KT)
        for t in range(tts):
            for k in range(KT):
                for sh, wh in ((0, 0), (0, 1), (1, 0)):
                    last = self.nc.tensor.matmul(acc[:, t * P:t * P + mw], src[:, sh, k, t * P:(t + 1) * P],
                                                 w[:, wh, k, 0:mw], start=(k == 0 and wh == 0 and sh == 0),
                                                 stop=(k == KT - 1 and sh == 1))
        return last


def input_projection(nc, e, sem, l, f):
    nq = TOK if l < DEPTH - 1 else LAT
    w = e.w_in[l].rearrange("(k p) n -> p k n", p=P)
    tiles = []
    for i in range(2):
        tiles.append(([(0, C_CFF + i * P, P)], P, TOK, f.z[:, 2 + i, :]))
        tiles.append(([(0, C_CFB + i * P, P)], P, TOK, f.z[:, i, :]))
    for i in range(2):
        tiles.append(([(0, C_CI + i * P, P)], P, None, f.cv[:, :, i * P:(i + 1) * P]))
    for i in range(2):
        tiles.append(([(0, C_CQ + i * P, P)], P, nq, f.cq[:, i, :]))
        tiles.append(([(0, C_CG + i * P, P)], P, nq, f.cg[:, i, :]))
    tiles.append(([(0, C_AK, P)], P, TOK, f.ak[:, :]))
    tiles.append(([(0, C_AV, P)], P, None, None))
    for i in range(4):
        tiles.append(([(0, C_AQ + i * P, P)], P, nq, f.aq[:, i, :]))
    tiles.append(([(0, C_BKV, P)], P, TOK, f.bkv[:, :]))
    tiles.append(([(0, C_BQ, P)], P, nq, f.bq[:, 0, :]))
    tiles.append(([(0, C_BQ + P, 64), (64, C_BKR, 32)], 96, TOK, f.bq[0:96, 1, :]))
    N = len(tiles)
    with ExitStack() as st:
        nm = f"in{l}_"
        L = Linear(nc, e, sem, st, nm)
        s_ev, s_av = sem(nm + "evacuated"), sem(nm + "av_hi")
        avf = st.enter_context(nc.sbuf_tensor(nm + "avf", [P, TT * P], F32))
        av4 = avf[:, :].rearrange("p (t h n) -> p t h n", h=2, n=64)
        counts, seen = [], [0] * L.RING
        for n, t in enumerate(tiles):
            seen[n % L.RING] += len(t[0])
            counts.append(seen[n % L.RING])
        with nc.Block() as block:
            @block.sync
            def _(sp):
                for n, (cols, row, _, _) in enumerate(tiles):
                    L.load(sp, n, [(KT, row, at, w[:, :, c0:c0 + cn]) for at, c0, cn in cols])

            @block.scalar
            def _(act):
                for n in range(-2, N):
                    if n + 2 < N:
                        L.high(act, n + 2, counts[n + 2], KT * tiles[n + 2][1])
                    if n < 0:
                        continue
                    _, row, ntok, dst = tiles[n]
                    act.wait_ge(L.s_used, n + 1)
                    if dst is None:
                        nc.scalar.activation(avf[:, :], L.ps[n % 2][:, 0:TOK], ACT.Copy, scale=1.0 / WSCALE)\
                          .then_inc(s_ev, 1)
                        act.wait_ge(s_ev, n + 1)
                        for h in range(2):
                            last = nc.scalar.activation(f.av[:, :, h, 0:64], av4[:, :, h, :], ACT.Copy)
                        last.then_inc(s_av, 1)
                    elif ntok is None:
                        nc.scalar.activation(dst, L.ps[n % 2][:, 0:TOK].rearrange("p (t n) -> p t n", n=P), ACT.Copy,
                                             scale=1.0 / WSCALE).then_inc(s_ev, 1)
                    else:
                        nc.scalar.activation(dst[:, 0:ntok], L.ps[n % 2][0:row, 0:ntok], ACT.Copy, scale=1.0 / WSCALE)\
                          .then_inc(s_ev, 1)

            @block.vector
            def _(dve):
                for n in range(N):
                    L.low(dve, n, KT * tiles[n][1])
                dve.wait_ge(s_av, 1)
                for h in range(2):
                    nc.vector.tensor_tensor(f.av[:, :, h, 64:P], av4[:, :, h, :], f.av[:, :, h, 0:64], ALU.subtract)

            @block.tensor
            def _(pe):
                for n, (cols, row, ntok, dst) in enumerate(tiles):
                    pe.wait_ge(L.s_lo, n + 1)
                    if n >= 2:
                        pe.wait_ge(s_ev, n - 1)
                    if ntok is None:
                        L.product_t(n, L.ps[n % 2], e.hh, row, P, TT).then_inc(L.s_used, 1)
                    else:
                        L.product(n, L.ps[n % 2], e.hh, 0, KT, 0, row, row, ntok).then_inc(L.s_used, 1)


def output_projection(nc, e, sem, l, x, y, ntok):
    w = e.w_out[l].rearrange("(k p) n -> p k n", p=P)
    with ExitStack() as st:
        nm = f"out{l}_"
        L = Linear(nc, e, sem, st, nm)
        s_ev, s_x = sem(nm + "evacuated"), sem(nm + "x_loaded")
        with nc.Block() as block:
            @block.sync
            def _(sp):
                for n in range(KT):
                    L.load(sp, n, [(KT, P, 0, w[:, :, n * P:(n + 1) * P])])
                sp.dma_start(x[:, :, 0:ntok], e.x_dram[:, :, 0:ntok]).then_inc(s_x, 16)
                sp.wait_ge(s_x, 16)

            @block.scalar
            def _(act):
                for n in range(-2, KT):
                    if n + 2 < KT:
                        L.high(act, n + 2, (n + 2) // 4 + 1)
                    if n >= 0:
                        act.wait_ge(L.s_used, n + 1)
                        nc.scalar.activation(y[:, n, 0:ntok], L.ps[n % 2][:, 0:ntok], ACT.Copy, scale=1.0 / WSCALE)\
                          .then_inc(s_ev, 1)

            @block.vector
            def _(dve):
                for n in range(KT):
                    L.low(dve, n)

            @block.tensor
            def _(pe):
                for n in range(KT):
                    pe.wait_ge(L.s_lo, n + 1)
                    if n >= 2:
                        pe.wait_ge(s_ev, n - 1)
                    L.product(n, L.ps[n % 2], e.hh, 0, KT, 0, P, P, ntok).then_inc(L.s_used, 1)


MG = 4
NG = FF // P // MG


def mlp(nc, e, sem, l, y, ntok):
    w1 = e.w_ff1[l].rearrange("(k p) n -> p k n", p=P)
    w2 = e.w_ff2[l].rearrange("(g k p) n -> g p k n", p=P, k=MG)
    slots = []
    for g in range(NG + 1):
        if g < NG:
            slots += [("up", g, j) for j in range(MG)]
        if g:
            slots += [("down", g - 1, j) for j in range(KT // 2)]
    N = len(slots)
    with ExitStack() as st:
        nm = f"mlp{l}_"
        L = Linear(nc, e, sem, st, nm)
        sb = lambda n, s, d=F32: st.enter_context(nc.sbuf_tensor(nm + n, s, d))
        aa = sb("aa", [P, 2, 2, MG, TOK], F16)
        r = sb("r", [P, TOK])
        s_ev, s_relu, s_sq, s_ahi, s_alo, s_out = (sem(nm + x) for x in (
            "y_added", "relu", "squared", "a_hi", "a_lo", "outputs_done"))
        outs = []
        for n, (kind, g, j) in enumerate(slots):
            outs += [(n, kind, g, j, 0)] if kind == "up" else [(n, kind, g, 2 * j + m, m) for m in range(2)]
        M = len(outs)
        done = {o[0]: i + 1 for i, o in enumerate(outs)}
        ups = [sum(o[1] == "up" for o in outs[:i]) for i in range(M + 1)]

        def free(eng, i):
            if i >= 2:
                if outs[i - 2][1] == "up":
                    eng.wait_ge(s_relu, ups[i - 1])
                else:
                    eng.wait_ge(s_ev, i - 1 - ups[i - 1])

        with nc.Block() as block:
            @block.sync
            def _(sp):
                for n, (kind, g, j) in enumerate(slots):
                    if kind == "up":
                        L.load(sp, n, [(KT, P, 0, w1[:, :, (MG * g + j) * P:(MG * g + j + 1) * P])])
                    else:
                        L.load(sp, n, [(MG, 2 * P, 0, w2[g, :, :, 2 * j * P:2 * (j + 1) * P])])

            @block.scalar
            def _(act):
                u = 0
                L.high(act, 0, 1)
                L.high(act, 1, 1)
                for i, (n, kind, g, j, m) in enumerate(outs):
                    if m == 0 and n + 2 < N:
                        L.high(act, n + 2, (n + 2) // 4 + 1, used=(s_out, done[n - 2]) if n >= 2 else None)
                    if kind == "down":
                        continue
                    act.wait_ge(s_out, i + 1)
                    if u >= 1:
                        act.wait_ge(s_alo, u)
                    nc.scalar.activation(r[:, 0:ntok], L.ps[i % 2][:, 0:ntok], ACT.Relu,
                                         scale=ASCALE ** 0.5 / WSCALE).then_inc(s_relu, 1)
                    act.wait_ge(s_sq, u + 1)
                    if g >= 2:
                        act.wait_ge(s_out, max(q for q, o in enumerate(outs) if o[1] == "down" and o[2] == g - 2) + 1)
                    nc.scalar.activation(aa[:, g % 2, 0, j, 0:ntok], r[:, 0:ntok], ACT.Copy).then_inc(s_ahi, 1)
                    u += 1

            @block.vector
            def _(dve):
                u = v = 0
                L.low(dve, 0)
                L.low(dve, 1)
                for i, (n, kind, g, j, m) in enumerate(outs):
                    if m == 0 and n + 2 < N:
                        L.low(dve, n + 2)
                    if kind == "up":
                        dve.wait_ge(s_relu, u + 1)
                        nc.vector.tensor_tensor(r[:, 0:ntok], r[:, 0:ntok], r[:, 0:ntok], ALU.mult).then_inc(s_sq, 1)
                        dve.wait_ge(s_ahi, u + 1)
                        nc.vector.tensor_tensor(aa[:, g % 2, 1, j, 0:ntok], r[:, 0:ntok], aa[:, g % 2, 0, j, 0:ntok],
                                                ALU.subtract).then_inc(s_alo, 1)
                        u += 1
                    else:
                        dve.wait_ge(s_out, i + 1)
                        if g == 0:
                            nc.vector.tensor_scalar(y[:, j, 0:ntok], L.ps[i % 2][:, 0:ntok],
                                                    1.0 / (WSCALE * ASCALE), None, ALU.mult).then_inc(s_ev, 1)
                        else:
                            if j == 0:
                                dve.wait_ge(s_ev, KT * g)
                            nc.vector.scalar_tensor_tensor(y[:, j, 0:ntok], L.ps[i % 2][:, 0:ntok],
                                                           1.0 / (WSCALE * ASCALE), y[:, j, 0:ntok], ALU.mult, ALU.add)\
                              .then_inc(s_ev, 1)
                        v += 1

            @block.tensor
            def _(pe):
                for i, (n, kind, g, j, m) in enumerate(outs):
                    if m == 0:
                        pe.wait_ge(L.s_lo, n + 1)
                    free(pe, i)
                    if kind == "up":
                        L.product(n, L.ps[i % 2], e.hh, 0, KT, 0, P, P, ntok).then_inc(s_out, 1)
                    else:
                        if j == 0:
                            pe.wait_ge(s_alo, MG * (g + 1))
                        L.product(n, L.ps[i % 2], aa[:, g % 2], 0, MG, m * P, P, 2 * P, ntok).then_inc(s_out, 1)


def between(nc, e, sem, x, ntok, nm, l=0, y=None, gate=0, mod=None, store=False, final=False):
    cks = chunks(ntok)
    order = [w for w in ("Sy0", "My0", "Sy1", "Ny0", "My1", "U0", "Sx0", "Ny1", "Sy2", "My2", "U1", "Mx0", "Sx1",
                         "Nx0", "H0", "Ny2", "U2", "Mx1", "Sx2", "Nx1", "H1", "Mx2", "Nx2", "H2")
             if int(w[-1]) < len(cks) and (y is not None or "y" not in w and w[0] != "U")
             and (mod is not None or "x" not in w and w[0] != "H")]
    S = [w[1:] for w in order if w[0] == "S"]
    M = [w[1:] for w in order if w[0] == "M"]
    with ExitStack() as st:
        sb = lambda n, s, d=F32: st.enter_context(nc.sbuf_tensor(nm + n, s, d))
        sq = sb("sq", [P, 4, 512])
        mean, rs, t1 = sb("mean", [P, len(S), 512]), sb("rs", [P, len(S), 512]), sb("t1", [P, 512])
        ys, h = sb("ys", [P, 4, 512]), sb("h", [P, 4, 512])
        xo = sb("xo", [P, 2, D]) if final else None
        ss = [st.enter_context(nc.psum_tensor(f"{nm}ss{i}", [P, 512], F32)) for i in range(len(S))]
        tp = [st.enter_context(nc.psum_tensor(f"{nm}tp{i}", [P, 4, P], F32)) for i in range(2)] if final else None
        s_sq, s_sum, s_m, s_r, s_d, s_ys, s_xn, s_t, s_h, s_hi, s_lo, s_tp, s_te = (sem(nm + n) for n in (
            "squared", "summed", "mean", "rsqrt", "dve", "y_scaled", "x_updated", "x_scaled", "h_ready", "hi", "lo",
            "transposed", "evacuated"))
        s_st = e.s_final if final else sem(nm + "stored")
        with nc.Block() as block:
            @block.sync
            def _(sp):
                if store:
                    for c, (a, n) in enumerate(cks):
                        if y is not None:
                            sp.wait_ge(s_xn, KT * (c + 1))
                        sp.dma_start(e.x_dram[:, :, a:a + n], x[:, :, a:a + n]).then_inc(s_st, 16)
                    sp.wait_ge(s_st, 16 * len(cks))
                if final:
                    for t in range(ntok // P):
                        sp.wait_ge(s_te, 2 * (t + 1))
                        sp.dma_start(e.out[0, t * P:(t + 1) * P, :], xo[:, t % 2, :]).then_inc(s_st, 16)
                        sp.wait_ge(s_st, 16 * (t + 1))

            @block.scalar
            def _(act):
                i = 0
                for w in order:
                    c = int(w[-1])
                    a, n = cks[c]
                    if w[0] == "S":
                        for k in range(KT):
                            if i >= 4:
                                act.wait_ge(s_sum, i - 3)
                            if w[1] == "x" and y is not None:
                                act.wait_ge(s_xn, KT * c + k + 1)
                            src = x if w[1] == "x" else y
                            nc.scalar.activation(sq[:, i % 4, 0:n], src[:, k, a:a + n], ACT.Square).then_inc(s_sq, 1)
                            i += 1
                    elif w[0] == "M":
                        j, p = M.index(w[1:]), S.index(w[1:])
                        act.wait_ge(s_m, j + 1)
                        nc.scalar.activation(rs[:, p, 0:n], mean[:, p, 0:n], ACT.Ln).then_inc(s_r, 1)
                        act.wait_ge(s_r, 2 * j + 1)
                        nc.scalar.activation(rs[:, p, 0:n], rs[:, p, 0:n], ACT.Exp, scale=-0.5).then_inc(s_r, 1)
                    elif w[0] == "H":
                        for k in range(KT):
                            act.wait_ge(s_h, KT * c + k + 1)
                            nc.scalar.activation(e.hh[:, 0, k, a:a + n], h[:, k % 4, 0:n], ACT.Copy).then_inc(s_hi, 1)

            @block.tensor
            def _(pe):
                i = 0
                for p, w in enumerate(S):
                    n = cks[int(w[-1])][1]
                    for k in range(KT):
                        pe.wait_ge(s_sq, i + 1)
                        nc.tensor.matmul(ss[p][:, 0:n], e.ones[:, :], sq[:, i % 4, 0:n],
                                         start=(k == 0), stop=(k == KT - 1)).then_inc(s_sum, 1)
                        i += 1
                if final:
                    for i in range(2 * ntok // P):
                        t, half = i // 2, i % 2
                        pe.wait_ge(s_xn, KT * (t * P // 512 + 1))
                        if i >= 2:
                            pe.wait_ge(s_te, i - 1)
                        for k in range(4):
                            last = nc.tensor.transpose(tp[i % 2][:, k, :], x[:, 4 * half + k, t * P:(t + 1) * P],
                                                       e.ident[:, :])
                        last.then_inc(s_tp, 1)

            @block.vector
            def _(dve):
                ch = Chain(s_d)
                for w in order:
                    c = int(w[-1])
                    a, n = cks[c]
                    who = int(a >= LAT)
                    if w[0] == "M":
                        p = S.index(w[1:])
                        dve.wait_ge(s_sum, KT * (p + 1))
                        nc.vector.tensor_scalar(mean[:, p, 0:n], ss[p][:, 0:n], 1.0 / D, EPS, ALU.mult, ALU.add)\
                          .then_inc(s_m, 1)
                    elif w[0] == "N":
                        p = S.index(w[1:])
                        dve.wait_ge(s_r, 2 * M.index(w[1:]) + 2)
                        newton(nc, dve, ch, mean[:, p, 0:n], rs[:, p, 0:n], t1[:, 0:n])
                    elif w[0] == "U":
                        p = S.index("y" + w[-1])
                        for k in range(KT + 1):
                            if k < KT:
                                if KT * c + k >= 4:
                                    dve.wait_ge(s_xn, KT * c + k - 3)
                                nc.vector.tensor_tensor(ys[:, k % 4, 0:n], y[:, k, a:a + n], rs[:, p, 0:n],
                                                        ALU.mult).then_inc(s_ys, 1)
                            if k:
                                dve.wait_ge(s_ys, KT * c + k)
                                nc.vector.scalar_tensor_tensor(x[:, k - 1, a:a + n], ys[:, (k - 1) % 4, 0:n],
                                                               e.mod[:, l, gate + k - 1, who:who + 1],
                                                               x[:, k - 1, a:a + n], ALU.mult, ALU.add)\
                                  .then_inc(s_xn, 1)
                    elif w[0] == "H":
                        sc, sh, lm = mod
                        p = S.index("x" + w[-1])
                        if y is not None:
                            dve.wait_ge(s_xn, KT * (c + 1))
                        for k in range(KT + 2):
                            if k < KT:
                                if KT * c + k >= 4:
                                    dve.wait_ge(s_lo, KT * c + k - 3)
                                nc.vector.tensor_tensor(h[:, k % 4, 0:n], x[:, k, a:a + n], rs[:, p, 0:n],
                                                        ALU.mult).then_inc(s_t, 1)
                            if 1 <= k <= KT:
                                j = k - 1
                                dve.wait_ge(s_t, KT * c + k)
                                nc.vector.tensor_scalar(h[:, j % 4, 0:n], h[:, j % 4, 0:n],
                                                        e.mod[:, lm, sc + j, who:who + 1],
                                                        e.mod[:, lm, sh + j, who:who + 1], ALU.mult, ALU.add)\
                                  .then_inc(s_h, 1)
                            if k >= 2:
                                j = k - 2
                                dve.wait_ge(s_hi, KT * c + j + 1)
                                nc.vector.tensor_tensor(e.hh[:, 1, j, a:a + n], h[:, j % 4, 0:n],
                                                        e.hh[:, 0, j, a:a + n], ALU.subtract).then_inc(s_lo, 1)
                if final:
                    for i in range(2 * ntok // P):
                        t, half = i // 2, i % 2
                        dve.wait_ge(s_tp, i + 1)
                        if t >= 2:
                            dve.wait_ge(s_st, 16 * (t - 1))
                        nc.vector.tensor_copy(xo[:, t % 2, 512 * half:512 * half + 512],
                                              tp[i % 2][:, :, :].rearrange("p a b -> p (a b)")).then_inc(s_te, 1)




def mixers(nc, e, sem, l, stop):
    f = Env()
    with ExitStack() as st:
        sb = lambda n, s, d=F32, st=st, side="left": st.enter_context(nc.sbuf_tensor(f"{n}{l}", s, d, side=side))
        f.aq, f.ak = sb("aq", [P, 4, TOK]), sb("ak", [P, TOK])
        f.av = sb("av", [P, TT, 2, P], F16)
        with ExitStack() as low:
            f.bq, f.bkv = sb("bq", [P, 2, TOK], st=low, side="right"), sb("bkv", [P, TOK], st=low, side="right")
            with ExitStack() as st2:
                f.z = sb("z", [P, 4, TOK], st=st2)
                f.cq, f.cg = sb("cq", [P, 2, TOK], st=st2), sb("cg", [P, 2, TOK], st=st2)
                f.cv = sb("cv", [P, TT, 2 * P], st=st2)
                input_projection(nc, e, sem, l, f)
                if stop == f"mix{l}in":
                    return
                if stop != f"mix{l}at":
                    recurrence(nc, e, sem, l, f, stop)
                if stop in [f"mix{l}" + x for x in ("rec", "g", "s", "o")]:
                    return
            prepare_norms(nc, e, sem, l, f)
            if stop == f"mix{l}pa":
                return
            f.qb, f.kb = sb("qb", [97, 2, 4, TOK], F16), sb("kb", [97, 2, 4, TOK], F16)
            f.bv = sb("bv", [P, TT, 4, P], F16)
            prepare_latent(nc, e, sem, l, f)
            if stop == f"mix{l}pb":
                return
        attention(nc, e, sem, l, f)


MSHIFT = 8.3178


def halves(t, a, n):
    v = t.bitcast(F16)
    return v[:, 2 * a:2 * a + n], v[:, 2 * a + n:2 * a + 2 * n]


def prepare_norms(nc, e, sem, l, f):
    nq = TOK if l < DEPTH - 1 else LAT
    nm = f"pa{l}_"
    items = []
    for a, n in chunks(TOK):
        items.append(("rope", [f.ak[:, :]], [R_AK], e.pair, 64, 1.0, a, n))
        items.append(("flat", [f.bkv[:, :]], [R_BKV], e.ones, 128, 1.0, a, n))
        if a < nq:
            items += [("rope", [f.aq[:, t, :]], [R_AQ], e.pair, 64, 0.125, a, n) for t in range(4)]
            items.append(("flat", [f.bq[:, 0, :], f.bq[0:64, 1, :]], [R_BQ, R_BQ + 1], e.ones, 192, 1.0, a, n))
    N = len(items)
    with ExitStack() as st:
        sb = lambda n, s, d=F32: st.enter_context(nc.sbuf_tensor(nm + n, s, d))
        rope = sb("rope", [P, 2, TOK])
        sq = sb("sq", [P, 2, 2, 512])
        xg = sb("xg", [P, 2, 2, 512])
        m, r = sb("m", [P, 2, 512]), sb("r", [P, 2, 512])
        t1 = sb("t1", [P, 512])
        u = sb("u", [P, 2, 2, 512])
        pss = [st.enter_context(nc.psum_tensor(f"{nm}ss{i}", [P, 512], F32)) for i in range(2)]
        prot = [st.enter_context(nc.psum_tensor(f"{nm}rot{i}", [P, 512], F32)) for i in range(2)]
        s_rope, s_xg, s_pp, s_m, s_r, s_uc, s_u, s_hi, s_lo, s_d = (sem(nm + x) for x in (
            "rope_loaded", "gained", "products", "mean", "rsqrt", "cos_done", "u_ready", "hi", "lo", "dve"))
        ada = Ada(nc, e, sem, st, nm, l + 1, 0, 4, 4) if l + 1 < DEPTH else None
        with nc.Block() as block:
            @block.sync
            def _(sp):
                sp.dma_start(rope[:, :, :], e.k_rope[:, 0:2, :]).then_inc(s_rope, 16)
                for j in range(ada.n if ada else 0):
                    ada.load(sp, j)
                sp.wait_ge(s_rope, 16)

            @block.scalar
            def _(act):
                def first(i):
                    _, xs, gs, _, _, _, a, n = items[i]
                    if i >= 2:
                        act.wait_ge(s_pp, i - 1)
                        act.wait_ge(s_u, i - 1)
                    for j, (x, g) in enumerate(zip(xs, gs)):
                        R = x.shape[0]
                        nc.scalar.activation(sq[0:R, i % 2, j, 0:n], x[:, a:a + n], ACT.Square)
                        last = nc.scalar.activation(xg[0:R, i % 2, j, 0:n], x[:, a:a + n], ACT.Copy,
                                                    scale=e.sv[0:R, l, g:g + 1])
                    last.then_inc(s_xg, 1)

                def second(i):
                    n = items[i][7]
                    act.wait_ge(s_m, i + 1)
                    nc.scalar.activation(r[:, i % 2, 0:n], m[:, i % 2, 0:n], ACT.Ln).then_inc(s_r, 1)
                    act.wait_ge(s_r, 2 * i + 1)
                    nc.scalar.activation(r[:, i % 2, 0:n], r[:, i % 2, 0:n], ACT.Exp, scale=-0.5).then_inc(s_r, 1)

                def third(i):
                    _, xs, _, _, _, _, a, n = items[i]
                    act.wait_ge(s_u, i + 1)
                    for j, x in enumerate(xs):
                        last = nc.scalar.activation(halves(x, a, n)[0], u[0:x.shape[0], i % 2, j, 0:n], ACT.Copy)
                    last.then_inc(s_hi, 1)

                first(0)
                for i in range(N):
                    if i + 1 < N:
                        first(i + 1)
                    second(i)
                    if i:
                        third(i - 1)
                third(N - 1)

            @block.tensor
            def _(pe):
                for i, (kind, xs, _, ones, _, _, a, n) in enumerate(items):
                    pe.wait_ge(s_xg, i + 1)
                    if i >= 2:
                        pe.wait_ge(s_u, i - 1)
                    for j, x in enumerate(xs):
                        R = x.shape[0]
                        last = nc.tensor.matmul(pss[i % 2][:, 0:n], ones[0:R, :], sq[0:R, i % 2, j, 0:n],
                                                start=(j == 0), stop=(j == len(xs) - 1))
                    if kind == "rope":
                        last = nc.tensor.matmul(prot[i % 2][:, 0:n], e.swap[:, 0, :], xg[:, i % 2, 0, 0:n],
                                                start=True, stop=True)
                    last.then_inc(s_pp, 1)
                    if ada and i >= 6 and i % 2 == 0 and (i - 6) // 2 < ada.n:
                        ada.product(pe, (i - 6) // 2)

            @block.gpsimd
            def _(pool):
                pool.wait_ge(s_rope, 16)
                for i, (kind, _, _, _, _, _, a, n) in enumerate(items):
                    pool.wait_ge(s_xg, i + 1)
                    if i >= 2:
                        pool.wait_ge(s_lo, i - 1)
                    if kind == "rope":
                        nc.gpsimd.tensor_tensor(u[:, i % 2, 0, 0:n], xg[:, i % 2, 0, 0:n], rope[:, 0, a:a + n],
                                                ALU.mult).then_inc(s_uc, 1)

            @block.vector
            def _(dve):
                ch = Chain(s_d)

                def mean(i):
                    _, _, _, _, F, _, _, n = items[i]
                    dve.wait_ge(s_pp, i + 1)
                    nc.vector.tensor_scalar(m[:, i % 2, 0:n], pss[i % 2][:, 0:n], 1.0 / F, EPS, ALU.mult, ALU.add)\
                      .then_inc(s_m, 1)

                def low(i):
                    _, xs, _, _, _, _, a, n = items[i]
                    dve.wait_ge(s_hi, i + 1)
                    for j, x in enumerate(xs):
                        hi, lo = halves(x, a, n)
                        last = nc.vector.tensor_tensor(lo, u[0:x.shape[0], i % 2, j, 0:n], hi, ALU.subtract)
                    last.then_inc(s_lo, 1)

                dve.wait_ge(s_rope, 16)
                mean(0)
                ropes = 0
                for i, (kind, xs, _, _, _, fac, a, n) in enumerate(items):
                    if i + 1 < N:
                        mean(i + 1)
                    p = i % 2
                    dve.wait_ge(s_r, 2 * i + 2)
                    ch(nc.vector.tensor_tensor(t1[:, 0:n], m[:, p, 0:n], r[:, p, 0:n], ALU.mult))
                    ch.wait(dve)
                    ch(nc.vector.tensor_tensor(t1[:, 0:n], t1[:, 0:n], r[:, p, 0:n], ALU.mult))
                    ch.wait(dve)
                    ch(nc.vector.scalar_tensor_tensor(r[:, p, 0:n], t1[:, 0:n], 3.0, r[:, p, 0:n],
                                                      ALU.subtract, ALU.mult))
                    ch.wait(dve)
                    if kind == "rope":
                        ropes += 1
                        ch(nc.vector.tensor_tensor(t1[:, 0:n], prot[p][:, 0:n], rope[:, 1, a:a + n], ALU.mult))
                        ch.wait(dve)
                        dve.wait_ge(s_uc, ropes)
                        ch(nc.vector.tensor_tensor(u[:, p, 0, 0:n], u[:, p, 0, 0:n], t1[:, 0:n], ALU.add))
                        ch.wait(dve)
                        nc.vector.scalar_tensor_tensor(u[:, p, 0, 0:n], u[:, p, 0, 0:n], fac, r[:, p, 0:n],
                                                       ALU.mult, ALU.mult).then_inc(s_u, 1)
                    else:
                        if i >= 2:
                            dve.wait_ge(s_lo, i - 1)
                        for j, x in enumerate(xs):
                            R = x.shape[0]
                            last = nc.vector.tensor_tensor(u[0:R, p, j, 0:n], xg[0:R, p, j, 0:n], r[0:R, p, 0:n],
                                                           ALU.mult)
                        last.then_inc(s_u, 1)
                    if i:
                        low(i - 1)
                low(N - 1)
                dve.wait_ge(s_lo, N)
                if ada:
                    ada.finish(dve, ch)


def prepare_latent(nc, e, sem, l, f):
    nq = TOK if l < DEPTH - 1 else LAT
    nm = f"pb{l}_"
    SC = 96.0 ** -0.5
    items = []
    for a, n in chunks(TOK):
        items.append(("kpe", 0, a, n))
        items += [("bk", h, a, n) for h in range(4)]
        if a < nq:
            items += [("bq", h, a, n) for h in range(4)]
    items += [("bv", t, 0, 256) for t in range(TT)]
    N = len(items)
    with ExitStack() as st:
        sb = lambda n, s, d=F32: st.enter_context(nc.sbuf_tensor(nm + n, s, d))
        rope = sb("rope", [P, 2, TOK])
        up = sb("up", [P, 3, 512])
        uw = sb("uw", [P, 2, 3, 512], F16)
        xg, u, t1 = sb("xg", [P, 2, 512]), sb("u", [P, 2, 512]), sb("t1", [P, 512])
        pup = [st.enter_context(nc.psum_tensor(f"{nm}up{i}", [P, 512], F32)) for i in range(2)]
        prot = [st.enter_context(nc.psum_tensor(f"{nm}rot{i}", [P, 512], F32)) for i in range(2)]
        s_rope, s_upl, s_uh, s_ul, s_one, s_p1, s_xg, s_p2, s_u, s_hi, s_lo, s_d = (sem(nm + x) for x in (
            "rope_loaded", "up_loaded", "up_hi", "up_lo", "ones_set", "up_done", "evacuated", "rotated", "u_ready",
            "hi", "lo", "dve"))
        bhi = lambda a, n: halves(f.bkv[:, :], a, n)
        rots = [sum(x[0] in ("kpe", "bq") for x in items[:i]) for i in range(N + 1)]
        ups = [sum(x[0] != "kpe" for x in items[:i]) for i in range(N + 1)]
        rows = {"kpe": (64, 96), "bq": (0, 96)}
        with nc.Block() as block:
            @block.sync
            def _(sp):
                sp.dma_start(rope[:, :, :], e.k_rope[:, 2:4, :]).then_inc(s_rope, 16)
                sp.dma_start(up[:, 0, 0:384], e.w_q_up[l, 0:P, :]).then_inc(s_upl, 16)
                sp.dma_start(up[0:64, 1, 0:384], e.w_q_up[l, P:192, :]).then_inc(s_upl, 16)
                sp.dma_start(up[:, 2, :], e.w_kv_up[l]).then_inc(s_upl, 16)

            @block.gpsimd
            def _(pool):
                nc.gpsimd.memset(f.kb[96:97, 0, :, :], 1.0).then_inc(s_one, 1)

            parts = ((P, 0, 384), (64, 1, 384), (P, 2, 512))

            @block.scalar
            def _(act):
                act.wait_ge(s_upl, 48)
                for R, j, n in parts:
                    nc.scalar.activation(uw[0:R, 0, j, 0:n], up[0:R, j, 0:n], ACT.Copy, scale=WSCALE).then_inc(s_uh, 1)

                def high(i):
                    kind, h, a, n = items[i]
                    if kind == "bk":
                        act.wait_ge(s_p1, ups[i] + 1)
                        nc.scalar.activation(f.kb[0:64, 0, h, a:a + n], pup[i % 2][0:64, 0:n], ACT.Copy,
                                             scale=1.0 / WSCALE).then_inc(s_hi, 1)
                    elif kind == "bv":
                        act.wait_ge(s_p1, ups[i] + 1)
                        nc.scalar.activation(f.bv[:, h, :, 0:64], pup[i % 2][:, 0:256].rearrange("p (h n) -> p h n", h=4),
                                             ACT.Copy, scale=1.0 / WSCALE).then_inc(s_hi, 1)
                    else:
                        lo, hi_ = rows[kind]
                        act.wait_ge(s_u, rots[i] + 1)
                        if kind == "kpe":
                            nc.scalar.activation(f.kb[lo:hi_, 0, :, a:a + n],
                                                 u[lo:hi_, i % 2, 0:n].unsqueeze(1).broadcast_to([32, 4, n]),
                                                 ACT.Copy).then_inc(s_hi, 1)
                        else:
                            nc.scalar.activation(f.qb[lo:hi_, 0, h, a:a + n], u[lo:hi_, i % 2, 0:n], ACT.Copy)\
                              .then_inc(s_hi, 1)

                for i in range(N + 1):
                    if i < N and items[i][0] in rows:
                        kind, h, a, n = items[i]
                        if i >= 2:
                            act.wait_ge(s_lo, i - 1)
                        if kind == "kpe":
                            nc.scalar.activation(xg[64:96, i % 2, 0:n], f.bq[64:96, 1, a:a + n], ACT.Copy)\
                              .then_inc(s_xg, 1)
                        else:
                            act.wait_ge(s_p1, ups[i] + 1)
                            nc.scalar.activation(xg[0:96, i % 2, 0:n], pup[i % 2][0:96, 0:n], ACT.Copy,
                                                 scale=SC / WSCALE).then_inc(s_xg, 1)
                    if i:
                        high(i - 1)

            @block.tensor
            def _(pe):
                pe.wait_ge(s_ul, 3)

                def rotate(i):
                    kind, h, a, n = items[i]
                    if kind in rows:
                        lo, hi_ = rows[kind]
                        pe.wait_ge(s_xg, rots[i] + 1)
                        nc.tensor.matmul(prot[i % 2][lo:hi_, 0:n], e.swap[lo:hi_, 1, lo:hi_], xg[lo:hi_, i % 2, 0:n],
                                         start=True, stop=True).then_inc(s_p2, 1)

                for i, (kind, h, a, n) in enumerate(items):
                    if i >= 2:
                        pe.wait_ge(s_lo, i - 1)
                    out = pup[i % 2]
                    passes = ((0, 0), (0, 1), (1, 0))
                    if kind == "bv":
                        ca = h * P // 512 * 512
                        cn = min(512, TOK - ca)
                        v = [x[:, h * P - ca:h * P - ca + P] for x in bhi(ca, cn)]
                        w = uw[:, :, 2, :].rearrange("p s (h n) -> p s h n", h=4)
                        for q, (xh, wh) in enumerate(passes):
                            last = nc.tensor.matmul(out[:, 0:256].rearrange("p (h n) -> p h n", h=4), v[xh],
                                                    w[:, wh, :, 64:128], start=(q == 0), stop=(q == 2))
                        last.then_inc(s_p1, 1)
                    elif kind == "bk":
                        v = bhi(a, n)
                        for q, (xh, wh) in enumerate(passes):
                            last = nc.tensor.matmul(out[0:64, 0:n], uw[:, wh, 2, h * P:h * P + 64], v[xh],
                                                    start=(q == 0), stop=(q == 2))
                        last.then_inc(s_p1, 1)
                    elif kind == "bq":
                        for j, R in ((0, P), (1, 64)):
                            v = halves(f.bq[0:R, j, :], a, n)
                            for q, (xh, wh) in enumerate(passes):
                                last = nc.tensor.matmul(out[0:96, 0:n], uw[0:R, wh, j, h * 96:(h + 1) * 96], v[xh],
                                                        start=(j == 0 and q == 0), stop=(j == 1 and q == 2))
                        last.then_inc(s_p1, 1)
                    else:
                        pass
                    if i:
                        rotate(i - 1)
                rotate(N - 1)

            @block.vector
            def _(dve):
                ch = Chain(s_d)
                dve.wait_ge(s_rope, 16)
                for q, (R, j, n) in enumerate(parts):
                    dve.wait_ge(s_uh, q + 1)
                    nc.vector.scalar_tensor_tensor(uw[0:R, 1, j, 0:n], up[0:R, j, 0:n], WSCALE, uw[0:R, 0, j, 0:n],
                                                   ALU.mult, ALU.subtract).then_inc(s_ul, 1)

                def low(i):
                    kind, h, a, n = items[i]
                    dve.wait_ge(s_hi, i + 1)
                    if kind == "bk":
                        last = nc.vector.scalar_tensor_tensor(f.kb[0:64, 1, h, a:a + n], pup[i % 2][0:64, 0:n],
                                                              1.0 / WSCALE, f.kb[0:64, 0, h, a:a + n],
                                                              ALU.mult, ALU.subtract)
                    elif kind == "bv":
                        last = nc.vector.scalar_tensor_tensor(f.bv[:, h, :, 64:128],
                                                              pup[i % 2][:, 0:256].rearrange("p (h n) -> p h n", h=4),
                                                              1.0 / WSCALE, f.bv[:, h, :, 0:64], ALU.mult, ALU.subtract)
                    elif kind == "kpe":
                        last = nc.vector.tensor_tensor(f.kb[64:96, 1, :, a:a + n],
                                                       u[64:96, i % 2, 0:n].unsqueeze(1).broadcast_to([32, 4, n]),
                                                       f.kb[64:96, 0, :, a:a + n], ALU.subtract)
                    else:
                        last = nc.vector.tensor_tensor(f.qb[0:96, 1, h, a:a + n], u[0:96, i % 2, 0:n],
                                                       f.qb[0:96, 0, h, a:a + n], ALU.subtract)
                    last.then_inc(s_lo, 1)

                for i, (kind, h, a, n) in enumerate(items):
                    if kind in rows:
                        lo, hi_ = rows[kind]
                        dve.wait_ge(s_xg, rots[i] + 1)
                        ch(nc.vector.tensor_tensor(u[lo:hi_, i % 2, 0:n], xg[lo:hi_, i % 2, 0:n],
                                                   rope[lo:hi_, 0, a:a + n], ALU.mult))
                    if i:
                        low(i - 1)
                    if kind in rows:
                        dve.wait_ge(s_p2, rots[i] + 1)
                        ch(nc.vector.tensor_tensor(t1[lo:hi_, 0:n], prot[i % 2][lo:hi_, 0:n],
                                                   rope[lo:hi_, 1, a:a + n], ALU.mult))
                        ch.wait(dve)
                        nc.vector.tensor_tensor(u[lo:hi_, i % 2, 0:n], u[lo:hi_, i % 2, 0:n], t1[lo:hi_, 0:n], ALU.add)\
                          .then_inc(s_u, 1)
                        dve.wait_ge(s_u, rots[i] + 1)
                low(N - 1)


LEAD = 2
EARLY = 2


def attention(nc, e, sem, l, f):
    nm = f"at{l}_"
    units = []
    for h in range(12):
        units.append((h, 0, LAT, list(range(TT))))
        if l < DEPTH - 1:
            units.append((h, LAT, CTX, [TT - 2, TT - 1]))
    U = len(units)
    key0 = lambda u: units[u][3][0] * P
    keyn = lambda u: len(units[u][3]) * P
    tasks, at = [], {}

    def put(u, s, t):
        at.setdefault((u, s), []).append(len(tasks))
        tasks.append(t)

    maxes = {u: [("max", u, q, c) for q in range(units[u][2] // P) for c in range(len(chunks(keyn(u))))]
             for u in range(U)}
    halfs = lambda u: range(len(chunks(units[u][2])))
    for t in maxes[0]:
        put(-1, 0, t)
    for c in halfs(0):
        put(-1, 0, ("row", 0, c))
    short = lambda u: u < U and units[u][2] < LAT
    for u in range(U):
        if short(u):
            continue
        nk = len(units[u][3])
        nxt = [v for v in range(u + 1, min(U, u + 3)) if v == u + 1 or short(u + 1)]
        ahead = [t for v in nxt for t in maxes[v]]
        for s in range(nk - LEAD):
            for _ in range(2 if s < 3 else -(-len(ahead) // (nk - LEAD - s))):
                if ahead:
                    put(u, s, ahead.pop(0))
        for v in nxt:
            for c in halfs(v):
                put(u, nk - LEAD + 1, ("row", v, c))
        for j, v in enumerate([v for v in (u - 2, u - 1) if v >= 0 and (v == u - 1 or short(u - 1))]):
            put(u, 1 + j, ("sum", v))
            for c in halfs(v):
                put(u, 2 + j, ("cast", v, c))
    for j, v in enumerate([v for v in (U - 2, U - 1) if v == U - 1 or short(U - 1)]):
        put(U, 1, ("sum", v))
        for c in halfs(v):
            put(U, 1, ("cast", v, c))
    order = sorted(at, key=lambda w: (w[0], w[1]))
    for w in order:
        at[w].sort(key=lambda j: tasks[j][0] != "max")
    tasks_ = [tasks[j] for w in order for j in at[w]]
    n0 = 0
    for w in order:
        at[w] = list(range(n0, n0 + len(at[w])))
        n0 += len(at[w])
    tasks = tasks_
    NT = len(tasks)
    kinds = [t[0] for t in tasks]
    nth = lambda kind, i: kinds[:i + 1].count(kind)
    steps = [(u, s) for u in range(U) for s in range(len(units[u][3]))]
    base = {u: sum(len(units[v][3]) for v in range(u)) for u in range(U + 1)}
    with ExitStack() as st:
        sb = lambda n, s, d=F32: st.enter_context(nc.sbuf_tensor(nm + n, s, d))
        ps = lambda n, s, d=F32: st.enter_context(nc.psum_tensor(nm + n, s, d))
        qq, qs = sb("qq", [P, 3, TOK], F16), sb("qs", [65, 3, TOK], F16)
        kk, ks = sb("kk", [P, 2, TOK], F16), sb("ks", [65, 2, TOK], F16)
        p32, phi, plo = sb("p32", [P, 3, LAT]), sb("phi", [P, 3, LAT], F16), sb("plo", [P, 3, LAT], F16)
        acc = sb("acc", [P, 2, LAT])
        mx, neg = sb("mx", [P, 2, 8, 3]), sb("neg", [P, 2, 8])
        vlo, ov = sb("vlo", [64, LAT]), sb("ov", [64, 2, LAT])
        rc, o32 = sb("rc", [P, 8]), sb("o32", [P, LAT])
        sT = [ps(f"sT{i}", [P, LAT]) for i in range(2)]
        pv = ps("pv", [P, LAT])
        small = [ps(f"small{i}", [P, 512]) for i in range(2)]
        s_load = [sem(f"{nm}queries_loaded{i}") for i in range(3)]
        s_kload = [sem(f"{nm}keys_loaded{i}") for i in range(2)]
        (s_ones, s_task, s_max, s_neg, s_row, s_rec, s_S, s_e32, s_e16, s_lo, s_acc, s_pv, s_vlo, s_ov, s_o, s_d,
         s_mn, s_cp) = (sem(nm + x) for x in (
            "ones_set", "small_done", "max_read", "shift_ready", "row_written", "sum_read", "scores_done", "exp32",
            "exp16", "p_lo", "p_summed", "pv_done", "vlo_out", "pv_read", "o_written", "dve", "max_merged", "first_kept"))

        def released(eng, i):
            eng.wait_ge({"max": s_max, "row": s_row, "sum": s_rec, "cast": s_o}[kinds[i]], nth(kinds[i], i))

        def ops(u):
            h = units[u][0]
            if h < 8:
                p, kv = h % 3, h // 4
                return ([(kk[:, kv, :], qq[:, p, :]), (ks[:, kv, :], qs[:, p, :])], kk[0:64, kv, :], qs[0:64, p, :],
                        qs[64:65, p, :])
            b = h - 8
            return ([(f.kb[0:97, 0, b, :], f.qb[0:97, 0, b, :]), (f.kb[0:96, 0, b, :], f.qb[0:96, 1, b, :]),
                     (f.kb[0:96, 1, b, :], f.qb[0:96, 0, b, :])], f.kb[0:96, 0, b, :], f.qb[0:96, 0, b, :],
                    f.qb[96:97, 0, b, :])

        values = lambda u, kt: f.av[:, kt, units[u][0] // 4, :] if units[u][0] < 8 else f.bv[:, kt, units[u][0] - 8, :]
        nq = TOK if l < DEPTH - 1 else LAT
        first_unit = {}
        for u in range(U):
            first_unit.setdefault(units[u][0], u)

        with nc.Block() as block:
            @block.sync
            def _(sp):
                def spread(t, n):
                    v, full = t.bitcast(F16), n // 512 * 512
                    whole = v[:, 0:2 * full].rearrange("p (c s n) -> p c s n", s=2, n=512)
                    parts = [(0, full, whole[:, :, 0, :], whole[:, :, 1, :])]
                    return parts + ([(full, n - full, *halves(t, full, n - full))] if n > full else [])

                def place(dst, a, n, src, signal):
                    to = dst[:, a:a + n]
                    if n > 512:
                        to = to.rearrange("p (c n) -> p c n", n=512)
                    sp.dma_start(to, src).then_inc(signal, 16)

                for h in range(8):
                    p, rows, kv = h % 3, slice(64 * (h % 2), 64 * (h % 2) + 64), h // 4
                    if h in (0, 2):
                        kv = h // 2
                        for a, n, khi, klo in spread(f.ak[64 * kv:64 * kv + 64, :], TOK):
                            place(kk[0:64, kv, :], a, n, khi, s_kload[kv])
                            place(kk[64:P, kv, :], a, n, khi, s_kload[kv])
                            place(ks[0:64, kv, :], a, n, klo, s_kload[kv])
                    if h >= 3:
                        sp.wait_ge(s_S, base[first_unit[h - 2]])
                    for a, n, qhi, qlo in spread(f.aq[rows, h // 2, :], nq):
                        place(qq[0:64, p, :], a, n, qhi, s_load[p])
                        place(qq[64:P, p, :], a, n, qlo, s_load[p])
                        place(qs[0:64, p, :], a, n, qhi, s_load[p])

            per_head = 16 * 3 * (1 if nq == LAT else 2)

            @block.gpsimd
            def _(pool):
                nc.gpsimd.memset(ks[64:65, :, :], 1.0).then_inc(s_ones, 1)
                for i, (u, s) in enumerate(steps):
                    n = units[u][2]
                    if s == 0:
                        continue
                    pool.wait_ge(s_e32, i + 1)
                    if s == 1:
                        if u >= 2:
                            pool.wait_ge(s_task, max(j for j, t in enumerate(tasks) if t[:2] == ("sum", u - 2)) + 1)
                        nc.gpsimd.tensor_tensor(acc[:, u % 2, 0:n], p32[:, (i - 1) % 3, 0:n], p32[:, i % 3, 0:n],
                                                ALU.add).then_inc(s_acc, 1)
                    else:
                        pool.wait_ge(s_acc, i - u - 1)
                        nc.gpsimd.tensor_tensor(acc[:, u % 2, 0:n], acc[:, u % 2, 0:n], p32[:, i % 3, 0:n],
                                                ALU.add).then_inc(s_acc, 1)

            def summed(i):
                u, s = steps[i]
                return i - u if s else i - u + 1

            @block.scalar
            def _(act):
                def small_tasks(where):
                    for j in at.get(where, []):
                        kind, u = tasks[j][:2]
                        if kind == "row":
                            a, n = chunks(units[u][2])[tasks[j][2]]
                            q0 = units[u][1]
                            act.wait_ge(s_task, j + 1)
                            row = ops(u)[3]
                            R = 64 if units[u][0] < 8 else 96
                            nc.scalar.activation(row[:, q0 + a:q0 + a + n], small[j % 2][R:R + 1, 0:n], ACT.Copy)\
                              .then_inc(s_row, 1)

                def read_pv(u):
                    n = units[u][2]
                    act.wait_ge(s_pv, base[u + 1])
                    if u:
                        act.wait_ge(s_ov, u)
                    nc.scalar.activation(vlo[:, 0:n], pv[64:P, 0:n], ACT.Copy).then_inc(s_vlo, 1)

                small_tasks((-1, 0))
                for i, (u, s) in enumerate(steps):
                    n = units[u][2]
                    act.wait_ge(s_S, i + 1)
                    if i >= 3:
                        act.wait_ge(s_lo, i - 2)
                        act.wait_ge(s_acc, summed(i - 3))
                    nc.scalar.activation(p32[:, i % 3, 0:n], sT[i % 2][:, 0:n], ACT.Exp).then_inc(s_e32, 1)
                    if i >= 3:
                        act.wait_ge(s_pv, i - 2)
                    nc.scalar.activation(phi[:, i % 3, 0:n], sT[i % 2][:, 0:n], ACT.Exp).then_inc(s_e16, 1)
                    if s == 1 and u:
                        read_pv(u - 1)
                    small_tasks((u, s))
                read_pv(U - 1)

            @block.vector
            def _(dve):
                ch = Chain(s_d)

                def small_tasks(where, which=("max", "sum", "cast")):
                    for j in at.get(where, []):
                        kind, u = tasks[j][:2]
                        if kind not in which:
                            continue
                        if kind == "max":
                            _, _, q, c = tasks[j]
                            n = chunks(keyn(u))[c][1]
                            dve.wait_ge(s_task, j + 1)
                            nc.vector.reduce_max(mx[:, u % 2, q, c:c + 1], small[j % 2][:, 0:n], AX.X).then_inc(s_max, 1)
                            if tasks[j] == maxes[u][-1]:
                                nqt, nc_ = units[u][2] // P, len(chunks(keyn(u)))
                                dve.wait_ge(s_max, nth("max", j))
                                ch(nc.vector.reduce_max(neg[:, u % 2, 0:nqt], mx[:, u % 2, 0:nqt, 0:nc_], AX.X))
                                ch.wait(dve)
                                nc.vector.tensor_scalar(neg[:, u % 2, 0:nqt], neg[:, u % 2, 0:nqt], -1.0, MSHIFT,
                                                        ALU.mult, ALU.add).then_inc(s_neg, 1)
                        elif kind == "sum":
                            dve.wait_ge(s_task, j + 1)
                            nqt = units[u][2] // P
                            nc.vector.reciprocal(rc[:, 0:nqt], small[j % 2][:, 0:nqt]).then_inc(s_rec, 1)
                        elif kind == "cast":
                            a, n = chunks(units[u][2])[tasks[j][2]]
                            R = 64 * (units[u][0] % 2)
                            dve.wait_ge(s_task, j + 1)
                            if ch.n:
                                ch.wait(dve)
                            nc.vector.tensor_tensor(o32[R:R + 64, a:a + n], ov[:, u % 2, a:a + n],
                                                    small[j % 2][0:64, 0:n], ALU.mult).then_inc(s_o, 1)
                            if a + n == units[u][2]:
                                dve.wait_ge(s_o, nth("cast", j))
                                finish(u)

                def finish(u):
                    h, q0, n, _ = units[u]
                    R = 64 * (h % 2)
                    hi, lo = (e.hh[R:R + 64, s, h // 2, q0:q0 + n] for s in range(2))
                    ch(nc.vector.tensor_copy(hi, o32[R:R + 64, 0:n]))
                    ch.wait(dve)
                    ch(nc.vector.tensor_tensor(lo, o32[R:R + 64, 0:n], hi, ALU.subtract))

                def read_pv(u):
                    n = units[u][2]
                    dve.wait_ge(s_vlo, u + 1)
                    nc.vector.tensor_tensor(ov[:, u % 2, 0:n], pv[0:64, 0:n], vlo[:, 0:n], ALU.add).then_inc(s_ov, 1)
                    dve.wait_ge(s_ov, u + 1)

                small_tasks((-1, 0))
                for i, (u, s) in enumerate(steps):
                    n = units[u][2]
                    small_tasks((u, s), ("max",))
                    dve.wait_ge(s_e16, i + 1)
                    if i >= 3:
                        dve.wait_ge(s_pv, i - 2)
                    nc.vector.tensor_tensor(plo[:, i % 3, 0:n], p32[:, i % 3, 0:n], phi[:, i % 3, 0:n], ALU.subtract)\
                      .then_inc(s_lo, 1)
                    if s == 1 and u:
                        read_pv(u - 1)
                    small_tasks((u, s), ("sum", "cast"))
                read_pv(U - 1)
                small_tasks((U, 1))

            @block.tensor
            def _(pe):
                loaded = set()

                def small_tasks(where, part=slice(None)):
                    for j in at.get(where, [])[part]:
                        kind, u = tasks[j][:2]
                        h, q0, n, kts = units[u]
                        if kind == "max" and h < 8 and h not in loaded:
                            if h % 4 == 0:
                                pe.wait_ge(s_kload[h // 4], 16 * 6)
                            pe.wait_ge(s_load[h % 3], per_head * (h // 3 + 1))
                            loaded.add(h)
                        if j >= 2:
                            released(pe, j - 2)
                        out = small[j % 2]
                        if kind == "max":
                            _, _, q, c = tasks[j]
                            a, w = chunks(keyn(u))[c]
                            _, k, qh, _ = ops(u)
                            last = nc.tensor.matmul(out[:, 0:w], qh[:, q0 + q * P:q0 + (q + 1) * P],
                                                    k[:, key0(u) + a:key0(u) + a + w], start=True, stop=True)
                        elif kind == "row":
                            a, w = chunks(n)[tasks[j][2]]
                            R = 64 if h < 8 else 96
                            pe.wait_ge(s_neg, u + 1)
                            for q in range(w // P):
                                last = nc.tensor.matmul(out[R:R + 1, q * P:(q + 1) * P],
                                                        neg[:, u % 2, a // P + q:a // P + q + 1], e.ident[:, :],
                                                        start=True, stop=True)
                        elif kind == "sum":
                            pe.wait_ge(s_acc, base[u + 1] - u - 1)
                            for q in range(n // P):
                                last = nc.tensor.matmul(out[:, q:q + 1], acc[:, u % 2, q * P:(q + 1) * P],
                                                        e.ones[:, 0:1], start=True, stop=True)
                        else:
                            a, w = chunks(n)[tasks[j][2]]
                            pe.wait_ge(s_rec, u + 1)
                            for q in range(w // P):
                                last = nc.tensor.matmul(out[0:64, q * P:(q + 1) * P],
                                                        rc[:, a // P + q:a // P + q + 1].broadcast_to([P, 64]),
                                                        e.ident[:, :], start=True, stop=True)
                        last.then_inc(s_task, 1)

                def weighted(i):
                    u, s = steps[i]
                    n, kts = units[u][2:]
                    pe.wait_ge(s_lo, i + 1)
                    if s == 0 and u:
                        pe.wait_ge(s_ov, u)
                    v = values(u, kts[s])
                    for a, w in chunks(n):
                        nc.tensor.matmul(pv[:, a:a + w], v, phi[:, i % 3, a:a + w], start=(s == 0), stop=False,
                                         skip_group_check=True)
                        last = nc.tensor.matmul(pv[0:64, a:a + w], v[:, 0:64], plo[:, i % 3, a:a + w],
                                                start=False, stop=(s == len(kts) - 1), skip_group_check=True)
                    last.then_inc(s_pv, 1)

                pe.wait_ge(s_ones, 1)
                small_tasks((-1, 0))
                rows = len(chunks(units[0][2]))
                for i, (u, s) in enumerate(steps):
                    h, q0, n, kts = units[u]
                    if s == 0:
                        done = max(j for j, t in enumerate(tasks) if t[:2] == ("row", u))
                        pe.wait_ge(s_row, nth("row", done))
                    if i >= 2:
                        pe.wait_ge(s_e16, i - 1)
                    pairs = ops(u)[0]
                    K = slice(kts[s] * P, (kts[s] + 1) * P)
                    for a, w in chunks(n):
                        for j, (k, q) in enumerate(pairs):
                            last = nc.tensor.matmul(sT[i % 2][:, a:a + w], k[:, K], q[:, q0 + a:q0 + a + w],
                                                    start=(j == 0), stop=(j == len(pairs) - 1))
                    last.then_inc(s_S, 1)
                    early = sum(tasks[j][0] == "max" for j in at.get((u, s), [])[0:EARLY])
                    small_tasks((u, s), slice(0, early))
                    if i >= 2:
                        weighted(i - 2)
                    small_tasks((u, s), slice(early, None))
                weighted(len(steps) - 2)
                weighted(len(steps) - 1)
                small_tasks((U, 1))


ORDER = {"f": [8, 9, 0, 1, 2, 3, 4, 5, 6, 7], "b": [9, 8, 7, 6, 5, 4, 3, 2, 1, 0]}


def gates(nc, e, sem, l, f):
    nm = f"ga{l}_"
    nq = TOK if l < DEPTH - 1 else LAT
    items = [("z", n, TOK) for n in range(4)] + [("q", i, nq) for i in range(2)] + [("g", i, nq) for i in range(2)]
    with ExitStack() as st:
        t = e.hh[:, 0, 0:6, :].rearrange("p a b -> p (a b)").bitcast(F32).rearrange("p (a b) -> p a b", a=3)
        t2 = e.hh[:, 1, 0:6, :].rearrange("p a b -> p (a b)").bitcast(F32).rearrange("p (a b) -> p a b", a=3)
        s_c, s_e, s_f, s_g, s_d, s_z0 = (sem(nm + x) for x in ("clamped", "exp", "f_ready", "logs", "dve", "zeroed"))
        ada = Ada(nc, e, sem, st, nm, l, 4, 12, 2)
        src = lambda kind, i: {"z": f.z, "q": f.cq, "g": f.cg}[kind][:, i, :]
        with nc.Block() as block:
            @block.sync
            def _(sp):
                for j in range(ada.n):
                    ada.load(sp, j)

            @block.tensor
            def _(pe):
                for j in range(ada.n):
                    ada.product(pe, j)

            @block.gpsimd
            def _(pool):
                nc.gpsimd.memset(f.cc[:, :, :, 0:1], 0.0).then_inc(s_z0, 1)
                pool.wait_ge(s_z0, 1)

            @block.scalar
            def _(act):
                for i, (kind, n, w) in enumerate(items):
                    act.wait_ge(s_c, i + 1)
                    nc.scalar.activation(t[:, i % 2, 0:w], t[:, i % 2, 0:w], ACT.Exp, scale=-1.0).then_inc(s_e, 1)
                    if kind == "z":
                        act.wait_ge(s_f, i + 1)
                        nc.scalar.activation(t2[:, 0, :], t2[:, 0, :], ACT.Ln)
                        nc.scalar.activation(t2[:, 1, :], t2[:, 1, :], ACT.Ln).then_inc(s_g, 1)

            @block.vector
            def _(dve):
                ch = Chain(s_d)

                def clamp(i):
                    kind, n, w = items[i]
                    nc.vector.tensor_scalar(t[:, i % 2, 0:w], src(kind, n)[:, 0:w], -80.0, None, ALU.max)\
                      .then_inc(s_c, 1)

                clamp(0)
                for i, (kind, n, w) in enumerate(items):
                    if i:
                        ch.wait(dve)
                    if i + 1 < len(items):
                        clamp(i + 1)
                    dve.wait_ge(s_e, i + 1)
                    x, ez, sg = src(kind, n)[:, 0:w], t[:, i % 2, 0:w], t[:, 2, 0:w]
                    ch(nc.vector.tensor_scalar_add(sg, ez, 1.0))
                    ch.wait(dve)
                    ch(nc.vector.reciprocal(sg, sg))
                    ch.wait(dve)
                    if kind == "z":
                        c = 2 + n if n < 2 else n - 2
                        lb, om = e.lb[:, l, 0, c:c + 1], e.lb[:, l, 1, c:c + 1]
                        if i:
                            dve.wait_ge(s_g, i)
                        ch(nc.vector.scalar_tensor_tensor(x, ez, om, sg, ALU.mult, ALU.mult))
                        ch(nc.vector.tensor_scalar(t2[:, 2, :], sg, om, lb, ALU.mult, ALU.add))
                        ch.wait(dve)
                        ch(nc.vector.tensor_scalar(t2[:, 1, :], t2[:, 2, :], 1e15, 1.0, ALU.mult, ALU.min))
                        ch.wait(dve)
                        ch(nc.vector.tensor_scalar(t2[:, 1, :], t2[:, 1, :], 1e-15, None, ALU.max))
                        ch.wait(dve)
                        nc.vector.tensor_scalar(t2[:, 0, :], t2[:, 2, :], 1e-15, None, ALU.max).then_inc(s_f, 1)
                        dve.wait_ge(s_g, i + 1)
                        ch(nc.vector.tensor_tensor(t2[:, 0, :], t2[:, 0, :], t2[:, 1, :], ALU.add))
                        ch.wait(dve)
                        for b in range(TT):
                            g = t2[:, 0, b * BLK:(b + 1) * BLK]
                            ch(nc.vector.tensor_tensor_scan(f.cc[:, n, b, 1:BLK + 1], e.ones[:, :], g, 0.0,
                                                            ALU.mult, ALU.add))
                    elif kind == "q":
                        ch(nc.vector.tensor_tensor(x, x, sg, ALU.mult))
                    else:
                        ch(nc.vector.scalar_tensor_tensor(x, x, e.sv[:, l, R_CO:R_CO + 1], sg, ALU.mult, ALU.mult))
                ada.finish(dve, ch)


def states(nc, e, sem, l, f):
    nm = f"st{l}_"
    with ExitStack() as st:
        sb = lambda n, s, d=F32: st.enter_context(nc.sbuf_tensor(nm + n, s, d))
        arg = sb("arg", [P, 2, 4, BLK])
        kd, kt = sb("kd", [P, 2, 4, BLK]), sb("kt", [P, 2, 4, BLK])
        ds, dec = sb("ds", [P, TT, 4, 64]), sb("dec", [P, 4, TT])
        tp = [st.enter_context(nc.psum_tensor(f"{nm}tp{i}", [P, 4, BLK], F32)) for i in range(2)]
        pd = [st.enter_context(nc.psum_tensor(f"{nm}pd{i}", [P, 4, BLK], F32)) for i in range(2)]
        s_arg, s_e, s_dec, s_kd, s_tp, s_kt, s_pd, s_ds, s_d, s_z = (sem(nm + x) for x in (
            "arg", "exp", "decay", "kd", "transposed", "kt", "increments", "ds", "dve", "zeroed"))
        with nc.Block() as block:
            @block.gpsimd
            def _(pool):
                nc.gpsimd.memset(f.st[:, 0:2, ORDER["b"][0], :], 0.0).then_inc(s_z, 1)
                nc.gpsimd.memset(f.st[:, 2:4, ORDER["f"][0], :], 0.0).then_inc(s_z, 1)

            @block.scalar
            def _(act):
                nc.scalar.activation(dec[:, :, :], f.cc[:, :, :, BLK], ACT.Exp).then_inc(s_dec, 1)
                for b in range(TT + 1):
                    if b < TT:
                        act.wait_ge(s_arg, b + 1)
                        nc.scalar.activation(arg[:, b % 2, :, :], arg[:, b % 2, :, :], ACT.Exp).then_inc(s_e, 1)
                    if b:
                        act.wait_ge(s_tp, b)
                        if b >= 3:
                            act.wait_ge(s_pd, b - 2)
                        nc.scalar.activation(kt[:, (b - 1) % 2, :, :], tp[(b - 1) % 2][:, :, :], ACT.Copy)\
                          .then_inc(s_kt, 1)

            @block.tensor
            def _(pe):
                for b in range(TT + 1):
                    if b < TT:
                        pe.wait_ge(s_kd, b + 1)
                        if b >= 2:
                            pe.wait_ge(s_kt, b - 1)
                        for n in range(4):
                            last = nc.tensor.transpose(tp[b % 2][:, n, :], kd[:, b % 2, n, :], e.ident[:, :])
                        last.then_inc(s_tp, 1)
                    if b:
                        c = b - 1
                        pe.wait_ge(s_kt, c + 1)
                        if c >= 2:
                            pe.wait_ge(s_ds, 2 * (c - 1))
                        for n in range(4):
                            last = nc.tensor.matmul(pd[c % 2][:, n, :], kt[:, c % 2, n, :],
                                                    f.cv[:, c, (n % 2) * P:(n % 2 + 1) * P], start=True, stop=True)
                        last.then_inc(s_pd, 1)

            @block.vector
            def _(dve):
                ch = Chain(s_d)

                def args(b):
                    if b >= 2:
                        dve.wait_ge(s_kd, b - 1)
                    nc.vector.tensor_copy(arg[:, b % 2, 0:2, :], f.cc[:, 0:2, b, 0:BLK])
                    nc.vector.tensor_tensor(arg[:, b % 2, 2:4, :],
                                            f.cc[:, 2:4, b, BLK:BLK + 1].broadcast_to([P, 2, BLK]),
                                            f.cc[:, 2:4, b, 1:BLK + 1], ALU.subtract).then_inc(s_arg, 1)

                args(0)
                for b in range(TT + 1):
                    if b + 1 < TT:
                        args(b + 1)
                    if b < TT:
                        dve.wait_ge(s_e, b + 1)
                        if b >= 2:
                            dve.wait_ge(s_tp, b - 1)
                        nc.vector.tensor_tensor(kd[:, b % 2, :, :], arg[:, b % 2, :, :],
                                                f.z[:, :, b * BLK:(b + 1) * BLK], ALU.mult).then_inc(s_kd, 1)
                    if b:
                        c = b - 1
                        dve.wait_ge(s_pd, c + 1)
                        for hp in range(2):
                            R = slice(64 * hp, 64 * hp + 64)
                            nc.vector.tensor_copy(ds[R, c, :, :], pd[c % 2][R, :, 64 * hp:64 * hp + 64])\
                              .then_inc(s_ds, 1)
                dve.wait_ge(s_z, 2)
                dve.wait_ge(s_dec, 1)
                dve.wait_ge(s_ds, 2 * TT)
                for i in range(TT - 1):
                    if i:
                        ch.wait(dve)
                    for n in range(4):
                        o = ORDER["b" if n < 2 else "f"]
                        ch(nc.vector.scalar_tensor_tensor(f.st[:, n, o[i + 1], :], f.st[:, n, o[i], :],
                                                          dec[:, n, o[i]:o[i] + 1], ds[:, o[i], n, :],
                                                          ALU.mult, ALU.add))


def outputs(nc, e, sem, l, f):
    nm = f"ro{l}_"
    nb = TT if l < DEPTH - 1 else LAT // P
    NL = len(LEVELS)
    with ExitStack() as st:
        sb = lambda n, s, d=F32: st.enter_context(nc.sbuf_tensor(nm + n, s, d))
        X = [e.hh[:, i, 0:6, :].rearrange("p a b -> p (a b)").bitcast(F32)[:, 0:4 * NL * BLK]
             .rearrange("p (n l t) -> p n l t", n=4, l=NL) for i in range(2)]
        val = sb("val", [P, 2, 4, BLK])
        dk = sb("dk", [P, 3, 4, BLK])
        ks = sb("ks", [P, 3, 2, BLK])
        A = sb("A", [P, 2, 2, 2, BLK])
        sc = [[st.enter_context(nc.psum_tensor(f"{nm}sc{i}{j}", [P, 2, 2, BLK], F32)) for j in range(2)] for i in range(3)]
        po = [st.enter_context(nc.psum_tensor(f"{nm}po{i}", [P, 2, BLK], F32)) for i in range(2)]
        s_val, s_a1, s_a2, s_e, s_x, s_sc, s_cp, s_A, s_o, s_ov, s_d, s_dk = (sem(nm + x) for x in (
            "val", "first_halves", "second_halves", "exp", "x", "scores", "level_copied", "scores_merged", "o", "o_out",
            "dve", "edge_decay"))

        def half(t, h, which):
            return t.rearrange("p n (s w h) -> p n s w h", w=2, h=h)[:, :, :, which, :]

        def mid(b, h):
            v = f.cc[:, :, b, h:BLK:2 * h] if h < 64 else f.cc[:, :, b, 64:65]
            return v.unsqueeze(3).broadcast_to([P, 4, BLK // (2 * h), h])

        with nc.Block() as block:
            @block.gpsimd
            def _(pool):
                for b in range(nb):
                    pool.wait_ge(s_val, b + 1)
                    if b >= 2:
                        pool.wait_ge(s_sc, 4 * (b - 1))
                    for i, h in enumerate(LEVELS):
                        last = nc.gpsimd.tensor_tensor(half(X[b % 2][:, :, i, :], h, 0), mid(b, h),
                                                       half(val[:, b % 2, :, :], h, 0), ALU.subtract)
                    last.then_inc(s_a1, 1)

            @block.scalar
            def _(act):
                def merge(b):
                    act.wait_ge(s_sc, 4 * b + 1)
                    if b >= 2:
                        act.wait_ge(s_o, b - 1)
                    for par in range(2):
                        nc.scalar.activation(A[:, b % 2, par, :, :], sc[4 * b % 3][par][:, 0, :, :], ACT.Copy).then_inc(s_cp, 1)
                    act.wait_ge(s_cp, 6 * b + 2)
                    for par in range(2):
                        for q in range(2):
                            R = slice(64 * q, 64 * q + 64)
                            nc.scalar.activation(A[R, b % 2, par, :, R], sc[4 * b % 3][par][R, 1, :, R], ACT.Copy)\
                              .then_inc(s_cp, 1)

                def exps(b):
                    act.wait_ge(s_dk, b + 1)
                    nc.scalar.activation(dk[:, b % 3, :, :], dk[:, b % 3, :, :], ACT.Exp).then_inc(s_e, 1)
                    act.wait_ge(s_a1, b + 1)
                    act.wait_ge(s_a2, b + 1)
                    x = X[b % 2].rearrange("p n l t -> p (n l t)")
                    nc.scalar.activation(x, x, ACT.Exp).then_inc(s_e, 1)

                def copy_out(b):
                    act.wait_ge(s_o, b + 1)
                    nc.scalar.activation(f.cq[:, :, b * BLK:(b + 1) * BLK], po[b % 2][:, :, :], ACT.Copy)\
                      .then_inc(s_ov, 1)

                for b in range(-1, nb):
                    if b + 1 < nb:
                        exps(b + 1)
                    if b >= 0:
                        merge(b)
                    if b > 0:
                        copy_out(b - 1)
                copy_out(nb - 1)

            @block.vector
            def _(dve):
                ch = Chain(s_d)

                def values(b):
                    if b >= 2:
                        dve.wait_ge(s_a1, b - 1)
                        dve.wait_ge(s_sc, 4 * (b - 1))
                    if b >= 3:
                        dve.wait_ge(s_o, b - 2)
                    last_ = f.cc[:, 0:2, b, BLK:BLK + 1].broadcast_to([P, 2, BLK])
                    nc.vector.tensor_copy(val[:, b % 2, 0:2, :], f.cc[:, 0:2, b, 0:BLK])
                    ch(nc.vector.tensor_copy(val[:, b % 2, 2:4, :], f.cc[:, 2:4, b, 1:BLK + 1]))
                    ch(nc.vector.tensor_tensor(dk[:, b % 3, 0:2, :], last_, f.cc[:, 0:2, b, 0:BLK], ALU.subtract))
                    nc.vector.tensor_copy(dk[:, b % 3, 2:4, :], f.cc[:, 2:4, b, 1:BLK + 1]).then_inc(s_dk, 1)
                    ch.wait(dve)
                    nc.vector.tensor_tensor(ks[:, b % 3, :, :], f.z[:, 0:2, b * BLK:(b + 1) * BLK],
                                            f.z[:, 2:4, b * BLK:(b + 1) * BLK], ALU.add).then_inc(s_val, 1)
                    for i, h in enumerate(LEVELS):
                        for d in range(2):
                            to, n = slice(2 - 2 * d, 4 - 2 * d), slice(2 * d, 2 * d + 2)
                            last = nc.vector.tensor_tensor(half(X[b % 2][:, to, i, :], h, 1),
                                                           half(val[:, b % 2, n, :], h, 1), mid(b, h)[:, n],
                                                           ALU.subtract)
                    last.then_inc(s_a2, 1)

                def decay(b):
                    B = slice(b * BLK, (b + 1) * BLK)
                    dve.wait_ge(s_e, 2 * b + 2)
                    x = X[b % 2]
                    q, k = f.cq[:, :, B], f.z[:, :, B]
                    for d in range(2):
                        n = slice(2 * d, 2 * d + 2)
                        nc.vector.tensor_tensor(dk[:, b % 3, n, :], dk[:, b % 3, n, :], q, ALU.mult)
                    nc.vector.tensor_tensor(x[:, 0:2, :, :], x[:, 0:2, :, :],
                                            q.unsqueeze(2).broadcast_to([P, 2, NL, BLK]), ALU.mult)
                    for i, h in enumerate(LEVELS):
                        for w in range(2):
                            xk = half(x[:, 2:4, i, :], h, w)
                            last = nc.vector.tensor_tensor(xk, xk, half(k[:, 2 - 2 * w:4 - 2 * w, :], h, w), ALU.mult)
                    last.then_inc(s_x, 1)

                def merge(b):
                    dve.wait_ge(s_cp, 6 * (b + 1))
                    for r in range(1, 4):
                        dve.wait_ge(s_sc, 4 * b + r + 1)
                        for lv in range(2):
                            i = 2 * r + lv
                            for par in range(2):
                                mask = e.same[:, i, :].unsqueeze(1).broadcast_to([P, 2, BLK])
                                ins = nc.vector.copy_predicated(A[:, b % 2, par, :, :], mask, sc[(4 * b + r) % 3][par][:, lv, :, :])
                                ins.then_inc(s_A, 1)
                            dve.wait_ge(s_A, 12 * b + 4 * (r - 1) + 2 * lv + 2)

                values(0)
                values(1)
                decay(0)
                for b in range(nb):
                    if b + 1 < nb:
                        decay(b + 1)
                    merge(b)
                    if b + 2 < nb:
                        values(b + 2)

            @block.tensor
            def _(pe):
                def scores(b, rounds):
                    x = X[b % 2]
                    B = slice(b * BLK, (b + 1) * BLK)
                    for r in rounds:
                        if 4 * b + r >= 3:
                            b0, r0 = divmod(4 * b + r - 3, 4)
                            if r0 == 0:
                                pe.wait_ge(s_cp, 6 * (b0 + 1))
                            else:
                                pe.wait_ge(s_A, 12 * b0 + 4 * r0)
                        for lv in range(2):
                            i = 2 * r + lv
                            for pr in range(2):
                                for par in range(2):
                                    R = slice(64 * par, 64 * par + 64)
                                    to = sc[(4 * b + r) % 3][par][:, lv, pr, :]
                                    keys = x[R, 2 + pr, i, :] if i < NL else ks[R, b % 3, pr, :]
                                    queries = x[R, pr, i, :] if i < NL else f.cq[R, pr, B]
                                    last = nc.tensor.matmul(to, keys, queries, start=True, stop=True)
                        last.then_inc(s_sc, 1)

                def out(b):
                    if b >= 2:
                        pe.wait_ge(s_ov, b - 1)
                    for pr in range(2):
                        for par in range(2):
                            R = slice(64 * par, 64 * par + 64)
                            for d in range(2):
                                n = 2 * d + pr
                                nc.tensor.matmul(po[b % 2][R, pr, :], f.st[R, n, b, :], dk[R, b % 3, n, :],
                                                 start=(d == 0 and pr == 0), stop=False, skip_group_check=True)
                    pe.wait_ge(s_A, 12 * (b + 1))
                    for pr in range(2):
                        for par in range(2):
                            R = slice(64 * par, 64 * par + 64)
                            hd = 2 * pr + par
                            last = nc.tensor.matmul(po[b % 2][R, pr, :], f.cv[:, b, 64 * hd:64 * hd + 64],
                                                    A[:, b % 2, par, pr, :], start=False, stop=True,
                                                    skip_group_check=True)
                    last.then_inc(s_o, 1)

                for b in range(nb):
                    pe.wait_ge(s_x, b + 1)
                    scores(b, (0, 1))
                    if b:
                        out(b - 1)
                    scores(b, (2, 3))
                out(nb - 1)


def readout(nc, e, sem, l, f):
    nm = f"rd{l}_"
    nq = TOK if l < DEPTH - 1 else LAT
    items = [(i, a, n) for i in range(2) for a, n in chunks(nq)]
    N = len(items)
    with ExitStack() as st:
        sb = lambda n, s, d=F32: st.enter_context(nc.sbuf_tensor(nm + n, s, d))
        sq, m, r = sb("sq", [P, 2, 512]), sb("m", [P, 2, 512]), sb("r", [P, 2, 512])
        t1, u = sb("t1", [P, 512]), sb("u", [P, 2, 512])
        pss = [st.enter_context(nc.psum_tensor(f"{nm}ss{i}", [P, 512], F32)) for i in range(2)]
        s_sq, s_pp, s_m, s_r, s_u, s_hi, s_d = (sem(nm + x) for x in (
            "squared", "sums", "mean", "rsqrt", "u_ready", "hi", "dve"))
        with nc.Block() as block:
            @block.scalar
            def _(act):
                def square(i):
                    t, a, n = items[i]
                    if i >= 2:
                        act.wait_ge(s_pp, i - 1)
                    nc.scalar.activation(sq[:, i % 2, 0:n], f.cq[:, t, a:a + n], ACT.Square).then_inc(s_sq, 1)

                def high(i):
                    t, a, n = items[i]
                    act.wait_ge(s_u, i + 1)
                    nc.scalar.activation(e.hh[:, 0, 6 + t, a:a + n], u[:, i % 2, 0:n], ACT.Copy).then_inc(s_hi, 1)

                square(0)
                for i, (t, a, n) in enumerate(items):
                    if i + 1 < N:
                        square(i + 1)
                    act.wait_ge(s_m, i + 1)
                    nc.scalar.activation(r[:, i % 2, 0:n], m[:, i % 2, 0:n], ACT.Ln).then_inc(s_r, 1)
                    act.wait_ge(s_r, 2 * i + 1)
                    nc.scalar.activation(r[:, i % 2, 0:n], r[:, i % 2, 0:n], ACT.Exp, scale=-0.5).then_inc(s_r, 1)
                    if i:
                        high(i - 1)
                high(N - 1)

            @block.tensor
            def _(pe):
                for i, (t, a, n) in enumerate(items):
                    pe.wait_ge(s_sq, i + 1)
                    if i >= 2:
                        pe.wait_ge(s_m, i - 1)
                    nc.tensor.matmul(pss[i % 2][:, 0:n], e.pair[:, :], sq[:, i % 2, 0:n], start=True, stop=True)\
                      .then_inc(s_pp, 1)

            @block.vector
            def _(dve):
                ch = Chain(s_d)

                def mean(i):
                    n = items[i][2]
                    dve.wait_ge(s_pp, i + 1)
                    nc.vector.tensor_scalar(m[:, i % 2, 0:n], pss[i % 2][:, 0:n], 1.0 / 64, EPS, ALU.mult, ALU.add)\
                      .then_inc(s_m, 1)

                def low(i):
                    t, a, n = items[i]
                    dve.wait_ge(s_hi, i + 1)
                    ch(nc.vector.tensor_tensor(e.hh[:, 1, 6 + t, a:a + n], u[:, i % 2, 0:n], e.hh[:, 0, 6 + t, a:a + n],
                                               ALU.subtract))

                mean(0)
                for i, (t, a, n) in enumerate(items):
                    if i + 1 < N:
                        mean(i + 1)
                    p = i % 2
                    dve.wait_ge(s_r, 2 * i + 2)
                    newton(nc, dve, ch, m[:, p, 0:n], r[:, p, 0:n], t1[:, 0:n])
                    ch(nc.vector.tensor_tensor(t1[:, 0:n], f.cq[:, t, a:a + n], f.cg[:, t, a:a + n], ALU.mult))
                    ch.wait(dve)
                    nc.vector.tensor_tensor(u[:, p, 0:n], t1[:, 0:n], r[:, p, 0:n], ALU.mult).then_inc(s_u, 1)
                    dve.wait_ge(s_u, i + 1)
                    if i:
                        low(i - 1)
                low(N - 1)


def recurrence(nc, e, sem, l, f, stop=None):
    with ExitStack() as st:
        f.cc = st.enter_context(nc.sbuf_tensor(f"cc{l}", [P, 4, TT, BLK + 1], F32))
        f.st = st.enter_context(nc.sbuf_tensor(f"st{l}", [P, 4, TT, 64], F32))
        gates(nc, e, sem, l, f)
        if stop == f"mix{l}g":
            return
        states(nc, e, sem, l, f)
        if stop == f"mix{l}s":
            return
        outputs(nc, e, sem, l, f)
        if stop == f"mix{l}o":
            return
        readout(nc, e, sem, l, f)


def build(nc, e, sem, stop):
    x_tile = lambda n: nc.sbuf_tensor(n, [P, KT, TOK], F32)
    with x_tile("x_first") as x:
        setup_phase(nc, e, sem, x)
        if stop == "setup":
            return
        between(nc, e, sem, x, TOK, "n0_", mod=(8, 0, 0), store=True)
        if stop == "norm0":
            return
    for l in range(DEPTH):
        nq = TOK if l < DEPTH - 1 else LAT
        mixers(nc, e, sem, l, stop)
        if stop and stop.startswith(f"mix{l}"):
            return
        e.recycle()
        with x_tile(f"x{l}") as x:
            with nc.sbuf_tensor(f"y{l}", [P, KT, TOK], F32) as y:
                output_projection(nc, e, sem, l, x, y, nq)
                if stop == f"out{l}":
                    return
                between(nc, e, sem, x, nq, f"nf{l}_", l, y, 16, mod=(32, 24, l))
                if stop == f"normf{l}":
                    return
            with nc.sbuf_tensor(f"yf{l}", [P, KT, TOK], F32) as y:
                mlp(nc, e, sem, l, y, nq)
                if stop == f"mlp{l}":
                    return
                if l < DEPTH - 1:
                    between(nc, e, sem, x, nq, f"n{l + 1}_", l, y, 40, mod=(8, 0, l + 1), store=True)
                else:
                    between(nc, e, sem, x, nq, "end_", l, y, 40, final=True)
        if stop == f"layer{l}":
            return
        if l < DEPTH - 1:
            e.recycle()


def shape_constants():
    f = np.float32
    tok = np.arange(LAT)
    row, col = (tok // 64).astype(f), (tok % 64).astype(f)

    def tables(rot, lead):
        nf = rot // 4
        inv = (f(10000.0) ** (-(np.arange(nf, dtype=f)) / f(nf))).astype(f)
        ang = np.concatenate([row[:, None] * inv, col[:, None] * inv], axis=-1).astype(f)
        cos, sin = np.ones((lead + rot, TOK), f), np.zeros((lead + rot, TOK), f)
        cos[lead:, :LAT] = np.tile(np.cos(ang).T, (2, 1))
        sin[lead:, :LAT] = np.tile(np.sin(ang).T, (2, 1))
        return cos, sin

    ca, sa = tables(64, 0)
    cb, sb_ = tables(32, 64)
    rope = np.zeros((P, 4, TOK), f)
    rope[:, 0], rope[:, 1] = np.tile(ca, (2, 1)), np.tile(sa, (2, 1))
    rope[0:96, 2], rope[0:96, 3] = cb, sb_
    swap = np.zeros((P, 2, P), f)
    for base in (0, 64):
        for d in range(32):
            swap[base + 32 + d, 0, base + d] = -1.0
            swap[base + d, 0, base + 32 + d] = 1.0
    for d in range(16):
        swap[80 + d, 1, 64 + d] = -1.0
        swap[64 + d, 1, 80 + d] = 1.0
    pair = np.zeros((P, P), f)
    pair[:64, :64] = pair[64:, 64:] = 1.0
    s = np.arange(P)
    same = np.stack([(s[:, None] // (2 * h) == s[None] // (2 * h)) for h in LEVELS] + [s[:, None] == s[None]], 1)
    return {"k_ident": np.eye(P, dtype=f), "k_ones": np.ones((P, P), f), "k_pair": pair, "k_swap": swap,
            "k_rope": rope, "k_same": same.astype(f)}


LN_EXP_SET = 6

NAMES = ['x', 'c', 'ctx', 'c_ctx', 'w_ada', 'b_ada', 'g_pre_mix', 'g_post_mix', 'g_pre_ffn', 'g_post_ffn', 'w_in',
         'a_q_norm', 'a_k_norm', 'b_q_norm', 'w_q_up', 'b_kv_norm', 'w_kv_up', 'c_lower_bounds', 'c_out_norm',
         'w_out', 'w_ff1', 'w_ff2']


def program(nc, args, out, stop=None):
    e = Env()
    (e.x, e.c, e.ctx, e.c_ctx, e.w_ada, e.b_ada, e.g_pre_mix, e.g_post_mix, e.g_pre_ffn, e.g_post_ffn, e.w_in,
     e.a_q_norm, e.a_k_norm, e.b_q_norm, e.w_q_up, e.b_kv_norm, e.w_kv_up, e.c_lb, e.c_out_norm, e.w_out,
     e.w_ff1, e.w_ff2) = [args[n] for n in NAMES]
    e.k_ident, e.k_ones, e.k_pair = args["k_ident"], args["k_ones"], args["k_pair"]
    e.k_swap, e.k_rope, e.k_same = args["k_swap"], args["k_rope"], args["k_same"]
    e.out = out
    with ExitStack() as st:
        names, live = set(), [ExitStack(), []]

        def sem(n):
            k, base = 2, n
            while n in names:
                n, k = f"{base}_{k}", k + 1
            names.add(n)
            s = live[0].enter_context(nc.semaphore(n))
            live[1].append(s)
            return s

        def recycle():
            with nc.Block() as block:
                @block.sync
                def _(sp):
                    for s in live[1]:
                        sp.sem_clear(s)
            live[0].close()
            live[:] = [ExitStack(), []]

        e.recycle = recycle
        e.s_final = st.enter_context(nc.semaphore("output_stored"))

        sb = lambda n, s, d=F32: st.enter_context(nc.sbuf_tensor(n, s, d))
        e.ident, e.ones, e.pair = sb("ident", [P, P]), sb("ones", [P, P]), sb("pair", [P, P])
        e.swap, e.same = sb("swap", [P, 2, P]), sb("same", [P, 8, P], U8)
        e.consts = [(e.ident[:, :], e.k_ident), (e.ones[:, :], e.k_ones), (e.pair[:, :], e.k_pair),
                    (e.swap[:, :, :], e.k_swap)]
        e.sv = sb("sv", [P, DEPTH, R_N])
        e.mod = sb("mod", [P, DEPTH, 48, 2])
        e.lb = sb("lb", [P, DEPTH, 2, 4])
        e.cact = sb("cact", [P, KT, 2])
        e.x_dram = nc.dram_tensor("x_scratch", [P, KT, TOK], F32, kind="Internal").ap()
        e.hh = sb("hh", [P, 2, KT, TOK], F16)
        nc.scalar.add_instruction(mybir.InstLoadActFuncSet(
            name=nc.get_next_instruction_name(), act_func_set_id=LN_EXP_SET, ins=[], outs=[]))
        build(nc, e, sem, stop)


def kernel(**inputs):
    import concourse.bacc as bacc
    from concourse.bass_utils import run_bass_kernel_spmd

    nc = bacc.Bacc("TRN2", target_bir_lowering=False, num_devices=1)
    arrays, args = {}, {}
    for name, a in {**{n: np.ascontiguousarray(inputs[n]) for n in NAMES}, **shape_constants()}.items():
        arrays["in_" + name] = a
        args[name] = nc.dram_tensor("in_" + name, a.shape, mybir.dt.from_np(a.dtype), kind="ExternalInput").ap()
    out = nc.dram_tensor("out_0_dram", (1, LAT, D), F32, kind="ExternalOutput").ap()
    program(nc, args, out)
    r = run_bass_kernel_spmd(nc, [arrays], core_ids=[0])
    return r.results[0]["out_0_dram"]
```
